# Optimizing a Trainium2 kernel written in Bass

```python
import math
import jax, jax.numpy as jnp
from jax import lax
import numpy as np

D_MODEL = 1024
BATCH = 1
SEQ = 256
DEPTH = 2

CHUNK = 64
Q_BLOCK = 128
HEAD_DIM = 64
A_HEADS = 8
A_KV_HEADS = 2
A_WINDOW = 128
A_WINDOW_CHUNKS = A_WINDOW // CHUNK
B_HEADS = 8
FORGET_BIAS_INIT = 2.0
C_HEADS = D_MODEL // (2 * HEAD_DIM)
A_Q = A_HEADS * HEAD_DIM
A_KV = A_KV_HEADS * HEAD_DIM
B_W = B_HEADS * HEAD_DIM
EVEN_IN = A_Q + 2 * A_KV + 3 * B_W + B_HEADS
EVEN_MIX = A_Q + B_W
C_QK = 2 * C_HEADS * HEAD_DIM
C_V = C_HEADS * 2 * HEAD_DIM
ODD_IN = 2 * C_QK + C_V
D_FF = 2816
N_EXPERTS = 8
TOP_K = 2
D_FF_EXPERT = 3584
MOE_BLOCK = 256
N_EVEN = (DEPTH + 1) // 2
N_ODD = DEPTH // 2
ALPHA = (2.0 * DEPTH) ** 0.25
BETA = (8.0 * DEPTH) ** -0.25
LN_EPS = 1e-5
RMS_EPS = 1e-5
NEG_INF = -1e30

kernel_name = "hybrid_swa_fox_diffattn_moe_deepnorm"

def layer_norm(x, g, b):
    xf = x.astype(jnp.float32)
    mu = jnp.mean(xf, axis=-1, keepdims=True)
    var = jnp.mean(jnp.square(xf - mu), axis=-1, keepdims=True)
    return ((xf - mu) * lax.rsqrt(var + LN_EPS) * g + b).astype(x.dtype)

def alibi_slopes(n):
    return jnp.asarray(2.0 ** (-8.0 * np.arange(1, n + 1) / n), dtype=jnp.float32)

def swiglu(x, w_gate, w_up, w_down):
    return jnp.dot(jax.nn.silu(jnp.dot(x, w_gate)) * jnp.dot(x, w_up), w_down)

def sliding_window_sink_attention(q, k, v, sinks, slopes):
    bsz, seq, n_heads, dh = q.shape
    n_kv = k.shape[2]
    grp = n_heads // n_kv
    n_chunks = seq // CHUNK
    lead = (A_WINDOW_CHUNKS - 1) * CHUNK
    band = A_WINDOW_CHUNKS * CHUNK
    qc = q.reshape(bsz, n_chunks, CHUNK, n_kv, grp, dh)
    pad = ((0, 0), (lead, 0), (0, 0), (0, 0))
    kc = jnp.pad(k, pad).reshape(bsz, n_chunks + A_WINDOW_CHUNKS - 1, CHUNK, n_kv, dh)
    vc = jnp.pad(v, pad).reshape(bsz, n_chunks + A_WINDOW_CHUNKS - 1, CHUNK, n_kv, dh)
    kb = jnp.concatenate([kc[:, j:j + n_chunks] for j in range(A_WINDOW_CHUNKS)], axis=2)
    vb = jnp.concatenate([vc[:, j:j + n_chunks] for j in range(A_WINDOW_CHUNKS)], axis=2)
    s = jnp.einsum('bcikgd,bcjkd->bckgij', qc, kb).astype(jnp.float32) * (dh ** -0.5)
    qi = jnp.arange(CHUNK)[:, None]
    kj = jnp.arange(band)[None, :]
    dist = jnp.abs(qi - kj + lead).astype(jnp.float32)
    s = s - slopes.reshape(n_kv, grp, 1, 1) * dist
    key_pos = jnp.arange(n_chunks)[:, None] * CHUNK + jnp.arange(band)[None, :] - lead
    valid = (key_pos >= 0)[None, :, None, None, None, :]
    s = jnp.where(valid, s, NEG_INF)
    sink = sinks.astype(jnp.float32).reshape(1, 1, n_kv, grp, 1, 1)
    m = jnp.maximum(jnp.max(s, axis=-1, keepdims=True), sink)
    p = jnp.exp(s - m)
    probs = p / (jnp.sum(p, axis=-1, keepdims=True) + jnp.exp(sink - m))
    o = jnp.einsum('bckgij,bcjkd->bcikgd', probs.astype(v.dtype), vb)
    return o.reshape(bsz, seq, n_heads * dh)

def forgetting_attention(q, k, v, log_f):
    bsz, seq, n_heads, dh = q.shape
    cum = jnp.cumsum(log_f.astype(jnp.float32), axis=1).transpose(0, 2, 1)
    outs = []
    for blk in range(seq // Q_BLOCK):
        lo, hi = blk * Q_BLOCK, (blk + 1) * Q_BLOCK
        s = jnp.einsum('bihd,bjhd->bhij', q[:, lo:hi], k[:, :hi]).astype(jnp.float32) * (dh ** -0.5)
        s = s + cum[:, :, lo:hi, None] - cum[:, :, None, :hi]
        causal = jnp.arange(lo, hi)[:, None] >= jnp.arange(hi)[None, :]
        s = jnp.where(causal, s, NEG_INF)
        p = jax.nn.softmax(s, axis=-1)
        outs.append(jnp.einsum('bhij,bjhd->bihd', p.astype(v.dtype), v[:, :hi]))
    return jnp.concatenate(outs, axis=1).reshape(bsz, seq, n_heads * dh)

def differential_attention(q, k, v, lam, slopes):
    bsz, seq, _, n_heads, dh = q.shape
    outs = []
    for blk in range(seq // Q_BLOCK):
        lo, hi = blk * Q_BLOCK, (blk + 1) * Q_BLOCK
        s = jnp.einsum('biphd,bjphd->bphij', q[:, lo:hi], k[:, :hi]).astype(jnp.float32) * (dh ** -0.5)
        tpos = jnp.arange(lo, hi)[:, None]
        spos = jnp.arange(hi)[None, :]
        dist = jnp.abs(tpos - spos).astype(jnp.float32)
        s = s - slopes[:, None, None] * dist
        mask = (spos // CHUNK) <= (tpos // CHUNK)
        s = jnp.where(mask, s, NEG_INF)
        p = jax.nn.softmax(s, axis=-1)
        a = p[:, 0] - lam * p[:, 1]
        outs.append(jnp.einsum('bhij,bjhd->bihd', a.astype(v.dtype), v[:, :hi]))
    return jnp.concatenate(outs, axis=1)

def even_mixer(x, w_in, b_forget, sinks, w_out):
    bsz, seq, _ = x.shape
    h = jnp.dot(x, w_in)
    cuts = [A_Q, A_Q + A_KV, A_Q + 2 * A_KV, A_Q + 2 * A_KV + B_W,
            A_Q + 2 * A_KV + 2 * B_W, A_Q + 2 * A_KV + 3 * B_W]
    qa, ka, va, qb, kb, vb, fb = jnp.split(h, cuts, axis=-1)
    qa = qa.reshape(bsz, seq, A_HEADS, HEAD_DIM)
    ka = ka.reshape(bsz, seq, A_KV_HEADS, HEAD_DIM)
    va = va.reshape(bsz, seq, A_KV_HEADS, HEAD_DIM)
    qb = qb.reshape(bsz, seq, B_HEADS, HEAD_DIM)
    kb = kb.reshape(bsz, seq, B_HEADS, HEAD_DIM)
    vb = vb.reshape(bsz, seq, B_HEADS, HEAD_DIM)
    log_f = jax.nn.log_sigmoid((fb + b_forget).astype(jnp.float32))
    oa = sliding_window_sink_attention(qa, ka, va, sinks, alibi_slopes(A_HEADS))
    ob = forgetting_attention(qb, kb, vb, log_f)
    return jnp.dot(jnp.concatenate([oa, ob], axis=-1), w_out)

def odd_mixer(x, w_in, lq1, lk1, lq2, lk2, subln_g, w_out, lambda_init):
    bsz, seq, _ = x.shape
    h = jnp.dot(x, w_in)
    q, k, v = jnp.split(h, [C_QK, 2 * C_QK], axis=-1)
    q = q.reshape(bsz, seq, 2, C_HEADS, HEAD_DIM)
    k = k.reshape(bsz, seq, 2, C_HEADS, HEAD_DIM)
    v = v.reshape(bsz, seq, C_HEADS, 2 * HEAD_DIM)
    lam = (jnp.exp(jnp.sum(lq1.astype(jnp.float32) * lk1.astype(jnp.float32)))
           - jnp.exp(jnp.sum(lq2.astype(jnp.float32) * lk2.astype(jnp.float32))) + lambda_init)
    o = differential_attention(q, k, v, lam, alibi_slopes(C_HEADS)).astype(jnp.float32)
    o = o * lax.rsqrt(jnp.mean(jnp.square(o), axis=-1, keepdims=True) + RMS_EPS)
    o = (o * subln_g * (1.0 - lambda_init)).astype(x.dtype)
    return jnp.dot(o.reshape(bsz, seq, C_HEADS * 2 * HEAD_DIM), w_out)

def moe_swiglu(x, w_router, w_gate, w_up, w_down):
    bsz, seq, d = x.shape
    xt = x.reshape(-1, d)
    n_tok = xt.shape[0]
    n_assign = n_tok * TOP_K
    logits = jnp.dot(xt, w_router).astype(jnp.float32)
    top_logit, top_e = lax.top_k(logits, TOP_K)
    gate = jax.nn.softmax(top_logit, axis=-1)
    flat_e = top_e.reshape(-1).astype(jnp.int32)
    flat_tok = jnp.arange(n_assign, dtype=jnp.int32) // TOP_K
    order = jnp.argsort(flat_e)
    sorted_e = flat_e[order]
    sorted_tok = flat_tok[order]
    sorted_gate = gate.reshape(-1)[order]
    counts = jnp.bincount(flat_e, length=N_EXPERTS).astype(jnp.int32)
    padded_counts = ((counts + MOE_BLOCK - 1) // MOE_BLOCK) * MOE_BLOCK
    padded_end = jnp.cumsum(padded_counts)
    padded_start = padded_end - padded_counts
    start = jnp.cumsum(counts) - counts
    rank = jnp.arange(n_assign, dtype=jnp.int32) - start[sorted_e]
    dest = padded_start[sorted_e] + rank
    n_rows = n_assign + N_EXPERTS * MOE_BLOCK
    n_blocks = n_rows // MOE_BLOCK
    row_tok = jnp.zeros((n_rows,), jnp.int32).at[dest].set(sorted_tok)
    row_w = jnp.zeros((n_rows,), jnp.float32).at[dest].set(sorted_gate)
    block_e = jnp.minimum(
        jnp.searchsorted(padded_end, jnp.arange(n_blocks, dtype=jnp.int32) * MOE_BLOCK, side='right'),
        N_EXPERTS - 1).astype(jnp.int32)
    x_rows = xt[row_tok].reshape(n_blocks, MOE_BLOCK, d)

    def expert_block(args):
        xb, e = args
        return swiglu(xb, w_gate[e], w_up[e], w_down[e])

    y_rows = lax.map(expert_block, (x_rows, block_e)).reshape(n_rows, d)
    y_rows = y_rows * row_w[:, None].astype(y_rows.dtype)
    out = jax.ops.segment_sum(y_rows, row_tok, num_segments=n_tok)
    return out.reshape(bsz, seq, d)

def setup_inputs(seed: int = 0) -> dict:
    key = jax.random.key(seed)
    ks = iter(jax.random.split(key, 32))

    def nrm(shape, scale):
        return scale * jax.random.normal(next(ks), shape, jnp.float32)

    D = D_MODEL
    return {
        "x": nrm((BATCH, SEQ, D), 1.0),
        "e_w_in": nrm((N_EVEN, D, EVEN_IN), D ** -0.5),
        "e_b_forget": FORGET_BIAS_INIT + nrm((N_EVEN, B_HEADS), 0.1),
        "e_sinks": nrm((N_EVEN, A_HEADS), 0.5),
        "e_w_out": nrm((N_EVEN, EVEN_MIX, D), BETA * EVEN_MIX ** -0.5),
        "e_ln1_g": 1.0 + nrm((N_EVEN, D), 0.02),
        "e_ln1_b": nrm((N_EVEN, D), 0.02),
        "e_w_gate": nrm((N_EVEN, D, D_FF), D ** -0.5),
        "e_w_up": nrm((N_EVEN, D, D_FF), D ** -0.5),
        "e_w_down": nrm((N_EVEN, D_FF, D), BETA * D_FF ** -0.5),
        "e_ln2_g": 1.0 + nrm((N_EVEN, D), 0.02),
        "e_ln2_b": nrm((N_EVEN, D), 0.02),
        "o_w_in": nrm((N_ODD, D, ODD_IN), D ** -0.5),
        "o_lambda_q1": nrm((N_ODD, HEAD_DIM), 0.1),
        "o_lambda_k1": nrm((N_ODD, HEAD_DIM), 0.1),
        "o_lambda_q2": nrm((N_ODD, HEAD_DIM), 0.1),
        "o_lambda_k2": nrm((N_ODD, HEAD_DIM), 0.1),
        "o_subln_g": 1.0 + nrm((N_ODD, 2 * HEAD_DIM), 0.02),
        "o_w_out": nrm((N_ODD, C_V, D), BETA * C_V ** -0.5),
        "o_ln1_g": 1.0 + nrm((N_ODD, D), 0.02),
        "o_ln1_b": nrm((N_ODD, D), 0.02),
        "o_w_router": nrm((N_ODD, D, N_EXPERTS), D ** -0.5),
        "o_w_gate": nrm((N_ODD, N_EXPERTS, D, D_FF_EXPERT), D ** -0.5),
        "o_w_up": nrm((N_ODD, N_EXPERTS, D, D_FF_EXPERT), D ** -0.5),
        "o_w_down": nrm((N_ODD, N_EXPERTS, D_FF_EXPERT, D), BETA * D_FF_EXPERT ** -0.5),
        "o_ln2_g": 1.0 + nrm((N_ODD, D), 0.02),
        "o_ln2_b": nrm((N_ODD, D), 0.02),
    }

def reference(x, e_w_in, e_b_forget, e_sinks, e_w_out, e_ln1_g, e_ln1_b,
              e_w_gate, e_w_up, e_w_down, e_ln2_g, e_ln2_b,
              o_w_in, o_lambda_q1, o_lambda_k1, o_lambda_q2, o_lambda_k2, o_subln_g,
              o_w_out, o_ln1_g, o_ln1_b, o_w_router, o_w_gate, o_w_up, o_w_down,
              o_ln2_g, o_ln2_b):
    for layer in range(DEPTH):
        if layer % 2 == 0:
            i = layer // 2
            mix = even_mixer(x, e_w_in[i], e_b_forget[i], e_sinks[i], e_w_out[i])
            x = layer_norm(ALPHA * x + mix, e_ln1_g[i], e_ln1_b[i])
            ffn = swiglu(x, e_w_gate[i], e_w_up[i], e_w_down[i])
            x = layer_norm(ALPHA * x + ffn, e_ln2_g[i], e_ln2_b[i])
        else:
            i = layer // 2
            lambda_init = 0.8 - 0.6 * math.exp(-0.3 * layer)
            mix = odd_mixer(x, o_w_in[i], o_lambda_q1[i], o_lambda_k1[i], o_lambda_q2[i],
                            o_lambda_k2[i], o_subln_g[i], o_w_out[i], lambda_init)
            x = layer_norm(ALPHA * x + mix, o_ln1_g[i], o_ln1_b[i])
            ffn = moe_swiglu(x, o_w_router[i], o_w_gate[i], o_w_up[i], o_w_down[i])
            x = layer_norm(ALPHA * x + ffn, o_ln2_g[i], o_ln2_b[i])
    return x


_drawn_inputs = setup_inputs


def setup_inputs(seed=0):
    import zlib

    import numpy as np

    out = dict(_drawn_inputs(seed))
    spreads = {}
    factors = {'e_b_forget': 64.0,
     'e_sinks': 8.0,
     'o_lambda_q1': 3.264,
     'o_lambda_k1': 5.007,
     'o_lambda_q2': 3.233,
     'o_lambda_k2': 4.407,
     'o_subln_g': 7.521,
     'o_ln2_g': 7.793,
     'o_ln2_b': 7.844}
    for name, (base, spread) in spreads.items():
        noise = np.random.default_rng([zlib.crc32(name.encode()), seed]).standard_normal(out[name].shape)
        drawn = base * np.exp(spread * noise) if base else spread * noise
        out[name] = __import__('jax').numpy.asarray(drawn.astype(out[name].dtype))
    for name, factor in factors.items():
        out[name] = (out[name] * factor).astype(out[name].dtype)
    return out
```

```python
from contextlib import ExitStack

import numpy as np
import concourse.bass as bass
from concourse import mybir

ALU = mybir.AluOpType
ACT = mybir.ActivationFunctionType
AX_X = mybir.AxisListType.X
F32 = mybir.dt.float32
F32R = mybir.dt.float32r
I32 = mybir.dt.int32

P = 128
D = 1024
TOK = 256
TB = TOK // P
KT = D // P
CHUNK = 64
DH = 64
HEADS = 8
A_Q, A_KV, B_W = 512, 128, 512
D_FF = 2816
N_EXP = 8
D_FFE = 3584
ALPHA = 4.0 ** 0.25
EPS = 1e-5
LAMBDA_INIT = 0.8 - 0.6 * float(np.exp(-0.3))
BIG = 3.0e38

UNIT = 2048
FC = D_FF // 256
EC = D_FFE // 512
U_IN_E, U_OUT, U_FFN, U_IN_O = 10, 4, 3 * FC, 12
K_OUT_E = U_IN_E
K_FFN = K_OUT_E + U_OUT
K_IN_O = K_FFN + U_FFN
K_OUT_O = K_IN_O + U_IN_O
N_DENSE = K_OUT_O + U_OUT
PER_EXP = 6 * EC
SPLIT_AHEAD = 3
N_MOE = N_EXP * PER_EXP
N_PASS0 = N_MOE + SPLIT_AHEAD
DENSE_SLOTS = 7
SLOTS = 14
assert N_DENSE % DENSE_SLOTS == 0 and PER_EXP % SLOTS == 0
assert N_DENSE % SPLIT_AHEAD == 0 and PER_EXP % SPLIT_AHEAD == 0

FFN_ORDER = []
for _c in range(FC):
    FFN_ORDER += [("gate", _c), ("up", _c)] + ([("down", _c - 1)] if _c else [])
FFN_ORDER.append(("down", FC - 1))
EXP_ORDER = []
for _c in range(EC):
    EXP_ORDER += [("gate", _c, 0), ("gate", _c, 1), ("up", _c, 0), ("up", _c, 1)]
    if _c:
        EXP_ORDER += [("down", _c - 1, 0), ("down", _c - 1, 1)]
EXP_ORDER += [("down", EC - 1, 0), ("down", EC - 1, 1)]

C_ID, C_TRI, C_QS, C_IOTA, C_REV, C_END = 0, 128, 384, 388, 516, 524
BIAS_W = 384
B_A, B_B, B_C, B_END = 0, 384, 768, 1152

GROUPS = [("A", 0, 0), ("A", 1, 0), ("B", 0, 0), ("B", 1, 0),
          ("C", 0, 0), ("C", 0, 1), ("C", 1, 0), ("C", 1, 1)]
TR_BEFORE = [0]
for _g in GROUPS:
    TR_BEFORE.append(TR_BEFORE[-1] + 2 * (_g[1] + 1))


def slope(h):
    return 2.0 ** (-(h + 1))


def dense_slot(k):
    if k < N_DENSE:
        return k % DENSE_SLOTS, k // DENSE_SLOTS + 1
    return moe_slot(k - N_DENSE)


def moe_slot(m):
    s = (m + DENSE_SLOTS) % SLOTS
    return s, (N_DENSE // DENSE_SLOTS if s < DENSE_SLOTS else 0) + m // SLOTS + 1


def trunk(nc, x_in, w_dense, w_moe, cst, bias_cst, vec_rows, sinks, b_forget, lam_rows, subln, w_router, out):
    with ExitStack() as ctx:
        def sb(name, shape, dt=F32):
            return ctx.enter_context(nc.sbuf_tensor(name, shape, dt))

        def sem(name):
            return ctx.enter_context(nc.semaphore(name))

        raw = sb("raw", [P, SLOTS * UNIT])
        whi = sb("whi", [P, SPLIT_AHEAD, UNIT], F32R)
        wlo = sb("wlo", [P, SPLIT_AHEAD, UNIT], F32R)
        x = sb("x", [P, TB, D])
        acc = sb("acc", [P, TB, D])
        xth = sb("xth", [P, KT, TOK], F32R)
        xtl = sb("xtl", [P, KT, TOK], F32R)
        hth = sb("hth", [P, 512], F32R)
        htl = sb("htl", [P, 512], F32R)
        htmp = sb("htmp", [P, 512])
        work = sb("work", [P, 1536])
        con = sb("con", [P, C_END])
        wrh = sb("wrh", [P, KT, N_EXP], F32R)
        wrl = sb("wrl", [P, KT, N_EXP], F32R)
        mx = sb("mx", [P, 2, 8])
        negm = sb("negm", [P, 2, 8])
        sm = sb("sm", [P, 2, 8])
        den = sb("den", [P, 2, 8])
        rec = sb("rec", [P, 2, 8])
        snk = sb("snk", [P, 3, 8])
        logf = sb("logf", [P, TB, 8])
        stats = sb("stats", [P, TB, 2, 6])
        mv = sb("mv", [P, TB, 2])
        var = sb("var", [P, 2, 8])
        std = sb("std", [P, 2, 8])
        eps = sb("eps", [P, 1])
        lam = sb("lam", [P, 4])
        posm = sb("posm", [P, TB, 17])
        gates = sb("gates", [P, TB, 17])
        flag = sb("flag", [1, 1], I32)
        lgt = sb("lgt", [8, TOK])

        extra = raw[:, DENSE_SLOTS * UNIT:]
        qa = extra[:, 0:1024].rearrange("p (b t) -> p b t", t=TOK)
        ka = extra[:, 1024:1536].rearrange("p (b t) -> p b t", t=TOK)
        qb = extra[:, 1536:2560].rearrange("p (b t) -> p b t", t=TOK)
        kb = extra[:, 2560:3584].rearrange("p (b t) -> p b t", t=TOK)
        ve = extra[:, 3584:4864].rearrange("p (t n) -> p t n", t=TB)
        cumt = extra[:, 4864:5120]
        ncumt = extra[:, 5120:5376]
        fz = extra[:, 5376:5520].rearrange("p (i n) -> p i n", n=16)
        qo = extra[:, 0:2048].rearrange("p (b t) -> p b t", t=TOK)
        ko = extra[:, 2048:4096].rearrange("p (b t) -> p b t", t=TOK)
        vo = extra[:, 4096:6144].rearrange("p (t n) -> p t n", t=TB)
        S = [extra[:, 6144 + 2048 * i:8192 + 2048 * i].rearrange("p (h n) -> p h n", h=8) for i in range(2)]
        PT = [extra[:, 10240 + 2048 * i:12288 + 2048 * i].rearrange("p (k n) -> p k n", k=2) for i in range(2)]
        gb_extra = extra[:, 12288:14336].rearrange("p (i n) -> p i n", i=2)
        gb_last = raw[:, 0:2048].rearrange("p (i n) -> p i n", i=2)
        bias = work[:, 0:B_END]
        wr_raw = work[:, B_END:B_END + 64].rearrange("p (k n) -> p k n", n=8)
        sub_g = work[:, B_END + 64:B_END + 192]
        lam_in = work[:, B_END + 192:B_END + 384].rearrange("p (i n) -> p i n", n=DH)
        lam_in2 = sb("lam_in2", [P, DH])
        y = work[:, 0:1024]
        ohot = work[:, 1024:1280].rearrange("p (t s) -> p t s", t=TB)
        ohot_t = work[:, 1280:1536]
        rt = [htmp[:, 16 * i:16 * i + 16].rearrange("p (t n) -> p t n", t=TB) for i in range(16)]
        r1 = [htmp[:, 256 + 2 * i:258 + 2 * i] for i in range(8)]
        ident = con[:, C_ID:C_ID + 128]
        tri = con[:, C_TRI:C_TRI + 128]
        ones = con[:, C_TRI + 128:C_TRI + 256]
        iota = con[:, C_IOTA:C_IOTA + 128]
        revidx = con[:, C_REV:C_REV + 8]

        ps = [ctx.enter_context(nc.psum_tensor(f"ps{i}", [P, 512], F32)) for i in range(8)]

        loaded = [sem(f"loaded{i}") for i in range(SLOTS)]
        c_in = sem("consts_in")
        x_in_s = sem("x_in")
        small_in = sem("small_in")
        gb_in = sem("gain_bias_in")
        hi_rdy = sem("hi_ready")
        lo_rdy = sem("lo_ready")
        w_used = sem("w_used")
        src_rdy = sem("src_ready")
        xt_ps = sem("xt_in_psum")
        xth_rdy = sem("xth_ready")
        xtl_rdy = sem("xtl_ready")
        in_ev = sem("proj_evacuated")
        s_ps = sem("scores_in_psum")
        s_max = sem("scores_biased")
        neg_rdy = sem("negmax_ready")
        e_rdy = sem("exp_ready")
        snk_exp = sem("sink_exp_ready")
        tr_ps = sem("probs_t_in_psum")
        pt_ev = sem("probs_t_ready")
        o_ps = sem("attn_out_in_psum")
        o_ev = sem("attn_out_ready")
        fg_v = sem("forget_vector")
        fg_s = sem("forget_scalar")
        cum_ps = sem("cum_in_psum")
        cum_rdy = sem("cum_ready")
        lam_v = sem("lambda_sums")
        lam_s = sem("lambda_exps")
        var_rdy = sem("var_ready")
        std_rdy = sem("std_ready")
        f_ps = sem("ffn_in_psum")
        f_silu = sem("ffn_silu")
        f_h = sem("ffn_hidden")
        f_hi = sem("ffn_hidden_hi")
        f_lo = sem("ffn_hidden_lo")
        wr_h = sem("router_hi")
        wr_l = sem("router_lo")
        lg_ps = sem("logits_in_psum")
        lgt_rdy = sem("logits_t_ready")
        top_v = sem("top2_diff")
        top_s = sem("top2_exp")
        sel_rdy = sem("choice_ready")
        pos_ps = sem("positions_in_psum")
        flag_rdy = sem("flag_ready")
        m_ps = sem("expert_gate_up_in_psum")
        m_silu = sem("expert_silu")
        m_h = sem("expert_hidden")
        m_tr = sem("expert_hidden_t_in_psum")
        m_hi = sem("expert_hidden_hi")
        m_lo = sem("expert_hidden_lo")
        ga_ps = sem("gathered_in_psum")
        ga_hi = sem("gathered_hi")
        ga_lo = sem("gathered_lo")
        oh_rdy = sem("onehot_ready")
        oht_ps = sem("onehot_t_in_psum")
        oht_rdy = sem("onehot_t_ready")
        ye_rdy = sem("expert_out_ready")
        sc_ps = sem("scattered_in_psum")
        sc_acc = sem("scattered_added")
        dve_self = sem("vector_chain")
        act_self = sem("scalar_chain")
        stored = sem("stored")


        SCORE_ORDER = (0, 2, 1, 3, 4, 6, 5, 7)

        def score_at(h):
            return ps[2 * (h % 2) + h // 4], (h // 2 % 2) * 256

        def unit(t, j):
            return t[:, j % SPLIT_AHEAD, :]

        def as_cols(t, j):
            return unit(t, j).rearrange("p (k n) -> p k n", k=KT)

        def as_rows(t, j):
            return unit(t, j).rearrange("p (k n) -> p k n", k=2)

        def as_half(t, j):
            return unit(t, j).rearrange("p (k n) -> p k n", k=4)

        def yb(tb, n):
            return ps[4 + 2 * tb + n]

        block = ctx.enter_context(nc.Block())

        @block.sync
        def _(sp):
            def load(src, s):
                sp.dma_start(raw[:, s * UNIT:(s + 1) * UNIT], src).then_inc(loaded[s], 16)

            sp.dma_start(x[:, :, :], x_in.rearrange("a (t p) d -> p (a t) d", p=P)).then_inc(x_in_s, 16)
            for k in range(N_DENSE):
                if k >= DENSE_SLOTS:
                    sp.wait_ge(lo_rdy, k - DENSE_SLOTS + 1)
                load(w_dense[k], dense_slot(k)[0])
            for m in range(SLOTS):
                if m < DENSE_SLOTS - 1:
                    sp.wait_ge(o_ev, 8)
                elif m == DENSE_SLOTS - 1:
                    sp.wait_ge(src_rdy, 8)
                else:
                    sp.wait_ge(lo_rdy, N_DENSE + m - 2 * DENSE_SLOTS + 1)
                load(w_moe[m], moe_slot(m)[0])
            with sp.Fori(0, N_EXP - 1) as e:
                for j in range(PER_EXP):
                    sp.wait_ge(lo_rdy, e * PER_EXP + (N_DENSE + j + 1))
                    load(w_moe[e * PER_EXP + (SLOTS + j)], moe_slot(SLOTS + j)[0])
            for m in range(SLOTS + (N_EXP - 1) * PER_EXP, N_PASS0):
                sp.wait_ge(lo_rdy, N_DENSE + m - SLOTS + 1)
                load(w_moe[m], moe_slot(m)[0])
            sp.wait_ge(flag_rdy, 1)
            more = sp.value_load(flag[0:1, 0:1], min_val=0, max_val=1)
            with sp.If(more > 0):
                with sp.Fori(N_EXP, 2 * N_EXP) as e:
                    for j in range(PER_EXP):
                        m0 = SPLIT_AHEAD + j
                        sp.wait_ge(lo_rdy, e * PER_EXP + (N_DENSE + m0 - SLOTS + 1))
                        load(w_moe[(e - N_EXP) * PER_EXP + m0], moe_slot(m0)[0])
            with sp.Else():
                sp.nop()
            for tb in range(TB):
                sp.wait_ge(src_rdy, 9 + tb)
                sp.dma_start(out[0, tb * P:(tb + 1) * P, :], x[:, tb, :]).then_inc(stored, 16)
            sp.wait_ge(stored, 32)

        @block.gpsimd
        def _(pool):
            pool.dma_start(con[:, :], cst).then_inc(c_in, 16)
            pool.dma_start(bias, bias_cst).then_inc(small_in, 16)
            pool.dma_start(snk[:, 0, :], sinks.partition_broadcast(P)).then_inc(small_in, 16)
            pool.dma_start(snk[:, 2, :], b_forget.partition_broadcast(P)).then_inc(small_in, 16)
            pool.dma_start(lam_in, lam_rows[0:3].partition_broadcast(P)).then_inc(small_in, 16)
            pool.dma_start(lam_in2[:, :], lam_rows[3].partition_broadcast(P)).then_inc(small_in, 16)
            pool.dma_start(sub_g, subln.partition_broadcast(P)).then_inc(small_in, 16)
            pool.dma_start(wr_raw, w_router).then_inc(small_in, 16)
            for n, (s, v) in enumerate(((o_ev, 4), (src_rdy, 2), (o_ev, 8))):
                pool.wait_ge(s, v)
                pool.dma_start(gb_extra, vec_rows[n].partition_broadcast(P)).then_inc(gb_in, 16)
            pool.wait_ge(flag_rdy, 1)
            more = pool.value_load(flag[0:1, 0:1], min_val=0, max_val=1)
            with pool.If(more > 0):
                pool.wait_ge(lo_rdy, N_DENSE + N_MOE + N_PASS0)
            with pool.Else():
                pool.wait_ge(lo_rdy, N_DENSE + N_PASS0)
            pool.dma_start(gb_last, vec_rows[3].partition_broadcast(P)).then_inc(gb_in, 16)

        @block.tensor
        def _(pe):
            mm = pe.matmul

            def three(o, lh, ll, rh, rl, start, stop):
                mm(o, lh, rh, start=start, stop=False)
                mm(o, lh, rl, start=False, stop=False)
                return mm(o, ll, rh, start=False, stop=stop)

            def turn(t, banks=(0, 1, 2, 3)):
                src = acc if t in (1, 4) else x
                for tb in range(TB):
                    if t == 0:
                        pe.wait_ge(x_in_s, 16)
                        pe.wait_ge(c_in, 16)
                    elif t == 1:
                        pe.wait_ge(o_ev, 3 + tb)
                    else:
                        pe.wait_ge(src_rdy, 2 * (t - 2) + tb + 1)
                    for half in range(2):
                        for i in range(4):
                            kt = 4 * half + i
                            r = pe.transpose(ps[banks[2 * tb + half]][:, i * P:(i + 1) * P],
                                             src[:, tb, kt * P:(kt + 1) * P], ident)
                        r.then_inc(xt_ps, 1)
                pe.wait_ge(xth_rdy, 4 * (t + 1))
                pe.wait_ge(xtl_rdy, 4 * (t + 1))

            def to_rows(k, bank):
                h, l = as_cols(whi, k), as_cols(wlo, k)
                for b in range(2):
                    for kt in range(KT):
                        c = slice(b * P, b * P + P)
                        r = three(ps[bank][:, b * TOK:(b + 1) * TOK], h[:, kt, c], l[:, kt, c],
                                  xth[:, kt, :], xtl[:, kt, :], kt == 0, kt == KT - 1)
                return r

            def to_cols(k, bank, n):
                h, l = as_cols(whi, k), as_cols(wlo, k)
                for tb in range(TB):
                    for kt in range(KT):
                        t = slice(tb * P, tb * P + P)
                        r = three(ps[bank][:, tb * 256:tb * 256 + n], xth[:, kt, t], xtl[:, kt, t],
                                  h[:, kt, 0:n], l[:, kt, 0:n], kt == 0, kt == KT - 1)
                return r

            def project(k0, n_t, widths):
                for i in range(n_t + len(widths)):
                    k = k0 + i
                    seen = (k - k0) + (0 if k0 == 0 else U_IN_E)
                    if i >= 4:
                        pe.wait_ge(in_ev, seen - 3)
                    pe.wait_ge(lo_rdy, k + 1)
                    if i < n_t:
                        r = to_rows(k, 4 + i % 4)
                    else:
                        r = to_cols(k, 4 + i % 4, widths[i - n_t])
                    r.then_inc(w_used, 1)

            def attention(layer):
                gs = range(4 * layer, 4 * layer + 4)
                pe.wait_ge(in_ev, U_IN_E if layer == 0 else U_IN_E + U_IN_O)

                def scores(g):
                    kind, qblk, mp = GROUPS[g]
                    nk = P * (qblk + 1)
                    q_cols = slice(qblk * P, qblk * P + P)
                    if g % 4:
                        pe.wait_ge(s_max, 8 * g)
                    if kind == "B" and qblk == 0:
                        cumulate()
                    for h in SCORE_ORDER:
                        rows = slice(64 * (h % 2), 64 * (h % 2) + 64)
                        if kind == "A":
                            q, kk = qa[rows, h // 2, q_cols], ka[rows, int(h // 4 != h % 2), 0:nk]
                        elif kind == "B":
                            q, kk = qb[rows, h // 2, q_cols], kb[rows, h // 2, 0:nk]
                        else:
                            b = 4 * mp + h // 2
                            q, kk = qo[rows, b, q_cols], ko[rows, b, 0:nk]
                        bank, c0 = score_at(h)
                        o = bank[:, c0:c0 + nk]
                        r = mm(o, q, kk, start=True, stop=kind != "B")
                        if kind == "B":
                            r0 = 64 * (h % 2)
                            pick = ident[r0:r0 + 8, r0 + h:r0 + h + 1]
                            mm(o, pick.to_broadcast([8, P]), ncumt[r0:r0 + 8, 0:nk], start=False, stop=False)
                            r = mm(o, cumt[r0:r0 + 8, q_cols], pick.to_broadcast([8, nk]), start=False, stop=True)
                        if h & 2:
                            r.then_inc(s_ps, 1)

                def cumulate():
                    pe.wait_ge(fg_v, 4)
                    for r0 in (0, 64):
                        mm(ps[7][r0:r0 + 8, 0:P], logf[:, 0, :], tri, start=True, stop=True)
                        mm(ps[7][r0:r0 + 8, P:TOK], logf[:, 0, :], ones, start=True, stop=False)
                        r = mm(ps[7][r0:r0 + 8, P:TOK], logf[:, 1, :], tri, start=False, stop=True)
                    r.then_inc(cum_ps, 1)
                    pe.wait_ge(cum_rdy, 1)

                def turn_probs(g):
                    n = TR_BEFORE[g]
                    for kt in range(GROUPS[g][1] + 1):
                        for half in range(2):
                            if n >= 2:
                                pe.wait_ge(pt_ev, n - 1)
                            pe.wait_ge(e_rdy, 8 * g + 4 * half + 4)
                            for i in range(4):
                                r = pe.transpose(ps[4 + half][:, i * P:(i + 1) * P],
                                                 S[g % 2][:, 4 * half + i, kt * P:(kt + 1) * P], ident)
                            r.then_inc(tr_ps, 1)
                            n += 1

                def values(g):
                    kind, qblk, _ = GROUPS[g]
                    pe.wait_ge(pt_ev, TR_BEFORE[g + 1])
                    if g >= 2:
                        pe.wait_ge(o_ev, g if kind == "C" else g - 1)
                    for h in range(8):
                        if kind == "C":
                            o = ps[6 + h // 4][:, (h % 4) * P:(h % 4) * P + P]
                        else:
                            o = ps[6 + g % 2][:, h * DH:(h + 1) * DH]
                        for kt in range(qblk + 1):
                            if kind == "A":
                                v = ve[:, kt, B_W + (h // 4) * DH:B_W + (h // 4) * DH + DH]
                            elif kind == "B":
                                v = ve[:, kt, h * DH:(h + 1) * DH]
                            else:
                                v = vo[:, kt, h * P:(h + 1) * P]
                            r = mm(o, PT[g % 2][:, kt, h * P:(h + 1) * P], v, start=kt == 0, stop=kt == qblk)
                    r.then_inc(o_ps, 1)

                scores(gs[0])
                for g in gs:
                    if g + 1 in gs:
                        scores(g + 1)
                    turn_probs(g)
                    values(g)

            def mix_rows(k, i, n_rows, lh, ll):
                h, l = as_rows(whi, k), as_rows(wlo, k)
                for r2 in range(2):
                    for tb in range(TB):
                        for n in range(2):
                            c = slice(n * 512, n * 512 + 512)
                            r = three(yb(tb, n)[:, :], lh(r2, tb), ll(r2, tb), h[:, r2, c], l[:, r2, c],
                                      i == 0 and r2 == 0, i == n_rows - 1 and r2 == 1)
                r.then_inc(w_used, 1)

            def out_proj(k0):
                for i in range(U_OUT):
                    pe.wait_ge(lo_rdy, k0 + i + 1)
                    mix_rows(k0 + i, i, U_OUT,
                             lambda r2, tb: xth[:, 2 * i + r2, tb * P:(tb + 1) * P],
                             lambda r2, tb: xtl[:, 2 * i + r2, tb * P:(tb + 1) * P])

            turn(0)
            project(0, 7, [256, 256, 136])
            attention(0)
            turn(1)
            out_proj(K_OUT_E)
            turn(2)
            for i, (what, c) in enumerate(FFN_ORDER):
                k = K_FFN + i
                pe.wait_ge(lo_rdy, k + 1)
                if what == "down":
                    pe.wait_ge(f_lo, c + 1)
                    mix_rows(k, c, FC,
                             lambda r2, tb: hth[:, r2 * TOK + tb * P:r2 * TOK + (tb + 1) * P],
                             lambda r2, tb: htl[:, r2 * TOK + tb * P:r2 * TOK + (tb + 1) * P])
                else:
                    if what == "gate" and c >= 2:
                        pe.wait_ge(f_h, c - 1)
                    r = to_rows(k, (0 if what == "gate" else 2) + c % 2)
                    r.then_inc(w_used, 1)
            turn(3)
            project(K_IN_O, 8, [256] * 4)
            attention(1)
            turn(4)
            out_proj(K_OUT_O)
            turn(5)

            pe.wait_ge(wr_l, 1)
            for kt in range(KT):
                for i, (a, b) in enumerate(((wrh, xth), (wrh, xtl), (wrl, xth), (wrl, xtl))):
                    r = mm(ps[0][0:8, 0:TOK], a[:, kt, :], b[:, kt, :],
                           start=kt == 0 and i == 0, stop=kt == KT - 1 and i == 3)
            r.then_inc(lg_ps, 1)
            pe.wait_ge(lgt_rdy, 1)
            for tb in range(TB):
                r = pe.transpose(ps[2][:, tb * 8:tb * 8 + 8], lgt[:, tb * P:(tb + 1) * P], ident[0:8, 0:8])
            r.then_inc(lg_ps, 1)
            pe.wait_ge(sel_rdy, 1)
            chosen = rt[10]
            mm(ps[1][:, 0:8], tri, chosen[:, 0, :], start=True, stop=True)
            mm(ps[1][:, 8:16], ones, chosen[:, 0, :], start=True, stop=False)
            mm(ps[1][:, 8:16], tri, chosen[:, 1, :], start=False, stop=True)
            mm(ps[1][0:1, 16:24], ones[:, 0:1], chosen[:, 0, :], start=True, stop=False)
            mm(ps[1][0:1, 16:24], ones[:, 0:1], chosen[:, 1, :], start=False, stop=True).then_inc(pos_ps, 1)

            def gather(n):
                pe.wait_ge(oh_rdy, n + 1)
                for kt in range(KT):
                    bank = ps[1 if kt < 4 else 3]
                    for tb in range(TB):
                        r = mm(bank[:, (kt % 4) * P:(kt % 4) * P + P], x[:, tb, kt * P:(kt + 1) * P],
                               ohot[:, tb, :], start=tb == 0, stop=tb == TB - 1)
                r.then_inc(ga_ps, 1)

            def scatter(n, tb):
                if tb == 0:
                    pe.wait_ge(ye_rdy, n + 1)
                    pe.wait_ge(oht_rdy, n + 1)
                for nn in range(2):
                    i = 2 * tb + nn
                    if tb == 1:
                        pe.wait_ge(sc_acc, n * 4 + (i - 1))
                    mm(ps[7 if i % 2 == 0 else 4][:, :], ohot_t[:, tb * P:(tb + 1) * P],
                       y[:, nn * 512:(nn + 1) * 512], start=True, stop=True).then_inc(sc_ps, 1)

            def expert(e):
                def hidden_t(c):
                    pe.wait_ge(m_h, e * EC + (c + 1))
                    if c == 0:
                        pe.wait_ge(sc_acc, e * 4 + 4)
                    for i in range(4):
                        r = pe.transpose(ps[4][:, i * P:(i + 1) * P], htmp[:, i * P:(i + 1) * P], ident)
                    r.then_inc(m_tr, 1)

                for j, (what, c, half) in enumerate(EXP_ORDER):
                    if j == 0:
                        pe.wait_ge(ga_lo, e + 1)
                    pe.wait_ge(lo_rdy, e * PER_EXP + (N_DENSE + j + 1))
                    if what == "down":
                        if half == 0:
                            pe.wait_ge(m_lo, e * EC + (c + 1))
                        h, l = as_rows(whi, j), as_rows(wlo, j)
                        for r2 in range(2):
                            f = slice((2 * half + r2) * P, (2 * half + r2 + 1) * P)
                            for n in range(2):
                                cc = slice(n * 512, n * 512 + 512)
                                r = three(ps[5 + n][:, :], hth[:, f], htl[:, f], h[:, r2, cc], l[:, r2, cc],
                                          c == 0 and half == 0 and r2 == 0,
                                          c == EC - 1 and half == 1 and r2 == 1)
                    else:
                        bank = ps[(0 if what == "gate" else 2) + c % 2]
                        h, l = as_half(whi, j), as_half(wlo, j)
                        for i in range(4):
                            kt = 4 * half + i
                            r = three(bank[:, :], xth[:, kt, 0:P], xtl[:, kt, 0:P], h[:, i, :], l[:, i, :],
                                      kt == 0, kt == KT - 1)
                    r.then_inc(w_used, 1)
                    if j == 1:
                        scatter(e, 0)
                    if j == 3:
                        scatter(e, 1)
                    if j == 5:
                        pe.wait_ge(sc_acc, e * 4 + 3)
                        for tb in range(TB):
                            r = pe.transpose(ps[7][:, tb * P:(tb + 1) * P], ohot[:, tb, :], ident)
                        r.then_inc(oht_ps, 1)
                    if (what, half) == ("gate", 1) and c:
                        hidden_t(c - 1)
                    if j == PER_EXP - 3:
                        hidden_t(EC - 1)
                        gather(e + 1)

            gather(0)
            with pe.Fori(0, N_EXP) as e:
                expert(e)
            pe.wait_ge(flag_rdy, 1)
            more = pe.value_load(flag[0:1, 0:1], min_val=0, max_val=1)
            with pe.If(more > 0):
                with pe.Fori(N_EXP, 2 * N_EXP) as e:
                    expert(e)
                scatter(2 * N_EXP, 0)
                scatter(2 * N_EXP, 1)
            with pe.Else():
                scatter(N_EXP, 0)
                scatter(N_EXP, 1)

        @block.scalar
        def _(act):
            A = act.activation

            def hi(wait, used, j, slot):
                act.wait_ge(loaded[slot], wait)
                if used is not None:
                    act.wait_ge(w_used, used)
                A(unit(whi, j), raw[:, slot * UNIT:(slot + 1) * UNIT], ACT.Copy).then_inc(hi_rdy, 1)

            def split(k):
                s, n = dense_slot(k)
                hi(16 * n, k - SPLIT_AHEAD + 1 if k >= SPLIT_AHEAD else None, k, s)

            def turned(t, banks=(0, 1, 2, 3)):
                for i in range(4):
                    tb, half = divmod(i, 2)
                    act.wait_ge(xt_ps, 4 * t + i + 1)
                    A(xth[:, 4 * half:4 * half + 4, tb * P:(tb + 1) * P],
                      ps[banks[i]][:, :].rearrange("p (k n) -> p k n", k=4), ACT.Copy).then_inc(xth_rdy, 1)

            def root(n, i, w, scale=1.0):
                act.wait_ge(var_rdy, n + 1)
                A(std[:, i, 0:w], var[:, i, 0:w], ACT.Sqrt, bias=eps[:, 0:1], scale=scale).then_inc(std_rdy, 1)

            def exps(g):
                act.wait_ge(neg_rdy, g + 1)
                nk = P * (GROUPS[g][1] + 1)
                for h in range(8):
                    A(S[g % 2][:, h, 0:nk], S[g % 2][:, h, 0:nk], ACT.Exp, bias=negm[:, g % 2, h:h + 1],
                      accum_out=sm[:, g % 2, h:h + 1]).then_inc(e_rdy, 1)
                if GROUPS[g][0] == "A":
                    A(den[:, g % 2, :], den[:, g % 2, :], ACT.Exp).then_inc(snk_exp, 1)

            def attention(layer):
                gs = range(4 * layer, 4 * layer + 4)
                exps(gs[0])
                for g in gs:
                    n = TR_BEFORE[g]
                    if g >= 2:
                        act.wait_ge(o_ps, g - 1)
                    for kt in range(GROUPS[g][1] + 1):
                        for half in range(2):
                            act.wait_ge(tr_ps, n + 1)
                            A(PT[g % 2][:, kt, half * 512:(half + 1) * 512], ps[4 + half][:, :],
                              ACT.Copy).then_inc(pt_ev, 1)
                            n += 1
                    if g == 0:
                        act.wait_ge(cum_ps, 1)
                        for r0 in (0, 64):
                            A(cumt[r0:r0 + 8, :], ps[7][r0:r0 + 8, 0:TOK], ACT.Copy)
                            r = A(ncumt[r0:r0 + 8, :], ps[7][r0:r0 + 8, 0:TOK], ACT.Copy, scale=-1.0)
                        r.then_inc(cum_rdy, 1)
                    if g + 1 in gs:
                        exps(g + 1)
                    if g in (5, 7):
                        root(4 + (g - 5) // 2, (g - 5) // 2, 8, 1.0 / P)

            def evac_even(i):
                b = ps[4 + i % 4][:, :].rearrange("p (b t) -> p b t", b=2)
                act.wait_ge(w_used, i + 1)
                if i < 2:
                    for s in range(2):
                        r = A(qa[:, 2 * i + s, :], b[:, s, :], ACT.Copy, scale=con[:, C_QS + 2 * i + s:C_QS + 2 * i + s + 1])
                elif i == 2:
                    r = A(ka[:, :, :], b, ACT.Copy)
                elif i < 5:
                    r = A(qb[:, 2 * (i - 3):2 * (i - 3) + 2, :], b, ACT.Copy, scale=DH ** -0.5)
                elif i < 7:
                    r = A(kb[:, 2 * (i - 5):2 * (i - 5) + 2, :], b, ACT.Copy)
                elif i < 9:
                    r = A(ve[:, :, (i - 7) * 256:(i - 6) * 256], b, ACT.Copy)
                else:
                    A(ve[:, :, B_W:B_W + A_KV], b[:, :, 0:A_KV], ACT.Copy)
                    r = A(fz[:, 0, :].rearrange("p (t n) -> p t n", t=TB), b[:, :, A_KV:A_KV + 8], ACT.Copy)
                r.then_inc(in_ev, 1)

            def evac_odd(i):
                b = ps[4 + i % 4][:, :].rearrange("p (b t) -> p b t", b=2)
                act.wait_ge(w_used, K_IN_O + i + 1)
                if i < 4:
                    for s in range(2):
                        blk = 2 * i + s
                        r = A(qo[:, blk, :], b[:, s, :], ACT.Copy, scale=con[:, C_QS + blk % 4:C_QS + blk % 4 + 1])
                elif i < 8:
                    r = A(ko[:, 2 * (i - 4):2 * (i - 4) + 2, :], b, ACT.Copy)
                else:
                    r = A(vo[:, :, (i - 8) * 256:(i - 7) * 256], b, ACT.Copy)
                r.then_inc(in_ev, 1)

            act.wait_ge(c_in, 16)
            split(0)
            turned(0)
            split(1)
            split(2)
            act.wait_ge(small_in, 7 * 16)
            A(wrh[:, :, :], wr_raw, ACT.Copy).then_inc(wr_h, 1)
            act.wait_ge(lam_v, 1)
            A(lam[:, 0:2], lam[:, 0:2], ACT.Exp).then_inc(lam_s, 1)
            for k in range(N_DENSE):
                split(k + SPLIT_AHEAD)
                if k < U_IN_E:
                    evac_even(k)
                if k == U_IN_E - 1:
                    act.wait_ge(fg_v, 1)
                    A(fz[:, 2, :], fz[:, 2, :], ACT.Exp, scale=-1.0).then_inc(fg_s, 1)
                    act.wait_ge(fg_v, 2)
                    A(fz[:, 4, :], fz[:, 3, :], ACT.Ln).then_inc(fg_s, 1)
                    attention(0)
                    turned(1)
                if k == K_FFN - 1:
                    root(0, 0, 1)
                    root(1, 1, 1)
                    turned(2)
                if K_FFN <= k < K_IN_O:
                    what, c = FFN_ORDER[k - K_FFN]
                    if what == "up":
                        act.wait_ge(w_used, k + 1)
                        if c:
                            act.wait_ge(f_lo, c)
                        A(htmp[:, :], ps[c % 2][:, :], ACT.Silu).then_inc(f_silu, 1)
                        if c == 0:
                            act.wait_ge(f_h, 1)
                            A(hth[:, :], htmp[:, :], ACT.Copy).then_inc(f_hi, 1)
                    if what == "down" and c < FC - 1:
                        act.wait_ge(w_used, k + 1)
                        act.wait_ge(f_h, c + 2)
                        A(hth[:, :], htmp[:, :], ACT.Copy).then_inc(f_hi, 1)
                if k == K_IN_O - 1:
                    root(2, 0, 1)
                    root(3, 1, 1)
                    turned(3)
                if K_IN_O <= k < K_OUT_O:
                    evac_odd(k - K_IN_O)
                if k == K_OUT_O - 1:
                    attention(1)
                    turned(4)
            root(6, 0, 1)
            root(7, 1, 1)
            turned(5)
            act.wait_ge(top_v, 1)
            A(r1[3], r1[2], ACT.Exp).then_inc(top_s, 1)
            act.wait_ge(flag_rdy, 1)
            A(y, iota.unsqueeze(1).to_broadcast([P, 8, P]), ACT.Copy, scale=0.0).then_inc(ye_rdy, 1)
            A(ohot_t, con[:, 0:256], ACT.Copy, scale=0.0).then_inc(oht_rdy, 1)

            def gathered(n):
                for q in range(2):
                    act.wait_ge(ga_ps, n + 1)
                    r = A(xth[:, 4 * q:4 * q + 4, 0:P], ps[1 + 2 * q][:, :].rearrange("p (k n) -> p k n", k=4), ACT.Copy)
                r.then_inc(ga_hi, 1)

            def expert(e):
                for j, (what, c, half) in enumerate(EXP_ORDER):
                    s, n = moe_slot(j + SPLIT_AHEAD)
                    if j != PER_EXP - 3:
                        hi(e * (16 * (PER_EXP // SLOTS)) + 16 * n, e * PER_EXP + (N_DENSE + j + 1), j, s)
                    if j == 6:
                        act.wait_ge(oht_ps, e + 1)
                        A(ohot_t, ps[7][:, 0:256], ACT.Copy).then_inc(oht_rdy, 1)
                    if (what, half) == ("up", 1):
                        act.wait_ge(w_used, e * PER_EXP + (N_DENSE + j + 1))
                        A(htmp[:, :], ps[c % 2][:, :], ACT.Silu).then_inc(m_silu, 1)
                    if ((what, half) == ("gate", 1) and c) or j == PER_EXP - 3:
                        act.wait_ge(m_tr, e * EC + (c if j != PER_EXP - 3 else EC))
                        A(hth[:, :], ps[4][:, :], ACT.Copy).then_inc(m_hi, 1)
                    if j == PER_EXP - 3:
                        hi(e * (16 * (PER_EXP // SLOTS)) + 16 * n, e * PER_EXP + (N_DENSE + j + 1), j, s)
                        gathered(e + 1)
                    if j == PER_EXP - 1:
                        act.wait_ge(w_used, e * PER_EXP + (N_DENSE + j + 1))
                        for nn in range(2):
                            r = A(y[:, nn * 512:(nn + 1) * 512], ps[5 + nn][:, :], ACT.Copy)
                        r.then_inc(ye_rdy, 1)

            gathered(0)
            A(r1[3], r1[3], ACT.Silu)
            with act.Fori(0, N_EXP) as e:
                expert(e)
            more = act.value_load(flag[0:1, 0:1], min_val=0, max_val=1)
            with act.If(more > 0):
                with act.Fori(N_EXP, 2 * N_EXP) as e:
                    expert(e)
            with act.Else():
                act.nop()
            root(8, 0, 1)
            root(9, 1, 1)

        @block.vector
        def _(dve):
            chained = [0]

            def link(r):
                chained[0] += 1
                r.then_inc(dve_self, 1)
                dve.wait_ge(dve_self, chained[0])

            def lo(count, j, slot):
                dve.wait_ge(hi_rdy, count)
                dve.tensor_tensor(unit(wlo, j), raw[:, slot * UNIT:(slot + 1) * UNIT],
                                  unit(whi, j).bitcast(F32), ALU.subtract).then_inc(lo_rdy, 1)

            def split(k):
                lo(k + 1, k, dense_slot(k)[0])

            def turned(t, banks=(0, 1, 2, 3)):
                for i in range(4):
                    tb, half = divmod(i, 2)
                    part = (slice(None), slice(4 * half, 4 * half + 4), slice(tb * P, (tb + 1) * P))
                    dve.wait_ge(xth_rdy, 4 * t + i + 1)
                    dve.tensor_tensor(xtl[part], ps[banks[i]][:, :].rearrange("p (k n) -> p k n", k=4),
                                      xth[part].bitcast(F32), ALU.subtract).then_inc(xtl_rdy, 1)

            def score_max(g):
                kind, qblk, _ = GROUPS[g]
                nk = P * (qblk + 1)
                b0 = {"A": B_A, "B": B_B, "C": B_C}[kind] + P * qblk
                if g % 4 >= 2:
                    dve.wait_ge(tr_ps, TR_BEFORE[g - 1])
                for i, h in enumerate(SCORE_ORDER):
                    dve.wait_ge(s_ps, 4 * g + i // 2 + 1)
                    bank, c0 = score_at(h)
                    dve.tensor_tensor_reduce(
                        out=S[g % 2][:, h, 0:nk], in0=bank[:, c0:c0 + nk],
                        in1=bias[:, b0:b0 + nk], scale=1.0 if kind == "B" else slope(h), scalar=-BIG,
                        op0=ALU.add, op1=ALU.max, accum_out=mx[:, g % 2, h:h + 1]).then_inc(s_max, 1)
                dve.wait_ge(s_max, 8 * g + 8)
                if kind == "A":
                    link(dve.scalar_tensor_tensor(out=negm[:, g % 2, :], in0=mx[:, g % 2, :], scalar=-1.0,
                                                  in1=snk[:, 1, :], op0=ALU.mult, op1=ALU.min))
                    dve.tensor_tensor(den[:, g % 2, :], snk[:, 0, :], negm[:, g % 2, :], ALU.add).then_inc(neg_rdy, 1)
                else:
                    dve.tensor_scalar(negm[:, g % 2, :], mx[:, g % 2, :], -1.0, None, ALU.mult).then_inc(neg_rdy, 1)

            def head_out(g):
                kind, qblk, mp = GROUPS[g]
                r8 = rec[:, g % 2, :]
                dve.wait_ge(e_rdy, 8 * g + 8)
                if kind == "A":
                    dve.wait_ge(snk_exp, g + 1)
                    link(dve.tensor_tensor(sm[:, g % 2, :], sm[:, g % 2, :], den[:, g % 2, :], ALU.add))
                link(dve.reciprocal(r8, sm[:, g % 2, :]))
                if kind == "C" and mp == 1:
                    link(dve.tensor_scalar(r8, r8, lam[:, 3:4], None, ALU.mult))
                dve.wait_ge(o_ps, g + 1)
                if kind != "C":
                    o = acc[:, qblk, (0 if kind == "A" else 512):(512 if kind == "A" else 1024)]
                    r = dve.tensor_tensor(o.rearrange("p (h n) -> p h n", h=8),
                                          ps[6 + g % 2][:, :].rearrange("p (h n) -> p h n", h=8),
                                          r8.unsqueeze(2).to_broadcast([P, 8, DH]), ALU.mult)
                    r.then_inc(o_ev, 1)
                    return
                for half in range(2):
                    o = acc[:, qblk, half * 512:(half + 1) * 512].rearrange("p (h n) -> p h n", h=4)
                    p4 = ps[6 + half][:, :].rearrange("p (h n) -> p h n", h=4)
                    rb = r8[:, 4 * half:4 * half + 4].unsqueeze(2).to_broadcast([P, 4, P])
                    if mp == 0:
                        r = dve.tensor_tensor(o, p4, rb, ALU.mult)
                        if half == 0:
                            link(r)
                    else:
                        t = htmp[:, :].rearrange("p (h n) -> p h n", h=4)
                        link(dve.tensor_tensor(t, p4, rb, ALU.mult))
                        r = dve.tensor_tensor(o, o, t, ALU.add)
                        if half == 0:
                            link(r)
                r.then_inc(o_ev, 1)
                dve.wait_ge(o_ev, g + 1)

            def head_norm(qblk):
                for half in range(2):
                    o = acc[:, qblk, half * 512:(half + 1) * 512]
                    link(dve.tensor_tensor(htmp[:, :], o, o, ALU.mult))
                    r = dve.reduce_sum(var[:, qblk, 4 * half:4 * half + 4],
                                       htmp[:, :].rearrange("p (h n) -> p h n", h=4), axis=AX_X)
                    if half == 0:
                        link(r)
                r.then_inc(var_rdy, 1)

            def head_norm_end(qblk):
                dve.wait_ge(std_rdy, 5 + qblk)
                link(dve.reciprocal(std[:, qblk, :], std[:, qblk, :]))
                o = acc[:, qblk, :].rearrange("p (h n) -> p h n", h=8)
                link(dve.tensor_tensor(o, o, std[:, qblk, :].unsqueeze(2).to_broadcast([P, 8, P]), ALU.mult))
                dve.tensor_tensor(o, o, sub_g.unsqueeze(1).to_broadcast([P, 8, P]), ALU.mult).then_inc(src_rdy, 1)

            def attention(layer):
                gs = range(4 * layer, 4 * layer + 4)
                score_max(gs[0])
                for g in gs:
                    if g + 1 in gs:
                        score_max(g + 1)
                    head_out(g)
                    if g in (5, 7):
                        head_norm((g - 5) // 2)
                        head_norm_end((g - 5) // 2)

            def norm(n, roots, gb, units=None):
                if units is not None:
                    dve.wait_ge(w_used, units)
                for tb in range(TB):
                    for h in range(2):
                        c = slice(h * 512, h * 512 + 512)
                        if units is not None:
                            link(dve.scalar_tensor_tensor(out=acc[:, tb, c], in0=x[:, tb, c], scalar=ALPHA,
                                                          in1=yb(tb, h)[:, :], op0=ALU.mult, op1=ALU.add))
                        link(dve.bn_stats(stats[:, tb, h, :], acc[:, tb, c]))
                    link(dve.bn_aggr(mv[:, tb, :], stats[:, tb, :, :]))
                    dve.tensor_copy(var[:, tb, 0:1], mv[:, tb, 1:2]).then_inc(var_rdy, 1)
                dve.wait_ge(gb_in, 16 * (n + 1))
                for tb in range(TB):
                    dve.wait_ge(std_rdy, roots + tb + 1)
                    link(dve.reciprocal(std[:, tb, 0:1], std[:, tb, 0:1]))
                    link(dve.tensor_scalar(x[:, tb, :], acc[:, tb, :], mv[:, tb, 0:1], std[:, tb, 0:1],
                                           ALU.subtract, ALU.mult))
                    link(dve.tensor_tensor(x[:, tb, :], x[:, tb, :], gb[:, 0, :], ALU.mult))
                    dve.tensor_tensor(x[:, tb, :], x[:, tb, :], gb[:, 1, :], ALU.add).then_inc(src_rdy, 1)

            link(dve.memset(eps[:, :], EPS))
            dve.wait_ge(c_in, 16)
            split(0)
            turned(0)
            split(1)
            split(2)
            dve.wait_ge(small_in, 7 * 16)
            dve.wait_ge(wr_h, 1)
            dve.tensor_tensor(wrl[:, :, :], wr_raw, wrh[:, :, :].bitcast(F32), ALU.subtract).then_inc(wr_l, 1)
            link(dve.tensor_scalar(snk[:, 1, :], snk[:, 0, :], -1.0, None, ALU.mult))
            link(dve.tensor_tensor_reduce(out=htmp[:, 0:DH], in0=lam_in[:, 0, :], in1=lam_in[:, 1, :], scale=1.0,
                                          scalar=0.0, op0=ALU.mult, op1=ALU.add, accum_out=lam[:, 0:1]))
            dve.tensor_tensor_reduce(out=htmp[:, DH:2 * DH], in0=lam_in[:, 2, :], in1=lam_in2[:, :], scale=1.0,
                                     scalar=0.0, op0=ALU.mult, op1=ALU.add, accum_out=lam[:, 1:2]).then_inc(lam_v, 1)
            dve.wait_ge(lam_s, 1)
            link(dve.tensor_tensor(lam[:, 2:3], lam[:, 1:2], lam[:, 0:1], ALU.subtract))
            link(dve.tensor_scalar(lam[:, 3:4], lam[:, 2:3], -LAMBDA_INIT, None, ALU.add))
            link(dve.tensor_scalar(sub_g, sub_g, 1.0 - LAMBDA_INIT, None, ALU.mult))

            for k in range(N_DENSE):
                split(k + SPLIT_AHEAD)
                if k == U_IN_E - 1:
                    dve.wait_ge(in_ev, U_IN_E)
                    for tb in range(TB):
                        link(dve.tensor_tensor(fz[:, 1, 8 * tb:8 * tb + 8], fz[:, 0, 8 * tb:8 * tb + 8],
                                               snk[:, 2, :], ALU.add))
                    dve.scalar_tensor_tensor(out=fz[:, 2, :], in0=fz[:, 1, :], scalar=-1.0, in1=fz[:, 1, :],
                                             op0=ALU.mult, op1=ALU.max).then_inc(fg_v, 1)
                    dve.wait_ge(fg_s, 1)
                    dve.tensor_scalar(fz[:, 3, :], fz[:, 2, :], 1.0, None, ALU.add).then_inc(fg_v, 1)
                    dve.wait_ge(fg_v, 2)
                    link(dve.tensor_scalar(fz[:, 5, :], fz[:, 3, :], -1.0, None, ALU.add))
                    link(dve.tensor_tensor(fz[:, 5, :], fz[:, 2, :], fz[:, 5, :], ALU.subtract))
                    link(dve.reciprocal(fz[:, 6, :], fz[:, 3, :]))
                    link(dve.tensor_tensor(fz[:, 5, :], fz[:, 5, :], fz[:, 6, :], ALU.mult))
                    dve.wait_ge(fg_s, 2)
                    link(dve.tensor_tensor(fz[:, 7, :], fz[:, 4, :], fz[:, 5, :], ALU.add))
                    dve.tensor_scalar(fz[:, 8, :], fz[:, 1, :], 0.0, None, ALU.min).then_inc(fg_v, 1)
                    dve.wait_ge(fg_v, 3)
                    dve.tensor_tensor(logf[:, :, :], fz[:, 8, :].rearrange("p (t n) -> p t n", t=TB),
                                      fz[:, 7, :].rearrange("p (t n) -> p t n", t=TB), ALU.subtract).then_inc(fg_v, 1)
                    attention(0)
                    turned(1)
                if k == K_FFN - 1:
                    norm(0, 0, gb_extra, K_FFN)
                    turned(2)
                if K_FFN <= k < K_IN_O:
                    what, c = FFN_ORDER[k - K_FFN]
                    if what == "up":
                        dve.wait_ge(f_silu, c + 1)
                        dve.tensor_tensor(htmp[:, :], htmp[:, :], ps[2 + c % 2][:, :], ALU.mult).then_inc(f_h, 1)
                    if (what == "up" and c == 0) or (what == "down" and c < FC - 1):
                        n = 0 if what == "up" else c + 1
                        dve.wait_ge(f_hi, n + 1)
                        dve.tensor_tensor(htl[:, :], htmp[:, :], hth[:, :].bitcast(F32), ALU.subtract).then_inc(f_lo, 1)
                if k == K_IN_O - 1:
                    norm(1, 2, gb_extra, K_IN_O)
                    turned(3)
                if k == K_OUT_O - 1:
                    attention(1)
                    turned(4)
            norm(2, 6, gb_extra, N_DENSE)
            turned(5)

            lg, eq, cand, oh1, lg2, oh2, g1o, g2o, chosen, pos = (rt[i] for i in (0, 1, 2, 3, 4, 5, 6, 7, 10, 11))
            rev_b = revidx.unsqueeze(1).to_broadcast([P, TB, 8])

            def over(a):
                return a.unsqueeze(2).to_broadcast([P, TB, 8])

            def pick_top(src, m, k1, oh):
                link(dve.tensor_reduce(m, src, AX_X, ALU.max))
                link(dve.tensor_tensor(eq, src, over(m), ALU.is_equal))
                link(dve.tensor_tensor(cand, eq, rev_b, ALU.mult))
                link(dve.tensor_reduce(k1, cand, AX_X, ALU.max))
                link(dve.tensor_tensor(oh, cand, over(k1), ALU.is_equal))

            dve.wait_ge(lg_ps, 1)
            dve.tensor_copy(lgt[:, :], ps[0][0:8, 0:TOK]).then_inc(lgt_rdy, 1)
            dve.wait_ge(lg_ps, 2)
            link(dve.tensor_copy(lg, ps[2][:, 0:16].rearrange("p (t n) -> p t n", t=TB)))
            pick_top(lg, r1[0], r1[4], oh1)
            link(dve.scalar_tensor_tensor(out=lg2, in0=oh1, scalar=-BIG, in1=lg, op0=ALU.mult, op1=ALU.add))
            pick_top(lg2, r1[1], r1[5], oh2)
            link(dve.tensor_tensor(r1[2], r1[1], r1[0], ALU.subtract))
            dve.tensor_tensor(chosen, oh1, oh2, ALU.add).then_inc(sel_rdy, 1)
            link(dve.memset(gates[:, :, 0:1], 0.0))
            dve.memset(posm[:, :, 16:17], -1.0).then_inc(top_v, 1)
            dve.wait_ge(top_s, 1)
            link(dve.tensor_scalar(r1[6], r1[3], 1.0, None, ALU.add))
            link(dve.reciprocal(r1[6], r1[6]))
            link(dve.tensor_tensor(r1[7], r1[3], r1[6], ALU.mult))
            link(dve.tensor_tensor(g1o, oh1, over(r1[6]), ALU.mult))
            link(dve.tensor_tensor(g2o, oh2, over(r1[7]), ALU.mult))
            link(dve.tensor_tensor(gates[:, :, 1:9], g1o, g2o, ALU.add))
            link(dve.tensor_copy(gates[:, :, 9:17], gates[:, :, 1:9]))
            dve.wait_ge(pos_ps, 1)
            link(dve.tensor_tensor(pos, ps[1][:, 0:16].rearrange("p (t n) -> p t n", t=TB), chosen, ALU.mult))
            link(dve.tensor_scalar(posm[:, :, 0:8], pos, -1.0, None, ALU.add))
            link(dve.tensor_scalar(posm[:, :, 8:16], pos, -1.0 - P, None, ALU.add))
            link(dve.tensor_reduce(r1[4][0:1, 0:1], ps[1][0:1, 16:24], AX_X, ALU.max))
            link(dve.tensor_scalar(r1[4][0:1, 0:1], r1[4][0:1, 0:1], float(P), None, ALU.is_gt))
            dve.tensor_copy(flag[:, :], r1[4][0:1, 0:1]).then_inc(flag_rdy, 1)
            link(dve.tensor_scalar(acc[:, :, :], x[:, :, :], ALPHA, None, ALU.mult))

            def one_hot(n, e):
                for tb in range(TB):
                    r = dve.tensor_scalar(ohot[:, tb, :], iota, posm[:, tb, bass.ds(e, 1)], None, ALU.is_equal)
                r.then_inc(oh_rdy, 1)

            def gathered(n):
                dve.wait_ge(ga_hi, n + 1)
                for q in range(2):
                    part = (slice(None), slice(4 * q, 4 * q + 4), slice(0, P))
                    r = dve.tensor_tensor(xtl[part], ps[1 + 2 * q][:, :].rearrange("p (k n) -> p k n", k=4),
                                          xth[part].bitcast(F32), ALU.subtract)
                r.then_inc(ga_lo, 1)

            def scattered(n, tb):
                for nn in range(2):
                    i = 2 * tb + nn
                    o = acc[:, tb, nn * 512:(nn + 1) * 512]
                    dve.wait_ge(sc_ps, n * 4 + (i + 1))
                    dve.scalar_tensor_tensor(out=o, in0=ps[7 if i % 2 == 0 else 4][:, :],
                                             scalar=gates[:, tb, bass.ds(n, 1)], in1=o,
                                             op0=ALU.mult, op1=ALU.add).then_inc(sc_acc, 1)

            def expert(e):
                for j, (what, c, half) in enumerate(EXP_ORDER):
                    if j != PER_EXP - 3:
                        lo(e * PER_EXP + (N_DENSE + j + SPLIT_AHEAD + 1), j, moe_slot(j + SPLIT_AHEAD)[0])
                    if (what, half) == ("up", 1):
                        dve.wait_ge(m_silu, e * EC + (c + 1))
                        dve.tensor_tensor(htmp[:, :], htmp[:, :], ps[2 + c % 2][:, :], ALU.mult).then_inc(m_h, 1)
                    if j == 1:
                        scattered(e, 0)
                    if j == 3:
                        scattered(e, 1)
                    if j == 6:
                        dve.wait_ge(oht_ps, e + 1)
                        one_hot(e + 1, e + 1)
                    if ((what, half) == ("gate", 1) and c) or j == PER_EXP - 3:
                        dve.wait_ge(m_hi, e * EC + (c if j != PER_EXP - 3 else EC))
                        dve.tensor_tensor(htl[:, :], ps[4][:, :], hth[:, :].bitcast(F32), ALU.subtract).then_inc(m_lo, 1)
                    if j == PER_EXP - 3:
                        lo(e * PER_EXP + (N_DENSE + j + SPLIT_AHEAD + 1), j, moe_slot(j + SPLIT_AHEAD)[0])
                        gathered(e + 1)

            one_hot(0, 0)
            gathered(0)
            with dve.Fori(0, N_EXP) as e:
                expert(e)
            dve.wait_ge(flag_rdy, 1)
            more = dve.value_load(flag[0:1, 0:1], min_val=0, max_val=1)
            with dve.If(more > 0):
                with dve.Fori(N_EXP, 2 * N_EXP) as e:
                    expert(e)
                scattered(2 * N_EXP, 0)
                scattered(2 * N_EXP, 1)
                dve.wait_ge(sc_acc, 4 * (2 * N_EXP + 1))
            with dve.Else():
                scattered(N_EXP, 0)
                scattered(N_EXP, 1)
                dve.wait_ge(sc_acc, 4 * (N_EXP + 1))
            norm(3, 8, gb_last)


def constants():
    c = np.zeros((P, C_END), np.float32)
    c[:, C_ID:C_ID + P] = np.eye(P)
    c[:, C_TRI:C_TRI + P] = np.triu(np.ones((P, P)))
    c[:, C_TRI + P:C_TRI + 2 * P] = 1.0
    for b in range(4):
        for r in range(2):
            c[64 * r:64 * r + 64, C_QS + b] = DH ** -0.5 / slope(2 * b + r)
    c[:, C_IOTA:C_IOTA + P] = np.arange(P)
    c[:, C_REV:C_REV + 8] = np.arange(8, 0, -1)
    t, s = np.arange(TOK)[:, None], np.arange(TOK)[None, :]
    near = -np.abs(t - s).astype(np.float32)
    ok = {B_A: (s // CHUNK <= t // CHUNK) & (s // CHUNK >= t // CHUNK - 1), B_B: s <= t, B_C: s // CHUNK <= t // CHUNK}
    b = np.zeros((P, B_END), np.float32)
    for at, valid in ok.items():
        full = np.where(valid, 0.0 if at == B_B else near, -1e30 if at == B_B else -1e34)
        b[:, at:at + P] = full[0:P, 0:P]
        b[:, at + P:at + BIAS_W] = full[P:TOK, :]
    return c, b


def col_units(w):
    n = w.shape[1] // 256
    return w.reshape(KT, P, n, 256).transpose(2, 1, 0, 3).reshape(n, P, UNIT)


def row_units(w):
    n = w.shape[0] // 256
    return w.reshape(n, 2, P, D).transpose(0, 2, 1, 3).reshape(n, P, UNIT)


def dense_stream(e_w_in, e_w_out, e_w_gate, e_w_up, e_w_down, o_w_in, o_w_out):
    w = e_w_in
    k0 = A_Q
    b0 = A_Q + 2 * A_KV
    ka = w[:, k0:k0 + A_KV]
    cols = [w[:, 0:A_Q], ka, ka[:, DH:], ka[:, :DH],
            w[:, b0:b0 + 3 * B_W], w[:, k0 + A_KV:b0], w[:, b0 + 3 * B_W:],
            np.zeros((D, 120), w.dtype)]
    gate, up, down = col_units(e_w_gate), col_units(e_w_up), row_units(e_w_down)
    part = {"gate": gate, "up": up, "down": down}
    ffn = np.stack([part[what][c] for what, c in FFN_ORDER])
    return np.concatenate([col_units(np.concatenate(cols, axis=1)), row_units(e_w_out), ffn,
                           col_units(o_w_in), row_units(o_w_out)])


def expert_stream(w_gate, w_up, w_down):
    out = np.empty((N_MOE + SPLIT_AHEAD, P, UNIT), w_gate.dtype)
    for e in range(N_EXP):
        for j, (what, c, half) in enumerate(EXP_ORDER):
            if what == "down":
                r = c * 512 + half * 256
                u = w_down[e, r:r + 256].reshape(2, P, D)
            else:
                w = w_gate if what == "gate" else w_up
                u = w[e, half * 512:half * 512 + 512, c * 512:(c + 1) * 512].reshape(4, P, 512)
            out[e * PER_EXP + j] = u.transpose(1, 0, 2).reshape(P, UNIT)
    out[N_MOE:] = out[:SPLIT_AHEAD]
    return out


def kernel(**inputs):
    import concourse.bacc as bacc
    from concourse.bass_utils import run_bass_kernel_spmd

    a = {k: np.asarray(v) for k, v in inputs.items()}
    cst, bias_cst = constants()
    arrays = {
        "x_in": a["x"],
        "w_dense": dense_stream(a["e_w_in"][0], a["e_w_out"][0], a["e_w_gate"][0], a["e_w_up"][0],
                                a["e_w_down"][0], a["o_w_in"][0], a["o_w_out"][0]),
        "w_moe": expert_stream(a["o_w_gate"][0], a["o_w_up"][0], a["o_w_down"][0]),
        "cst": cst,
        "bias_cst": bias_cst,
        "vec_rows": np.stack([np.stack([a[f"{l}_ln{n}_g"][0], a[f"{l}_ln{n}_b"][0]])
                              for l in "eo" for n in (1, 2)]),
        "sinks": a["e_sinks"][0],
        "b_forget": a["e_b_forget"][0],
        "lam_rows": np.stack([a["o_lambda_q1"][0], a["o_lambda_k1"][0], a["o_lambda_q2"][0], a["o_lambda_k2"][0]]),
        "subln": a["o_subln_g"][0],
        "w_router": a["o_w_router"][0].reshape(KT, P, N_EXP).transpose(1, 0, 2),
    }
    nc = bacc.Bacc("TRN2", target_bir_lowering=False, num_devices=1, dynamic_dma_scratch_size=4096)
    arrays = {k: np.ascontiguousarray(v) for k, v in arrays.items()}
    args = [nc.dram_tensor(k, v.shape, mybir.dt.from_np(v.dtype), kind="ExternalInput").ap()
            for k, v in arrays.items()]
    out = nc.dram_tensor("out", (1, TOK, D), F32, kind="ExternalOutput").ap()
    trunk(nc, *args, out)
    r = run_bass_kernel_spmd(nc, [arrays], core_ids=[0])
    return r.results[0]["out"]
```

```python
from contextlib import ExitStack

import numpy as np
import concourse.bass as bass
from concourse import mybir

ALU = mybir.AluOpType
ACT = mybir.ActivationFunctionType
AX_X = mybir.AxisListType.X
F32 = mybir.dt.float32
F32R = mybir.dt.float32r
I32 = mybir.dt.int32

P = 128
D = 1024
TOK = 256
TB = TOK // P
KT = D // P
CHUNK = 64
DH = 64
HEADS = 8
A_Q, A_KV, B_W = 512, 128, 512
D_FF = 2816
N_EXP = 8
D_FFE = 3584
ALPHA = 4.0 ** 0.25
EPS = 1e-5
LAMBDA_INIT = 0.8 - 0.6 * float(np.exp(-0.3))
BIG = 3.0e38

UNIT = 2048
FC = D_FF // 256
EC = D_FFE // 512
U_IN_E, U_OUT, U_FFN, U_IN_O = 10, 4, 3 * FC, 12
K_OUT_E = U_IN_E
K_FFN = K_OUT_E + U_OUT
K_IN_O = K_FFN + U_FFN
K_OUT_O = K_IN_O + U_IN_O
N_DENSE = K_OUT_O + U_OUT
PER_EXP = 6 * EC
SPLIT_AHEAD = 3
N_MOE = N_EXP * PER_EXP
N_PASS0 = N_MOE + SPLIT_AHEAD
DENSE_SLOTS = 7
SLOTS = 14
assert N_DENSE % DENSE_SLOTS == 0 and PER_EXP % SLOTS == 0
assert N_DENSE % SPLIT_AHEAD == 0 and PER_EXP % SPLIT_AHEAD == 0

FFN_ORDER = []
for _c in range(FC):
    FFN_ORDER += [("gate", _c), ("up", _c)] + ([("down", _c - 1)] if _c else [])
FFN_ORDER.append(("down", FC - 1))
EXP_ORDER = []
for _c in range(EC):
    EXP_ORDER += [("gate", _c, 0), ("gate", _c, 1), ("up", _c, 0), ("up", _c, 1)]
    if _c:
        EXP_ORDER += [("down", _c - 1, 0), ("down", _c - 1, 1)]
EXP_ORDER += [("down", EC - 1, 0), ("down", EC - 1, 1)]

C_ID, C_TRI, C_QS, C_IOTA, C_REV, C_END = 0, 128, 384, 388, 516, 524
BIAS_W = 384
B_A, B_B, B_C, B_END = 0, 384, 768, 1152

GROUPS = [("A", 0, 0), ("A", 1, 0), ("B", 0, 0), ("B", 1, 0),
          ("C", 0, 0), ("C", 1, 0), ("C", 0, 1), ("C", 1, 1)]
TR_BEFORE = [0]
for _g in GROUPS:
    TR_BEFORE.append(TR_BEFORE[-1] + 2 * (_g[1] + 1))


def hidden_after(what, c):
    if what == "up" and c in (0, FC - 1):
        return c
    if what == "down" and c + 1 < FC - 1:
        return c + 1
    return None


def slope(h):
    return 2.0 ** (-(h + 1))


def dense_slot(k):
    if k < N_DENSE:
        return k % DENSE_SLOTS, k // DENSE_SLOTS + 1
    return moe_slot(k - N_DENSE)


def moe_slot(m):
    s = (m + DENSE_SLOTS) % SLOTS
    return s, (N_DENSE // DENSE_SLOTS if s < DENSE_SLOTS else 0) + m // SLOTS + 1


def trunk(nc, x_in, w_dense, w_moe, cst, bias_cst, vec_rows, sinks, b_forget, lam_rows, subln, w_router, out):
    with ExitStack() as ctx:
        def sb(name, shape, dt=F32):
            return ctx.enter_context(nc.sbuf_tensor(name, shape, dt))

        def sem(name):
            return ctx.enter_context(nc.semaphore(name))

        raw = sb("raw", [P, SLOTS * UNIT])
        whi = sb("whi", [P, SPLIT_AHEAD, UNIT], F32R)
        wlo = sb("wlo", [P, SPLIT_AHEAD, UNIT], F32R)
        x = sb("x", [P, TB, D])
        acc = sb("acc", [P, TB, D])
        xth = sb("xth", [P, KT, TOK], F32R)
        xtl = sb("xtl", [P, KT, TOK], F32R)
        hth = sb("hth", [P, 512], F32R)
        htl = sb("htl", [P, 512], F32R)
        htmp = sb("htmp", [P, 512])
        work = sb("work", [P, 1536])
        con = sb("con", [P, C_END])
        wrh = sb("wrh", [P, KT, N_EXP], F32R)
        wrl = sb("wrl", [P, KT, N_EXP], F32R)
        mx = sb("mx", [P, 2, 8])
        negm = sb("negm", [P, 2, 8])
        sm = sb("sm", [P, 4, 8])
        den = sb("den", [P, 2, 8])
        rec = sb("rec", [P, 2, 8])
        snk = sb("snk", [P, 3, 8])
        logf = sb("logf", [P, TB, 8])
        cumtok = sb("cumtok", [P, TB, 8])
        biasb = sb("biasb", [P, 8, BIAS_W])
        stats = sb("stats", [P, TB, 2, 6])
        mv = sb("mv", [P, TB, 2])
        var = sb("var", [P, 2, 8])
        std = sb("std", [P, 2, 8])
        eps = sb("eps", [P, 1])
        lam = sb("lam", [P, 4])
        posm = sb("posm", [P, TB, 17])
        gates = sb("gates", [P, TB, 17])
        flag = sb("flag", [1, 1], I32)
        lgt = biasb[0:8, 0, 0:TOK]

        extra = raw[:, DENSE_SLOTS * UNIT:]
        qa = extra[:, 0:1024].rearrange("p (b t) -> p b t", t=TOK)
        ka = extra[:, 1024:1536].rearrange("p (b t) -> p b t", t=TOK)
        qb = extra[:, 1536:2560].rearrange("p (b t) -> p b t", t=TOK)
        kb = extra[:, 2560:3584].rearrange("p (b t) -> p b t", t=TOK)
        ve = extra[:, 3584:4864].rearrange("p (t n) -> p t n", t=TB)
        fz = extra[:, 5376:5520].rearrange("p (i n) -> p i n", n=16)
        qo = extra[:, 0:2048].rearrange("p (b t) -> p b t", t=TOK)
        ko = extra[:, 2048:4096].rearrange("p (b t) -> p b t", t=TOK)
        vo = extra[:, 4096:6144].rearrange("p (t n) -> p t n", t=TB)
        S = [extra[:, 6144 + 2048 * i:8192 + 2048 * i].rearrange("p (h n) -> p h n", h=8) for i in range(2)]
        spare = biasb[:, :, :].rearrange("p h n -> p (h n)")
        PT = 3 * [extra[:, 10240 + 2048 * i:12288 + 2048 * i].rearrange("p (k n) -> p k n", k=2) for i in range(2)]
        PT += [spare[:, 0:1024].rearrange("p (k n) -> p k n", k=1),
               spare[:, 1024:3072].rearrange("p (k n) -> p k n", k=2)]

        def hidden(c):
            if c < FC - 1:
                return hth[:, :], htl[:, :]
            return (t[:, 0:2, :].rearrange("p k n -> p (k n)") for t in (xth, xtl))

        gb_extra = extra[:, 12288:14336].rearrange("p (i n) -> p i n", i=2)
        gb_last = raw[:, 0:2048].rearrange("p (i n) -> p i n", i=2)
        bias = work[:, 0:B_END]
        wr_raw = work[:, B_END:B_END + 64].rearrange("p (k n) -> p k n", n=8)
        sub_g = work[:, B_END + 64:B_END + 192]
        lam_in = work[:, B_END + 192:B_END + 384].rearrange("p (i n) -> p i n", n=DH)
        lam_in2 = biasb[:, 0, 0:DH]
        y = work[:, 0:1024]
        ohot = work[:, 1024:1280].rearrange("p (t s) -> p t s", t=TB)
        ohot_t = work[:, 1280:1536]
        rt = [htmp[:, 16 * i:16 * i + 16].rearrange("p (t n) -> p t n", t=TB) for i in range(16)]
        r1 = [htmp[:, 256 + 2 * i:258 + 2 * i] for i in range(8)]
        ident = con[:, C_ID:C_ID + 128]
        tri = con[:, C_TRI:C_TRI + 128]
        ones = con[:, C_TRI + 128:C_TRI + 256]
        iota = con[:, C_IOTA:C_IOTA + 128]
        revidx = con[:, C_REV:C_REV + 8]

        ps = [ctx.enter_context(nc.psum_tensor(f"ps{i}", [P, 512], F32)) for i in range(8)]

        loaded = [sem(f"loaded{i}") for i in range(SLOTS)]
        c_in = sem("consts_in")
        x_here = [sem(f"x_block{tb}_in") for tb in range(TB)]
        small_in = sem("small_rows_in")
        tables_in = sem("bias_and_router_in")
        gb_in = sem("gain_bias_in")
        hi_rdy = sem("hi_ready")
        lo_rdy = sem("lo_ready")
        w_used = sem("w_used")
        src_rdy = sem("src_ready")
        xt_ps = sem("xt_in_psum")
        xth_rdy = sem("xth_ready")
        xtl_rdy = sem("xtl_ready")
        in_ev = sem("proj_evacuated")
        s_ps = sem("scores_in_psum")
        s_max = sem("scores_biased")
        neg_rdy = sem("negmax_ready")
        e_rdy = sem("exp_ready")
        snk_exp = sem("sink_exp_ready")
        tr_ps = sem("probs_t_in_psum")
        pt_ev = sem("probs_t_ready")
        o_ps = sem("attn_out_in_psum")
        o_ev = sem("attn_out_ready")
        fg_v = sem("forget_vector")
        fg_s = sem("forget_scalar")
        cum_ps = sem("cum_in_psum")
        bb_rdy = sem("b_bias_ready")
        lam_v = sem("lambda_sums")
        lam_s = sem("lambda_exps")
        var_rdy = sem("var_ready")
        std_rdy = sem("std_ready")
        sum_rdy = sem("branch_sum_ready")
        f_silu = sem("ffn_silu")
        f_h = sem("ffn_hidden")
        f_hi = sem("ffn_hidden_hi")
        f_lo = sem("ffn_hidden_lo")
        wr_h = sem("router_hi")
        wr_l = sem("router_lo")
        lg_ps = sem("logits_in_psum")
        lgt_rdy = sem("logits_t_ready")
        top_v = sem("top2_diff")
        top_s = sem("top2_exp")
        sel_rdy = sem("choice_ready")
        pos_ps = sem("positions_in_psum")
        flag_rdy = sem("flag_ready")
        m_ps = sem("expert_gate_up_in_psum")
        m_silu = sem("expert_silu")
        m_h = sem("expert_hidden")
        m_tr = sem("expert_hidden_t_in_psum")
        m_hi = sem("expert_hidden_hi")
        m_lo = sem("expert_hidden_lo")
        ga_ps = sem("gathered_in_psum")
        ga_hi = sem("gathered_hi")
        ga_lo = sem("gathered_lo")
        oh_rdy = sem("onehot_ready")
        oht_ps = sem("onehot_t_in_psum")
        oht_rdy = sem("onehot_t_ready")
        ye_rdy = sem("expert_out_ready")
        sc_ps = sem("scattered_in_psum")
        sc_acc = sem("scattered_added")
        dve_self = sem("vector_chain")
        act_self = sem("scalar_chain")
        stored = sem("stored")


        OUT_BANKS = [(0,), (1,), (2,), (3,), (4, 5), (2, 3), (0, 1), (6, 7)]

        def prob_banks(g):
            return (0, 1) if g == 3 else (6, 7)

        def tile_of(t, i):
            if t == 1:
                return i % 2, i // 2, (2, 3, 0, 1)[i]
            return i // 2, i % 2, i

        BETWEEN = [{4: [("scores", 0, 4)], 5: [("turn", 0, 0), ("scores", 1, 0)],
                    6: [("turn", 1, 0), ("values", 0, 0)], 7: [("values", 1, 0)],
                    8: [("scores", 2, 8)], 9: [("turn", 2, 0)]},
                   {6: [("scores", 4, 6)], 7: [("turn", 4, 0), ("scores", 5, 0)], 8: [("turn", 5, 0)],
                    10: [("scores", 6, 10)], 11: [("turn", 6, 0), ("scores", 7, 0), ("values", 4, 12)]}]
        VALUE_ORDER = (0, 1, 2, 3, 4, 6, 5, 7)

        SCORE_ORDER = (0, 2, 1, 3, 4, 6, 5, 7)

        def score_at(h):
            return ps[2 * (h % 2) + h // 4], (h // 2 % 2) * 256

        def unit(t, j):
            return t[:, j % SPLIT_AHEAD, :]

        def as_cols(t, j):
            return unit(t, j).rearrange("p (k n) -> p k n", k=KT)

        def as_rows(t, j):
            return unit(t, j).rearrange("p (k n) -> p k n", k=2)

        def as_half(t, j):
            return unit(t, j).rearrange("p (k n) -> p k n", k=4)

        def yb(tb, n):
            return ps[4 + 2 * tb + n]

        block = ctx.enter_context(nc.Block())

        @block.sync
        def _(sp):
            def load(src, s):
                sp.dma_start(raw[:, s * UNIT:(s + 1) * UNIT], src).then_inc(loaded[s], 16)

            for tb in range(TB):
                sp.dma_start(x[:, tb, :], x_in[0, tb * P:(tb + 1) * P, :]).then_inc(x_here[tb], 16)
            for k in range(N_DENSE):
                if k >= DENSE_SLOTS:
                    sp.wait_ge(lo_rdy, k - DENSE_SLOTS + 1)
                load(w_dense[k], dense_slot(k)[0])
            for m in range(SLOTS):
                if m < DENSE_SLOTS - 1:
                    sp.wait_ge(o_ev, 8)
                elif m == DENSE_SLOTS - 1:
                    sp.wait_ge(src_rdy, 8)
                else:
                    sp.wait_ge(lo_rdy, N_DENSE + m - 2 * DENSE_SLOTS + 1)
                load(w_moe[m], moe_slot(m)[0])
            with sp.Fori(0, N_EXP - 1) as e:
                for j in range(PER_EXP):
                    sp.wait_ge(lo_rdy, e * PER_EXP + (N_DENSE + j + 1))
                    load(w_moe[e * PER_EXP + (SLOTS + j)], moe_slot(SLOTS + j)[0])
            for m in range(SLOTS + (N_EXP - 1) * PER_EXP, N_PASS0):
                sp.wait_ge(lo_rdy, N_DENSE + m - SLOTS + 1)
                load(w_moe[m], moe_slot(m)[0])
            sp.wait_ge(flag_rdy, 1)
            more = sp.value_load(flag[0:1, 0:1], min_val=0, max_val=1)
            with sp.If(more > 0):
                with sp.Fori(N_EXP, 2 * N_EXP) as e:
                    for j in range(PER_EXP):
                        m0 = SPLIT_AHEAD + j
                        sp.wait_ge(lo_rdy, e * PER_EXP + (N_DENSE + m0 - SLOTS + 1))
                        load(w_moe[(e - N_EXP) * PER_EXP + m0], moe_slot(m0)[0])
            with sp.Else():
                sp.nop()
            for tb in range(TB):
                sp.wait_ge(src_rdy, 9 + tb)
                sp.dma_start(out[0, tb * P:(tb + 1) * P, :], x[:, tb, :]).then_inc(stored, 16)
            sp.wait_ge(stored, 32)

        @block.gpsimd
        def _(pool):
            pool.dma_start(snk[:, 0, :], sinks.partition_broadcast(P)).then_inc(small_in, 16)
            pool.dma_start(snk[:, 2, :], b_forget.partition_broadcast(P)).then_inc(small_in, 16)
            pool.dma_start(lam_in, lam_rows[0:3].partition_broadcast(P)).then_inc(small_in, 16)
            pool.dma_start(lam_in2, lam_rows[3].partition_broadcast(P)).then_inc(small_in, 16)
            pool.dma_start(sub_g, subln.partition_broadcast(P)).then_inc(small_in, 16)
            pool.wait_ge(loaded[1], 16)
            pool.dma_start(bias, bias_cst).then_inc(tables_in, 16)
            pool.dma_start(wr_raw, w_router).then_inc(tables_in, 16)
            for n, (s, v) in enumerate(((o_ev, 4), (src_rdy, 2), (o_ev, 8))):
                pool.wait_ge(s, v)
                pool.dma_start(gb_extra, vec_rows[n].partition_broadcast(P)).then_inc(gb_in, 16)
            pool.wait_ge(flag_rdy, 1)
            more = pool.value_load(flag[0:1, 0:1], min_val=0, max_val=1)
            with pool.If(more > 0):
                pool.wait_ge(lo_rdy, N_DENSE + N_MOE + N_PASS0)
            with pool.Else():
                pool.wait_ge(lo_rdy, N_DENSE + N_PASS0)
            pool.dma_start(gb_last, vec_rows[3].partition_broadcast(P)).then_inc(gb_in, 16)

        @block.tensor
        def _(pe):
            mm = pe.matmul

            def three(o, lh, ll, rh, rl, start, stop):
                mm(o, lh, rh, start=start, stop=False)
                mm(o, lh, rl, start=False, stop=False)
                return mm(o, ll, rh, start=False, stop=stop)

            def turn_wait(t, tiles):
                pe.wait_ge(xth_rdy, 4 * t + tiles[-1] + 1)
                pe.wait_ge(xtl_rdy, 4 * t + tiles[-1] + 1)

            def turn(t, tiles=range(4), wait=True):
                src = acc if t in (1, 4) else x
                for j in tiles:
                    tb, half, bank = tile_of(t, j)
                    if t == 0:
                        pe.wait_ge(x_here[tb], 16)
                        pe.wait_ge(c_in, 16)
                    elif t == 1:
                        pe.wait_ge(o_ev, 2 * half + tb + 1)
                    else:
                        pe.wait_ge(src_rdy, 2 * (t - 2) + tb + 1)
                    for i in range(4):
                        kt = 4 * half + i
                        r = pe.transpose(ps[bank][:, i * P:(i + 1) * P], src[:, tb, kt * P:(kt + 1) * P], ident)
                    r.then_inc(xt_ps, 1)
                if wait:
                    turn_wait(t, tiles)

            def to_rows(k, bank):
                h, l = as_cols(whi, k), as_cols(wlo, k)
                for b in range(2):
                    for kt in range(KT):
                        c = slice(b * P, b * P + P)
                        r = three(ps[bank][:, b * TOK:(b + 1) * TOK], h[:, kt, c], l[:, kt, c],
                                  xth[:, kt, :], xtl[:, kt, :], kt == 0, kt == KT - 1)
                return r

            def to_cols(k, bank, n, blocks=range(TB)):
                h, l = as_cols(whi, k), as_cols(wlo, k)
                for tb in blocks:
                    for kt in range(KT):
                        t = slice(tb * P, tb * P + P)
                        r = three(ps[bank][:, tb * 256:tb * 256 + n], xth[:, kt, t], xtl[:, kt, t],
                                  h[:, kt, 0:n], l[:, kt, 0:n], kt == 0, kt == KT - 1)
                return r

            def project(k0, kinds, first=0):
                g = 0 if k0 == 0 else 4
                seen = 0 if k0 == 0 else U_IN_E
                for i, width in list(enumerate(kinds))[first:]:
                    k = k0 + i
                    if i >= 2:
                        pe.wait_ge(in_ev, seen + i - 1)
                    pe.wait_ge(lo_rdy, k + 1)
                    r = to_cols(k, 4 + i % 2, width) if width else to_rows(k, 4 + i % 2)
                    r.then_inc(w_used, 1)
                    if k == 3:
                        cumulate()
                    for what, j, n in BETWEEN[g // 4].get(i, ()):
                        if n:
                            pe.wait_ge(in_ev, seen + n)
                        {"scores": scores, "turn": turn_probs, "values": values}[what](j)

            def scores(g):
                kind, qblk, mp = GROUPS[g]
                nk = P * (qblk + 1)
                q_cols = slice(qblk * P, qblk * P + P)
                if g == 0:
                    pe.wait_ge(bb_rdy, 1)
                if g % 2 or g == 6:
                    pe.wait_ge(s_max, 8 * g)
                elif g:
                    pe.wait_ge(o_ev, g)
                for h in SCORE_ORDER:
                    rows = slice(64 * (h % 2), 64 * (h % 2) + 64)
                    if kind == "A":
                        q, kk = qa[rows, h // 2, q_cols], ka[rows, int(h // 4 != h % 2), 0:nk]
                    elif kind == "B":
                        q, kk = qb[rows, h // 2, q_cols], kb[rows, h // 2, 0:nk]
                    else:
                        b = 4 * mp + h // 2
                        q, kk = qo[rows, b, q_cols], ko[rows, b, 0:nk]
                    bank, c0 = score_at(h)
                    r = mm(bank[:, c0:c0 + nk], q, kk, start=True, stop=True)
                    if h & 2:
                        r.then_inc(s_ps, 1)

            def cumulate():
                pe.wait_ge(fg_v, 4)
                mm(ps[6][:, 0:8], tri, logf[:, 0, :], start=True, stop=True)
                mm(ps[6][:, 8:16], ones, logf[:, 0, :], start=True, stop=False)
                mm(ps[6][:, 8:16], tri, logf[:, 1, :], start=False, stop=True).then_inc(cum_ps, 1)
                for h in range(8):
                    o = ps[h // 2][:, (h % 2) * 256:(h % 2) * 256 + 256]
                    f = [logf[:, b, h:h + 1].to_broadcast([P, P]) for b in range(TB)]
                    mm(o[:, 0:P], f[0], tri, start=True, stop=True)
                    mm(o[:, P:TOK], f[0], ones, start=True, stop=False)
                    r = mm(o[:, P:TOK], f[1], tri, start=False, stop=True)
                    if h % 2:
                        r.then_inc(cum_ps, 1)

            def turn_probs(g):
                n = TR_BEFORE[g]
                for kt in range(GROUPS[g][1] + 1):
                    for half in range(2):
                        if n >= 2:
                            pe.wait_ge(pt_ev, n - 1)
                        pe.wait_ge(e_rdy, 8 * g + 4 * half + 4)
                        for i in range(4):
                            r = pe.transpose(ps[prob_banks(g)[half]][:, i * P:(i + 1) * P],
                                             S[g % 2][:, 4 * half + i, kt * P:(kt + 1) * P], ident)
                        r.then_inc(tr_ps, 1)
                        n += 1

            def values(g):
                kind, qblk, _ = GROUPS[g]
                pe.wait_ge(pt_ev, TR_BEFORE[g + 1])
                if g == 6:
                    pe.wait_ge(s_max, 8 * len(GROUPS))
                for h in range(8):
                    if kind == "C":
                        o = ps[OUT_BANKS[g][h // 4]][:, (h % 4) * P:(h % 4) * P + P]
                    else:
                        o = ps[OUT_BANKS[g][0]][:, h * DH:(h + 1) * DH]
                    for kt in range(qblk + 1):
                        if kind == "A":
                            v = ve[:, kt, (h // 4) * DH:(h // 4) * DH + DH]
                        elif kind == "B":
                            v = ve[:, kt, A_KV + h * DH:A_KV + (h + 1) * DH]
                        else:
                            v = vo[:, kt, h * P:(h + 1) * P]
                        r = mm(o, PT[g][:, kt, h * P:(h + 1) * P], v, start=kt == 0, stop=kt == qblk)
                r.then_inc(o_ps, 1)

            def mix(k, tb, first, last, lh, ll):
                h, l = as_rows(whi, k), as_rows(wlo, k)
                for r2 in range(2):
                    for n in range(2):
                        c = slice(n * 512, n * 512 + 512)
                        r = three(yb(tb, n)[:, :], lh(r2, tb), ll(r2, tb), h[:, r2, c], l[:, r2, c],
                                  first and r2 == 0, last and r2 == 1)
                if tb == 1:
                    r.then_inc(w_used, 1)
                elif last:
                    r.then_inc(sum_rdy, 1)

            def out_rows(k0, u, tb):
                pe.wait_ge(lo_rdy, k0 + u + 1)
                mix(k0 + u, tb, u == 0, u == U_OUT - 1,
                    lambda r2, tb: xth[:, 2 * u + r2, tb * P:(tb + 1) * P],
                    lambda r2, tb: xtl[:, 2 * u + r2, tb * P:(tb + 1) * P])

            def even_end():
                k0 = K_OUT_E
                scores(3)
                pe.wait_ge(s_max, 8 * 4)
                turn(1, (0, 1))
                pe.wait_ge(in_ev, U_IN_E)
                pe.wait_ge(pt_ev, TR_BEFORE[3])
                out_rows(k0, 0, 0)
                out_rows(k0, 0, 1)
                turn_probs(3)
                values(2)
                values(3)
                out_rows(k0, 1, 0)
                out_rows(k0, 1, 1)
                turn(1, (2, 3))
                for tb in range(TB):
                    out_rows(k0, 2, tb)
                    out_rows(k0, 3, tb)

            def odd_end():
                k0 = K_OUT_O
                values(6)
                turn_probs(7)
                values(5)
                values(7)
                for tb in range(TB):
                    turn(4, (2 * tb, 2 * tb + 1))
                    for u in range(3):
                        out_rows(k0, u, tb)
                for tb in range(TB):
                    out_rows(k0, 3, tb)

            def down(c, tb, k):
                h, l = hidden(c)
                mix(k, tb, c == 0, c == FC - 1,
                    lambda r2, tb: h[:, r2 * TOK + tb * P:r2 * TOK + (tb + 1) * P],
                    lambda r2, tb: l[:, r2 * TOK + tb * P:r2 * TOK + (tb + 1) * P])

            turn(0)
            project(0, [256] + 7 * [None] + [256, 256])
            even_end()
            turn(2)
            for i, (what, c) in enumerate(FFN_ORDER):
                k = K_FFN + i
                pe.wait_ge(lo_rdy, k + 1)
                if what == "down":
                    if c < FC - 2:
                        pe.wait_ge(f_lo, c + 1)
                        down(c, 0, k)
                        down(c, 1, k)
                    elif c == FC - 1:
                        pe.wait_ge(f_lo, c)
                        down(c - 1, 0, k - 1)
                        pe.wait_ge(f_lo, c + 1)
                        down(c, 0, k)
                        down(c - 1, 1, k - 1)
                        down(c, 1, k)
                else:
                    if what == "gate" and c >= 2:
                        pe.wait_ge(f_h, c - 1)
                    r = to_rows(k, (0 if what == "gate" else 2) + c % 2)
                    r.then_inc(w_used, 1)
            turn(3, (0, 1))
            pe.wait_ge(lo_rdy, K_IN_O + 1)
            to_cols(K_IN_O, 4, 256, [0])
            turn(3, (2, 3), wait=False)
            pe.wait_ge(lo_rdy, K_IN_O + 2)
            to_cols(K_IN_O + 1, 5, 256, [0])
            turn_wait(3, (2, 3))
            for i in range(2):
                to_cols(K_IN_O + i, 4 + i, 256, [1]).then_inc(w_used, 1)
            project(K_IN_O, 2 * [256] + 8 * [None] + 2 * [256], first=2)
            odd_end()
            turn(5)

            pe.wait_ge(wr_l, 1)
            for kt in range(KT):
                for i, (a, b) in enumerate(((wrh, xth), (wrh, xtl), (wrl, xth), (wrl, xtl))):
                    r = mm(ps[0][0:8, 0:TOK], a[:, kt, :], b[:, kt, :],
                           start=kt == 0 and i == 0, stop=kt == KT - 1 and i == 3)
            r.then_inc(lg_ps, 1)
            pe.wait_ge(lgt_rdy, 1)
            for tb in range(TB):
                r = pe.transpose(ps[2][:, tb * 8:tb * 8 + 8], lgt[:, tb * P:(tb + 1) * P], ident[0:8, 0:8])
            r.then_inc(lg_ps, 1)
            pe.wait_ge(sel_rdy, 1)
            chosen = rt[10]
            mm(ps[1][:, 0:8], tri, chosen[:, 0, :], start=True, stop=True)
            mm(ps[1][:, 8:16], ones, chosen[:, 0, :], start=True, stop=False)
            mm(ps[1][:, 8:16], tri, chosen[:, 1, :], start=False, stop=True)
            mm(ps[1][0:1, 16:24], ones[:, 0:1], chosen[:, 0, :], start=True, stop=False)
            mm(ps[1][0:1, 16:24], ones[:, 0:1], chosen[:, 1, :], start=False, stop=True).then_inc(pos_ps, 1)

            def gather(n):
                pe.wait_ge(oh_rdy, n + 1)
                for kt in range(KT):
                    bank = ps[1 if kt < 4 else 3]
                    for tb in range(TB):
                        r = mm(bank[:, (kt % 4) * P:(kt % 4) * P + P], x[:, tb, kt * P:(kt + 1) * P],
                               ohot[:, tb, :], start=tb == 0, stop=tb == TB - 1)
                r.then_inc(ga_ps, 1)

            def scatter(n, tb):
                if tb == 0:
                    pe.wait_ge(ye_rdy, n + 1)
                    pe.wait_ge(oht_rdy, n + 1)
                for nn in range(2):
                    i = 2 * tb + nn
                    if tb == 1:
                        pe.wait_ge(sc_acc, n * 4 + (i - 1))
                    mm(ps[7 if i % 2 == 0 else 4][:, :], ohot_t[:, tb * P:(tb + 1) * P],
                       y[:, nn * 512:(nn + 1) * 512], start=True, stop=True).then_inc(sc_ps, 1)

            def expert(e):
                def hidden_t(c):
                    pe.wait_ge(m_h, e * EC + (c + 1))
                    if c == 0:
                        pe.wait_ge(sc_acc, e * 4 + 4)
                    for i in range(4):
                        r = pe.transpose(ps[4][:, i * P:(i + 1) * P], htmp[:, i * P:(i + 1) * P], ident)
                    r.then_inc(m_tr, 1)

                for j, (what, c, half) in enumerate(EXP_ORDER):
                    if j == 0:
                        pe.wait_ge(ga_lo, e + 1)
                    pe.wait_ge(lo_rdy, e * PER_EXP + (N_DENSE + j + 1))
                    if what == "down":
                        if half == 0:
                            pe.wait_ge(m_lo, e * EC + (c + 1))
                        h, l = as_rows(whi, j), as_rows(wlo, j)
                        for r2 in range(2):
                            f = slice((2 * half + r2) * P, (2 * half + r2 + 1) * P)
                            for n in range(2):
                                cc = slice(n * 512, n * 512 + 512)
                                r = three(ps[5 + n][:, :], hth[:, f], htl[:, f], h[:, r2, cc], l[:, r2, cc],
                                          c == 0 and half == 0 and r2 == 0,
                                          c == EC - 1 and half == 1 and r2 == 1)
                    else:
                        bank = ps[(0 if what == "gate" else 2) + c % 2]
                        h, l = as_half(whi, j), as_half(wlo, j)
                        for i in range(4):
                            kt = 4 * half + i
                            r = three(bank[:, :], xth[:, kt, 0:P], xtl[:, kt, 0:P], h[:, i, :], l[:, i, :],
                                      kt == 0, kt == KT - 1)
                    r.then_inc(w_used, 1)
                    if j == 1:
                        scatter(e, 0)
                    if j == 3:
                        scatter(e, 1)
                    if j == 5:
                        pe.wait_ge(sc_acc, e * 4 + 3)
                        for tb in range(TB):
                            r = pe.transpose(ps[7][:, tb * P:(tb + 1) * P], ohot[:, tb, :], ident)
                        r.then_inc(oht_ps, 1)
                    if (what, half) == ("gate", 1) and c:
                        hidden_t(c - 1)
                    if j == PER_EXP - 3:
                        hidden_t(EC - 1)
                        gather(e + 1)

            gather(0)
            with pe.Fori(0, N_EXP) as e:
                expert(e)
            pe.wait_ge(flag_rdy, 1)
            more = pe.value_load(flag[0:1, 0:1], min_val=0, max_val=1)
            with pe.If(more > 0):
                with pe.Fori(N_EXP, 2 * N_EXP) as e:
                    expert(e)
                scatter(2 * N_EXP, 0)
                scatter(2 * N_EXP, 1)
            with pe.Else():
                scatter(N_EXP, 0)
                scatter(N_EXP, 1)

        @block.scalar
        def _(act):
            A = act.activation

            def hi(wait, used, j, slot):
                act.wait_ge(loaded[slot], wait)
                if used is not None:
                    act.wait_ge(w_used, used)
                A(unit(whi, j), raw[:, slot * UNIT:(slot + 1) * UNIT], ACT.Copy).then_inc(hi_rdy, 1)

            def split(k):
                s, n = dense_slot(k)
                hi(16 * n, k - SPLIT_AHEAD + 1 if k >= SPLIT_AHEAD else None, k, s)

            def splits(k):
                if k + 2 not in (K_FFN, K_IN_O, N_DENSE):
                    split(k + SPLIT_AHEAD)

            def turned(t, tiles=range(4)):
                for i in tiles:
                    tb, half, bank = tile_of(t, i)
                    act.wait_ge(xt_ps, 4 * t + i + 1)
                    A(xth[:, 4 * half:4 * half + 4, tb * P:(tb + 1) * P],
                      ps[bank][:, :].rearrange("p (k n) -> p k n", k=4), ACT.Copy).then_inc(xth_rdy, 1)

            def root(n, i, v, scale=1.0):
                act.wait_ge(var_rdy, n + 1)
                A(std[:, i, 0:v.shape[1]], v, ACT.Sqrt, bias=eps[:, 0:1], scale=scale).then_inc(std_rdy, 1)

            def norm(k, n, t):
                root(n, 0, mv[:, 0, 1:2])
                turned(t, (0, 1))
                root(n + 1, 1, mv[:, 1, 1:2])
                split(k - 1 + SPLIT_AHEAD)
                turned(t, (2, 3))

            def exps(g):
                act.wait_ge(neg_rdy, g + 1)
                nk = P * (GROUPS[g][1] + 1)
                for h in range(8):
                    A(S[g % 2][:, h, 0:nk], S[g % 2][:, h, 0:nk], ACT.Exp, bias=negm[:, g % 2, h:h + 1],
                      accum_out=sm[:, g % 4, h:h + 1]).then_inc(e_rdy, 1)
                if GROUPS[g][0] == "A":
                    A(den[:, g % 2, :], den[:, g % 2, :], ACT.Exp).then_inc(snk_exp, 1)

            def probs_out(g):
                n = TR_BEFORE[g]
                if 2 <= g < 6:
                    act.wait_ge(o_ps, g - 1)
                for kt in range(GROUPS[g][1] + 1):
                    for half in range(2):
                        act.wait_ge(tr_ps, n + 1)
                        A(PT[g][:, kt, half * 512:(half + 1) * 512], ps[prob_banks(g)[half]][:, :],
                          ACT.Copy).then_inc(pt_ev, 1)
                        n += 1

            def between(layer, i):
                for what, g, _ in BETWEEN[layer].get(i, ()):
                    if what == "scores":
                        exps(g)
                    if what == "turn":
                        probs_out(g)

            def even_end():
                turned(1, (0, 1))
                exps(3)
                split(U_IN_E - 1 + SPLIT_AHEAD)
                probs_out(3)
                turned(1, (2, 3))

            def evac_even(i):
                b = ps[4 + i % 2][:, :].rearrange("p (b t) -> p b t", b=2)
                act.wait_ge(w_used, i + 1)
                if i == 0:
                    A(ve[:, :, 0:A_KV], b[:, :, 0:A_KV], ACT.Copy)
                    r = A(fz[:, 0, :].rearrange("p (t n) -> p t n", t=TB), b[:, :, A_KV:A_KV + 8], ACT.Copy)
                elif i < 3:
                    for s in range(2):
                        blk = 2 * (i - 1) + s
                        r = A(qa[:, blk, :], b[:, s, :], ACT.Copy, scale=con[:, C_QS + blk:C_QS + blk + 1])
                elif i == 3:
                    r = A(ka[:, :, :], b, ACT.Copy)
                elif i < 6:
                    r = A(qb[:, 2 * (i - 4):2 * (i - 4) + 2, :], b, ACT.Copy, scale=DH ** -0.5)
                elif i < 8:
                    r = A(kb[:, 2 * (i - 6):2 * (i - 6) + 2, :], b, ACT.Copy)
                else:
                    r = A(ve[:, :, A_KV + (i - 8) * 256:A_KV + (i - 7) * 256], b, ACT.Copy)
                r.then_inc(in_ev, 1)

            def evac_odd(i):
                b = ps[4 + i % 2][:, :].rearrange("p (b t) -> p b t", b=2)
                act.wait_ge(w_used, K_IN_O + i + 1)
                if i < 2 or i >= 10:
                    n = i % 8
                    r = A(vo[:, :, n * 256:(n + 1) * 256], b, ACT.Copy)
                else:
                    j = i - 2
                    blk = 4 * (j // 4) + 2 * (j % 2)
                    if j % 4 < 2:
                        for s in range(2):
                            r = A(qo[:, blk + s, :], b[:, s, :], ACT.Copy,
                                  scale=con[:, C_QS + (blk + s) % 4:C_QS + (blk + s) % 4 + 1])
                    else:
                        r = A(ko[:, blk:blk + 2, :], b, ACT.Copy)
                r.then_inc(in_ev, 1)

            act.dma_start(con[:, :], cst).then_inc(c_in, 16)
            act.wait_ge(c_in, 16)
            A(lam[:, 0:1], con[:, 0:1], ACT.Copy)
            turned(0)
            split(0)
            split(1)
            split(2)
            for k in range(N_DENSE):
                if k < U_IN_E:
                    evac_even(k)
                if K_IN_O <= k < K_OUT_O:
                    evac_odd(k - K_IN_O)
                if k == K_FFN - 1:
                    norm(k, 0, 2)
                if K_FFN <= k < K_IN_O:
                    what, c = FFN_ORDER[k - K_FFN]
                    if what == "up":
                        act.wait_ge(w_used, k + 1)
                        if c:
                            act.wait_ge(f_lo, c)
                        A(htmp[:, :], ps[c % 2][:, :], ACT.Silu).then_inc(f_silu, 1)
                    n = hidden_after(what, c)
                    if n is not None:
                        act.wait_ge(w_used, k + 1)
                        act.wait_ge(f_h, n + 1)
                        A(list(hidden(n))[0], htmp[:, :], ACT.Copy).then_inc(f_hi, 1)
                if k == K_IN_O - 1:
                    norm(k, 2, 3)
                if k == N_DENSE - 1:
                    norm(k, 6, 5)
                if k != U_IN_E - 1:
                    splits(k)
                if k < U_IN_E:
                    between(0, k)
                if K_IN_O <= k < K_OUT_O:
                    between(1, k - K_IN_O)
                if k == 1:
                    act.wait_ge(lam_v, 1)
                    A(lam[:, 0:2], lam[:, 0:2], ACT.Exp).then_inc(lam_s, 1)
                    act.wait_ge(fg_v, 1)
                    A(fz[:, 2, :], fz[:, 2, :], ACT.Exp, scale=-1.0).then_inc(fg_s, 1)
                    act.wait_ge(fg_v, 2)
                    A(fz[:, 4, :], fz[:, 3, :], ACT.Ln).then_inc(fg_s, 1)
                if k == 3:
                    act.wait_ge(tables_in, 2 * 16)
                    A(wrh[:, :, :], wr_raw, ACT.Copy).then_inc(wr_h, 1)
                if k == U_IN_E - 1:
                    even_end()
                if k == K_OUT_O - 1:
                    probs_out(7)
                    for tb in range(TB):
                        root(4 + tb, tb, var[:, tb, :], 1.0 / P)
                        turned(4, (2 * tb, 2 * tb + 1))
            act.wait_ge(top_v, 1)
            A(r1[3], r1[2], ACT.Exp).then_inc(top_s, 1)
            act.wait_ge(flag_rdy, 1)
            A(y, iota.unsqueeze(1).to_broadcast([P, 8, P]), ACT.Copy, scale=0.0).then_inc(ye_rdy, 1)
            A(ohot_t, con[:, 0:256], ACT.Copy, scale=0.0).then_inc(oht_rdy, 1)

            def gathered(n):
                for q in range(2):
                    act.wait_ge(ga_ps, n + 1)
                    r = A(xth[:, 4 * q:4 * q + 4, 0:P], ps[1 + 2 * q][:, :].rearrange("p (k n) -> p k n", k=4), ACT.Copy)
                r.then_inc(ga_hi, 1)

            def expert(e):
                for j, (what, c, half) in enumerate(EXP_ORDER):
                    s, n = moe_slot(j + SPLIT_AHEAD)
                    if j != PER_EXP - 3:
                        hi(e * (16 * (PER_EXP // SLOTS)) + 16 * n, e * PER_EXP + (N_DENSE + j + 1), j, s)
                    if j == 6:
                        act.wait_ge(oht_ps, e + 1)
                        A(ohot_t, ps[7][:, 0:256], ACT.Copy).then_inc(oht_rdy, 1)
                    if (what, half) == ("up", 1):
                        act.wait_ge(w_used, e * PER_EXP + (N_DENSE + j + 1))
                        A(htmp[:, :], ps[c % 2][:, :], ACT.Silu).then_inc(m_silu, 1)
                    if ((what, half) == ("gate", 1) and c) or j == PER_EXP - 3:
                        act.wait_ge(m_tr, e * EC + (c if j != PER_EXP - 3 else EC))
                        A(hth[:, :], ps[4][:, :], ACT.Copy).then_inc(m_hi, 1)
                    if j == PER_EXP - 3:
                        hi(e * (16 * (PER_EXP // SLOTS)) + 16 * n, e * PER_EXP + (N_DENSE + j + 1), j, s)
                        gathered(e + 1)
                    if j == PER_EXP - 1:
                        act.wait_ge(w_used, e * PER_EXP + (N_DENSE + j + 1))
                        for nn in range(2):
                            r = A(y[:, nn * 512:(nn + 1) * 512], ps[5 + nn][:, :], ACT.Copy)
                        r.then_inc(ye_rdy, 1)

            gathered(0)
            A(r1[3], r1[3], ACT.Silu)
            with act.Fori(0, N_EXP) as e:
                expert(e)
            more = act.value_load(flag[0:1, 0:1], min_val=0, max_val=1)
            with act.If(more > 0):
                with act.Fori(N_EXP, 2 * N_EXP) as e:
                    expert(e)
            with act.Else():
                act.nop()
            for tb in range(TB):
                root(8 + tb, tb, mv[:, tb, 1:2])

        @block.vector
        def _(dve):
            chained = [0]

            def link(r):
                chained[0] += 1
                r.then_inc(dve_self, 1)
                dve.wait_ge(dve_self, chained[0])

            def lo(count, j, slot):
                dve.wait_ge(hi_rdy, count)
                dve.tensor_tensor(unit(wlo, j), raw[:, slot * UNIT:(slot + 1) * UNIT],
                                  unit(whi, j).bitcast(F32), ALU.subtract).then_inc(lo_rdy, 1)

            def split(k):
                lo(k + 1, k, dense_slot(k)[0])

            def splits(k):
                if k + 2 not in (K_FFN, K_IN_O, N_DENSE):
                    split(k + SPLIT_AHEAD)

            def turned(t, tiles=range(4)):
                for i in tiles:
                    tb, half, bank = tile_of(t, i)
                    part = (slice(None), slice(4 * half, 4 * half + 4), slice(tb * P, (tb + 1) * P))
                    dve.wait_ge(xth_rdy, 4 * t + i + 1)
                    dve.tensor_tensor(xtl[part], ps[bank][:, :].rearrange("p (k n) -> p k n", k=4),
                                      xth[part].bitcast(F32), ALU.subtract).then_inc(xtl_rdy, 1)

            def score_max(g):
                kind, qblk, _ = GROUPS[g]
                nk = P * (qblk + 1)
                b0 = P * qblk
                if g % 4 >= 2:
                    dve.wait_ge(tr_ps, TR_BEFORE[g - 1])
                for i, h in enumerate(SCORE_ORDER):
                    dve.wait_ge(s_ps, 4 * g + i // 2 + 1)
                    bank, c0 = score_at(h)
                    dve.tensor_tensor_reduce(
                        out=S[g % 2][:, h, 0:nk], in0=bank[:, c0:c0 + nk],
                        in1=biasb[:, h, b0:b0 + nk] if kind == "B" else
                        bias[:, (B_A if kind == "A" else B_C) + b0:(B_A if kind == "A" else B_C) + b0 + nk],
                        scale=1.0 if kind == "B" else slope(h), scalar=-BIG,
                        op0=ALU.subtract if kind == "B" else ALU.add, op1=ALU.max,
                        accum_out=mx[:, g % 2, h:h + 1]).then_inc(s_max, 1)
                dve.wait_ge(s_max, 8 * g + 8)
                if kind == "A":
                    link(dve.scalar_tensor_tensor(out=negm[:, g % 2, :], in0=mx[:, g % 2, :], scalar=-1.0,
                                                  in1=snk[:, 1, :], op0=ALU.mult, op1=ALU.min))
                    dve.tensor_tensor(den[:, g % 2, :], snk[:, 0, :], negm[:, g % 2, :], ALU.add).then_inc(neg_rdy, 1)
                else:
                    dve.tensor_scalar(negm[:, g % 2, :], mx[:, g % 2, :], -1.0, None, ALU.mult).then_inc(neg_rdy, 1)

            def head_out(g):
                kind, qblk, mp = GROUPS[g]
                r8 = rec[:, g % 2, :]
                dve.wait_ge(e_rdy, 8 * g + 8)
                if kind == "A":
                    dve.wait_ge(snk_exp, g + 1)
                    link(dve.tensor_tensor(sm[:, g % 4, :], sm[:, g % 4, :], den[:, g % 2, :], ALU.add))
                link(dve.reciprocal(r8, sm[:, g % 4, :]))
                if kind == "C" and mp == 1:
                    link(dve.tensor_scalar(r8, r8, lam[:, 3:4], None, ALU.mult))
                dve.wait_ge(o_ps, VALUE_ORDER.index(g) + 1)
                if kind != "C":
                    o = acc[:, qblk, (0 if kind == "A" else 512):(512 if kind == "A" else 1024)]
                    r = dve.tensor_tensor(o.rearrange("p (h n) -> p h n", h=8),
                                          ps[OUT_BANKS[g][0]][:, :].rearrange("p (h n) -> p h n", h=8),
                                          r8.unsqueeze(2).to_broadcast([P, 8, DH]), ALU.mult)
                    r.then_inc(o_ev, 1)
                    return
                for half in range(2):
                    p4 = ps[OUT_BANKS[g][half]]
                    if mp == 0:
                        o = acc[:, qblk, half * 512:(half + 1) * 512].rearrange("p (h n) -> p h n", h=4)
                        rb = r8[:, 4 * half:4 * half + 4].unsqueeze(2).to_broadcast([P, 4, P])
                        r = dve.tensor_tensor(o, p4[:, :].rearrange("p (h n) -> p h n", h=4), rb, ALU.mult)
                    else:
                        for h in range(4 * half, 4 * half + 4):
                            o = acc[:, qblk, h * P:(h + 1) * P]
                            r = dve.scalar_tensor_tensor(out=o, in0=p4[:, (h % 4) * P:(h % 4) * P + P],
                                                         scalar=r8[:, h:h + 1], in1=o, op0=ALU.mult, op1=ALU.add)
                r.then_inc(o_ev, 1)
                dve.wait_ge(o_ev, VALUE_ORDER.index(g) + 1)

            def head_norm(qblk):
                for h in range(8):
                    o = acc[:, qblk, h * P:(h + 1) * P]
                    r = dve.tensor_tensor_reduce(out=spare[:, (8 * qblk + h) * P:(8 * qblk + h + 1) * P], in0=o, in1=o, scale=1.0,
                                                 scalar=0.0, op0=ALU.mult, op1=ALU.add,
                                                 accum_out=var[:, qblk, h:h + 1])
                r.then_inc(var_rdy, 1)

            def head_norm_end(qblk):
                dve.wait_ge(std_rdy, 5 + qblk)
                link(dve.reciprocal(std[:, qblk, :], std[:, qblk, :]))
                for h in range(8):
                    o = acc[:, qblk, h * P:(h + 1) * P]
                    r = dve.scalar_tensor_tensor(out=o, in0=o, scalar=std[:, qblk, h:h + 1], in1=sub_g,
                                                 op0=ALU.mult, op1=ALU.mult)
                r.then_inc(src_rdy, 1)

            def between(layer, i):
                for what, g, _ in BETWEEN[layer].get(i, ()):
                    if what == "scores":
                        score_max(g)
                    if what == "values":
                        head_out(g)

            def even_end():
                score_max(3)
                turned(1, (0, 1))
                head_out(2)
                split(U_IN_E - 1 + SPLIT_AHEAD)
                head_out(3)
                turned(1, (2, 3))

            def odd_end():
                head_out(6)
                head_norm(0)
                head_norm_end(0)
                head_out(5)
                turned(4, (0, 1))
                split(K_OUT_O - 1 + SPLIT_AHEAD)
                head_out(7)
                head_norm(1)
                head_norm_end(1)
                turned(4, (2, 3))

            def norm_sum(n, tb, roots, units=None):
                if units is not None:
                    if tb == 0:
                        dve.wait_ge(sum_rdy, n + 1)
                    else:
                        dve.wait_ge(w_used, units)
                for h in range(2):
                    c = slice(h * 512, h * 512 + 512)
                    if units is not None:
                        link(dve.scalar_tensor_tensor(out=acc[:, tb, c], in0=x[:, tb, c], scalar=ALPHA,
                                                      in1=yb(tb, h)[:, :], op0=ALU.mult, op1=ALU.add))
                    link(dve.bn_stats(stats[:, tb, h, :], acc[:, tb, c]))
                dve.bn_aggr(mv[:, tb, :], stats[:, tb, :, :]).then_inc(var_rdy, 1)
                dve.wait_ge(var_rdy, roots + tb + 1)

            def norm_end(n, tb, roots, gb):
                if tb == 0:
                    dve.wait_ge(gb_in, 16 * (n + 1))
                link(dve.scalar_tensor_tensor(out=x[:, tb, :], in0=acc[:, tb, :], scalar=mv[:, tb, 0:1],
                                              in1=gb[:, 0, :], op0=ALU.subtract, op1=ALU.mult))
                dve.wait_ge(std_rdy, roots + tb + 1)
                link(dve.reciprocal(std[:, tb, 0:1], std[:, tb, 0:1]))
                dve.scalar_tensor_tensor(out=x[:, tb, :], in0=x[:, tb, :], scalar=std[:, tb, 0:1],
                                         in1=gb[:, 1, :], op0=ALU.mult, op1=ALU.add).then_inc(src_rdy, 1)

            def norm(k, n, roots, t):
                norm_sum(n, 0, roots, k + 1)
                norm_end(n, 0, roots, gb_extra)
                norm_sum(n, 1, roots, k + 1)
                turned(t, (0, 1))
                norm_end(n, 1, roots, gb_extra)
                split(k - 1 + SPLIT_AHEAD)
                turned(t, (2, 3))

            link(dve.memset(eps[:, :], EPS))
            dve.wait_ge(c_in, 16)
            turned(0)
            split(0)
            split(1)
            split(2)
            for k in range(N_DENSE):
                if k < U_IN_E:
                    between(0, k)
                if K_IN_O <= k < K_OUT_O:
                    between(1, k - K_IN_O)
                if k == K_FFN - 1:
                    norm(k, 0, 0, 2)
                if K_FFN <= k < K_IN_O:
                    what, c = FFN_ORDER[k - K_FFN]
                    if what == "up":
                        dve.wait_ge(f_silu, c + 1)
                        dve.tensor_tensor(htmp[:, :], htmp[:, :], ps[2 + c % 2][:, :], ALU.mult).then_inc(f_h, 1)
                    n = hidden_after(what, c)
                    if n is not None:
                        h, l = hidden(n)
                        dve.wait_ge(f_hi, n + 1)
                        dve.tensor_tensor(l, htmp[:, :], h.bitcast(F32), ALU.subtract).then_inc(f_lo, 1)
                if k == K_IN_O - 1:
                    norm(k, 1, 2, 3)
                if k == N_DENSE - 1:
                    norm(k, 2, 6, 5)
                if k not in (U_IN_E - 1, K_OUT_O - 1):
                    splits(k)
                if k == 1:
                    dve.wait_ge(small_in, 5 * 16)
                    link(dve.tensor_scalar(snk[:, 1, :], snk[:, 0, :], -1.0, None, ALU.mult))
                    link(dve.tensor_tensor_reduce(out=htmp[:, 0:DH], in0=lam_in[:, 0, :], in1=lam_in[:, 1, :], scale=1.0,
                                                  scalar=0.0, op0=ALU.mult, op1=ALU.add, accum_out=lam[:, 0:1]))
                    dve.tensor_tensor_reduce(out=htmp[:, DH:2 * DH], in0=lam_in[:, 2, :], in1=lam_in2, scale=1.0,
                                             scalar=0.0, op0=ALU.mult, op1=ALU.add, accum_out=lam[:, 1:2]).then_inc(lam_v, 1)
                    dve.wait_ge(lam_s, 1)
                    link(dve.tensor_tensor(lam[:, 2:3], lam[:, 1:2], lam[:, 0:1], ALU.subtract))
                    link(dve.tensor_scalar(lam[:, 3:4], lam[:, 2:3], -LAMBDA_INIT, None, ALU.add))
                    link(dve.tensor_scalar(sub_g, sub_g, 1.0 - LAMBDA_INIT, None, ALU.mult))
                    dve.wait_ge(in_ev, 1)
                    for tb in range(TB):
                        link(dve.tensor_tensor(fz[:, 1, 8 * tb:8 * tb + 8], fz[:, 0, 8 * tb:8 * tb + 8],
                                               snk[:, 2, :], ALU.add))
                    dve.scalar_tensor_tensor(out=fz[:, 2, :], in0=fz[:, 1, :], scalar=-1.0, in1=fz[:, 1, :],
                                             op0=ALU.mult, op1=ALU.max).then_inc(fg_v, 1)
                    dve.wait_ge(fg_s, 1)
                    dve.tensor_scalar(fz[:, 3, :], fz[:, 2, :], 1.0, None, ALU.add).then_inc(fg_v, 1)
                    dve.wait_ge(fg_v, 2)
                    link(dve.tensor_scalar(fz[:, 5, :], fz[:, 3, :], -1.0, None, ALU.add))
                    link(dve.tensor_tensor(fz[:, 5, :], fz[:, 2, :], fz[:, 5, :], ALU.subtract))
                    link(dve.reciprocal(fz[:, 6, :], fz[:, 3, :]))
                    link(dve.tensor_tensor(fz[:, 5, :], fz[:, 5, :], fz[:, 6, :], ALU.mult))
                    dve.wait_ge(fg_s, 2)
                    link(dve.tensor_tensor(fz[:, 7, :], fz[:, 4, :], fz[:, 5, :], ALU.add))
                    dve.tensor_scalar(fz[:, 8, :], fz[:, 1, :], 0.0, None, ALU.min).then_inc(fg_v, 1)
                    dve.wait_ge(fg_v, 3)
                    dve.tensor_tensor(logf[:, :, :], fz[:, 8, :].rearrange("p (t n) -> p t n", t=TB),
                                      fz[:, 7, :].rearrange("p (t n) -> p t n", t=TB), ALU.subtract).then_inc(fg_v, 1)
                if k == 3:
                    dve.wait_ge(tables_in, 2 * 16)
                    dve.wait_ge(cum_ps, 1)
                    link(dve.tensor_copy(cumtok[:, :, :], ps[6][:, 0:16].rearrange("p (t n) -> p t n", t=TB)))
                    for h in range(8):
                        dve.wait_ge(cum_ps, 2 + h // 2)
                        for b in range(TB):
                            c = slice(P * b, P * b + P * (b + 1))
                            r = dve.scalar_tensor_tensor(
                                out=biasb[:, h, c], in0=ps[h // 2][:, (h % 2) * 256:(h % 2) * 256 + P * (b + 1)],
                                scalar=cumtok[:, b, h:h + 1], in1=bias[:, B_B + P * b:B_B + P * b + P * (b + 1)],
                                op0=ALU.subtract, op1=ALU.subtract)
                    r.then_inc(bb_rdy, 1)
                    dve.wait_ge(bb_rdy, 1)
                    dve.wait_ge(wr_h, 1)
                    dve.tensor_tensor(wrl[:, :, :], wr_raw, wrh[:, :, :].bitcast(F32), ALU.subtract).then_inc(wr_l, 1)
                if k == U_IN_E - 1:
                    even_end()
                if k == K_OUT_O - 1:
                    odd_end()

            lg, eq, cand, oh1, lg2, oh2, g1o, g2o, chosen, pos = (rt[i] for i in (0, 1, 2, 3, 4, 5, 6, 7, 10, 11))
            rev_b = revidx.unsqueeze(1).to_broadcast([P, TB, 8])

            def over(a):
                return a.unsqueeze(2).to_broadcast([P, TB, 8])

            def pick_top(src, m, k1, oh):
                link(dve.tensor_reduce(m, src, AX_X, ALU.max))
                link(dve.tensor_tensor(eq, src, over(m), ALU.is_equal))
                link(dve.tensor_tensor(cand, eq, rev_b, ALU.mult))
                link(dve.tensor_reduce(k1, cand, AX_X, ALU.max))
                link(dve.tensor_tensor(oh, cand, over(k1), ALU.is_equal))

            dve.wait_ge(lg_ps, 1)
            dve.tensor_copy(lgt[:, :], ps[0][0:8, 0:TOK]).then_inc(lgt_rdy, 1)
            dve.wait_ge(lg_ps, 2)
            link(dve.tensor_copy(lg, ps[2][:, 0:16].rearrange("p (t n) -> p t n", t=TB)))
            pick_top(lg, r1[0], r1[4], oh1)
            link(dve.scalar_tensor_tensor(out=lg2, in0=oh1, scalar=-BIG, in1=lg, op0=ALU.mult, op1=ALU.add))
            pick_top(lg2, r1[1], r1[5], oh2)
            link(dve.tensor_tensor(r1[2], r1[1], r1[0], ALU.subtract))
            dve.tensor_tensor(chosen, oh1, oh2, ALU.add).then_inc(sel_rdy, 1)
            link(dve.memset(gates[:, :, 0:1], 0.0))
            dve.memset(posm[:, :, 16:17], -1.0).then_inc(top_v, 1)
            dve.wait_ge(top_s, 1)
            link(dve.tensor_scalar(r1[6], r1[3], 1.0, None, ALU.add))
            link(dve.reciprocal(r1[6], r1[6]))
            link(dve.tensor_tensor(r1[7], r1[3], r1[6], ALU.mult))
            link(dve.tensor_tensor(g1o, oh1, over(r1[6]), ALU.mult))
            link(dve.tensor_tensor(g2o, oh2, over(r1[7]), ALU.mult))
            link(dve.tensor_tensor(gates[:, :, 1:9], g1o, g2o, ALU.add))
            link(dve.tensor_copy(gates[:, :, 9:17], gates[:, :, 1:9]))
            dve.wait_ge(pos_ps, 1)
            link(dve.tensor_tensor(pos, ps[1][:, 0:16].rearrange("p (t n) -> p t n", t=TB), chosen, ALU.mult))
            link(dve.tensor_scalar(posm[:, :, 0:8], pos, -1.0, None, ALU.add))
            link(dve.tensor_scalar(posm[:, :, 8:16], pos, -1.0 - P, None, ALU.add))
            link(dve.tensor_reduce(r1[4][0:1, 0:1], ps[1][0:1, 16:24], AX_X, ALU.max))
            link(dve.tensor_scalar(r1[4][0:1, 0:1], r1[4][0:1, 0:1], float(P), None, ALU.is_gt))
            dve.tensor_copy(flag[:, :], r1[4][0:1, 0:1]).then_inc(flag_rdy, 1)
            link(dve.tensor_scalar(acc[:, :, :], x[:, :, :], ALPHA, None, ALU.mult))

            def one_hot(n, e):
                for tb in range(TB):
                    r = dve.tensor_scalar(ohot[:, tb, :], iota, posm[:, tb, bass.ds(e, 1)], None, ALU.is_equal)
                r.then_inc(oh_rdy, 1)

            def gathered(n):
                dve.wait_ge(ga_hi, n + 1)
                for q in range(2):
                    part = (slice(None), slice(4 * q, 4 * q + 4), slice(0, P))
                    r = dve.tensor_tensor(xtl[part], ps[1 + 2 * q][:, :].rearrange("p (k n) -> p k n", k=4),
                                          xth[part].bitcast(F32), ALU.subtract)
                r.then_inc(ga_lo, 1)

            def scattered(n, tb):
                for nn in range(2):
                    i = 2 * tb + nn
                    o = acc[:, tb, nn * 512:(nn + 1) * 512]
                    dve.wait_ge(sc_ps, n * 4 + (i + 1))
                    dve.scalar_tensor_tensor(out=o, in0=ps[7 if i % 2 == 0 else 4][:, :],
                                             scalar=gates[:, tb, bass.ds(n, 1)], in1=o,
                                             op0=ALU.mult, op1=ALU.add).then_inc(sc_acc, 1)

            def expert(e):
                for j, (what, c, half) in enumerate(EXP_ORDER):
                    if j != PER_EXP - 3:
                        lo(e * PER_EXP + (N_DENSE + j + SPLIT_AHEAD + 1), j, moe_slot(j + SPLIT_AHEAD)[0])
                    if (what, half) == ("up", 1):
                        dve.wait_ge(m_silu, e * EC + (c + 1))
                        dve.tensor_tensor(htmp[:, :], htmp[:, :], ps[2 + c % 2][:, :], ALU.mult).then_inc(m_h, 1)
                    if j == 1:
                        scattered(e, 0)
                    if j == 3:
                        scattered(e, 1)
                    if j == 6:
                        dve.wait_ge(oht_ps, e + 1)
                        one_hot(e + 1, e + 1)
                    if ((what, half) == ("gate", 1) and c) or j == PER_EXP - 3:
                        dve.wait_ge(m_hi, e * EC + (c if j != PER_EXP - 3 else EC))
                        dve.tensor_tensor(htl[:, :], ps[4][:, :], hth[:, :].bitcast(F32), ALU.subtract).then_inc(m_lo, 1)
                    if j == PER_EXP - 3:
                        lo(e * PER_EXP + (N_DENSE + j + SPLIT_AHEAD + 1), j, moe_slot(j + SPLIT_AHEAD)[0])
                        gathered(e + 1)

            one_hot(0, 0)
            gathered(0)
            with dve.Fori(0, N_EXP) as e:
                expert(e)
            dve.wait_ge(flag_rdy, 1)
            more = dve.value_load(flag[0:1, 0:1], min_val=0, max_val=1)
            with dve.If(more > 0):
                with dve.Fori(N_EXP, 2 * N_EXP) as e:
                    expert(e)
                scattered(2 * N_EXP, 0)
                scattered(2 * N_EXP, 1)
                dve.wait_ge(sc_acc, 4 * (2 * N_EXP + 1))
            with dve.Else():
                scattered(N_EXP, 0)
                scattered(N_EXP, 1)
                dve.wait_ge(sc_acc, 4 * (N_EXP + 1))
            for tb in range(TB):
                norm_sum(3, tb, 8)
                norm_end(3, tb, 8, gb_last)


def constants():
    c = np.zeros((P, C_END), np.float32)
    c[:, C_ID:C_ID + P] = np.eye(P)
    c[:, C_TRI:C_TRI + P] = np.triu(np.ones((P, P)))
    c[:, C_TRI + P:C_TRI + 2 * P] = 1.0
    for b in range(4):
        for r in range(2):
            c[64 * r:64 * r + 64, C_QS + b] = DH ** -0.5 / slope(2 * b + r)
    c[:, C_IOTA:C_IOTA + P] = np.arange(P)
    c[:, C_REV:C_REV + 8] = np.arange(8, 0, -1)
    t, s = np.arange(TOK)[:, None], np.arange(TOK)[None, :]
    near = -np.abs(t - s).astype(np.float32)
    ok = {B_A: (s // CHUNK <= t // CHUNK) & (s // CHUNK >= t // CHUNK - 1), B_B: s <= t, B_C: s // CHUNK <= t // CHUNK}
    b = np.zeros((P, B_END), np.float32)
    for at, valid in ok.items():
        full = np.where(valid, 0.0 if at == B_B else near, -1e30 if at == B_B else -1e34)
        b[:, at:at + P] = full[0:P, 0:P]
        b[:, at + P:at + BIAS_W] = full[P:TOK, :]
    return c, b


def col_units(w):
    n = w.shape[1] // 256
    return w.reshape(KT, P, n, 256).transpose(2, 1, 0, 3).reshape(n, P, UNIT)


def row_units(w):
    n = w.shape[0] // 256
    return w.reshape(n, 2, P, D).transpose(0, 2, 1, 3).reshape(n, P, UNIT)


def dense_stream(e_w_in, e_w_out, e_w_gate, e_w_up, e_w_down, o_w_in, o_w_out):
    w = e_w_in
    k0 = A_Q
    b0 = A_Q + 2 * A_KV
    ka = w[:, k0:k0 + A_KV]
    cols = [w[:, k0 + A_KV:b0], w[:, b0 + 3 * B_W:], np.zeros((D, 120), w.dtype),
            w[:, 0:A_Q], ka, ka[:, DH:], ka[:, :DH],
            w[:, b0:b0 + 3 * B_W]]
    gate, up, down = col_units(e_w_gate), col_units(e_w_up), row_units(e_w_down)
    part = {"gate": gate, "up": up, "down": down}
    ffn = np.stack([part[what][c] for what, c in FFN_ORDER])
    return np.concatenate([col_units(np.concatenate(cols, axis=1)), row_units(e_w_out), ffn,
                           col_units(o_w_in)[[8, 9, 0, 1, 4, 5, 2, 3, 6, 7, 10, 11]], row_units(o_w_out)])


def expert_stream(w_gate, w_up, w_down):
    out = np.empty((N_MOE + SPLIT_AHEAD, P, UNIT), w_gate.dtype)
    for e in range(N_EXP):
        for j, (what, c, half) in enumerate(EXP_ORDER):
            if what == "down":
                r = c * 512 + half * 256
                u = w_down[e, r:r + 256].reshape(2, P, D)
            else:
                w = w_gate if what == "gate" else w_up
                u = w[e, half * 512:half * 512 + 512, c * 512:(c + 1) * 512].reshape(4, P, 512)
            out[e * PER_EXP + j] = u.transpose(1, 0, 2).reshape(P, UNIT)
    out[N_MOE:] = out[:SPLIT_AHEAD]
    return out


def kernel(**inputs):
    import concourse.bacc as bacc
    from concourse.bass_utils import run_bass_kernel_spmd

    a = {k: np.asarray(v) for k, v in inputs.items()}
    cst, bias_cst = constants()
    arrays = {
        "x_in": a["x"],
        "w_dense": dense_stream(a["e_w_in"][0], a["e_w_out"][0], a["e_w_gate"][0], a["e_w_up"][0],
                                a["e_w_down"][0], a["o_w_in"][0], a["o_w_out"][0]),
        "w_moe": expert_stream(a["o_w_gate"][0], a["o_w_up"][0], a["o_w_down"][0]),
        "cst": cst,
        "bias_cst": bias_cst,
        "vec_rows": np.stack([np.stack([a[f"{l}_ln{n}_g"][0], a[f"{l}_ln{n}_b"][0]])
                              for l in "eo" for n in (1, 2)]),
        "sinks": a["e_sinks"][0],
        "b_forget": a["e_b_forget"][0],
        "lam_rows": np.stack([a["o_lambda_q1"][0], a["o_lambda_k1"][0], a["o_lambda_q2"][0], a["o_lambda_k2"][0]]),
        "subln": a["o_subln_g"][0],
        "w_router": a["o_w_router"][0].reshape(KT, P, N_EXP).transpose(1, 0, 2),
    }
    nc = bacc.Bacc("TRN2", target_bir_lowering=False, num_devices=1, dynamic_dma_scratch_size=4096)
    arrays = {k: np.ascontiguousarray(v) for k, v in arrays.items()}
    args = [nc.dram_tensor(k, v.shape, mybir.dt.from_np(v.dtype), kind="ExternalInput").ap()
            for k, v in arrays.items()]
    out = nc.dram_tensor("out", (1, TOK, D), F32, kind="ExternalOutput").ap()
    trunk(nc, *args, out)
    r = run_bass_kernel_spmd(nc, [arrays], core_ids=[0])
    return r.results[0]["out"]
```

```python
from contextlib import ExitStack

import numpy as np
import concourse.bass as bass
from concourse import mybir

ALU = mybir.AluOpType
ACT = mybir.ActivationFunctionType
AX_X = mybir.AxisListType.X
F32 = mybir.dt.float32
F32R = mybir.dt.float32r
I32 = mybir.dt.int32

P = 128
D = 1024
TOK = 256
TB = TOK // P
KT = D // P
CHUNK = 64
DH = 64
HEADS = 8
A_Q, A_KV, B_W = 512, 128, 512
D_FF = 2816
N_EXP = 8
D_FFE = 3584
ALPHA = 4.0 ** 0.25
EPS = 1e-5
LAMBDA_INIT = 0.8 - 0.6 * float(np.exp(-0.3))
BIG = 3.0e38

UNIT = 2048
FC = D_FF // 256
EC = D_FFE // 512
U_IN_E, U_OUT, U_FFN, U_IN_O = 10, 4, 3 * FC, 12
K_OUT_E = U_IN_E
K_FFN = K_OUT_E + U_OUT
K_IN_O = K_FFN + U_FFN
K_OUT_O = K_IN_O + U_IN_O
N_DENSE = K_OUT_O + U_OUT
PER_EXP = 6 * EC
SPLIT_AHEAD = 3
N_MOE = N_EXP * PER_EXP
N_PASS0 = N_MOE + SPLIT_AHEAD
DENSE_SLOTS = 7
SLOTS = 14
assert N_DENSE % DENSE_SLOTS == 0 and PER_EXP % SLOTS == 0
assert N_DENSE % SPLIT_AHEAD == 0 and PER_EXP % SPLIT_AHEAD == 0

FFN_ORDER = []
for _c in range(FC):
    FFN_ORDER += [("gate", _c), ("up", _c)] + ([("down", _c - 1)] if _c else [])
FFN_ORDER.append(("down", FC - 1))
EXP_ORDER = []
for _c in range(EC):
    EXP_ORDER += [("gate", _c, 0), ("gate", _c, 1), ("up", _c, 0), ("up", _c, 1)]
    if _c:
        EXP_ORDER += [("down", _c - 1, 0), ("down", _c - 1, 1)]
EXP_ORDER += [("down", EC - 1, 0), ("down", EC - 1, 1)]

C_ID, C_TRI, C_QS, C_IOTA, C_REV, C_END = 0, 128, 384, 388, 516, 524
BIAS_W = 384
B_A, B_B, B_C, B_END = 0, 384, 768, 1152

GROUPS = [("A", 0, 0), ("A", 1, 0), ("B", 0, 0), ("B", 1, 0),
          ("C", 0, 0), ("C", 0, 1), ("C", 1, 0), ("C", 1, 1)]
TR_BEFORE = [0]
for _kind, _qblk, _map in GROUPS:
    TR_BEFORE.append(TR_BEFORE[-1] + (2 * (_qblk + 1) if _kind != "C" or _map == 1 else 0))

WARM_START, WARM_FIRST, WARM_NORM, WARM_HEADS, WARM_TAIL = 9, 26, 16, 8, 14
WARM_ROUTE = (12, 16, 10)


def hidden_after(what, c):
    if what == "up" and c in (0, FC - 1):
        return c
    if what == "down" and c + 1 < FC - 1:
        return c + 1
    return None


def slope(h):
    return 2.0 ** (-(h + 1))


def dense_slot(k):
    if k < N_DENSE:
        return k % DENSE_SLOTS, k // DENSE_SLOTS + 1
    return moe_slot(k - N_DENSE)


def moe_slot(m):
    s = (m + DENSE_SLOTS) % SLOTS
    return s, (N_DENSE // DENSE_SLOTS if s < DENSE_SLOTS else 0) + m // SLOTS + 1


def trunk(nc, x_in, w_dense, w_moe, cst, bias_cst, vec_rows, sinks, b_forget, lam_rows, subln, w_router, out):
    with ExitStack() as ctx:
        def sb(name, shape, dt=F32):
            return ctx.enter_context(nc.sbuf_tensor(name, shape, dt))

        def sem(name):
            return ctx.enter_context(nc.semaphore(name))

        raw = sb("raw", [P, SLOTS * UNIT])
        whi = sb("whi", [P, SPLIT_AHEAD, UNIT], F32R)
        wlo = sb("wlo", [P, SPLIT_AHEAD, UNIT], F32R)
        x = sb("x", [P, TB, D])
        acc = sb("acc", [P, TB, D])
        xth = sb("xth", [P, KT, TOK], F32R)
        xtl = sb("xtl", [P, KT, TOK], F32R)
        hth = sb("hth", [P, 512], F32R)
        htl = sb("htl", [P, 512], F32R)
        htmp = sb("htmp", [P, 512])
        work = sb("work", [P, 1536])
        con = sb("con", [P, C_END])
        wrh = sb("wrh", [P, KT, N_EXP], F32R)
        wrl = sb("wrl", [P, KT, N_EXP], F32R)
        mx = sb("mx", [P, 2, 8])
        negm = sb("negm", [P, 2, 8])
        sm = sb("sm", [P, 4, 8])
        den = sb("den", [P, 2, 8])
        rec = sb("rec", [P, 2, 8])
        snk = sb("snk", [P, 3, 8])
        logf = sb("logf", [P, TB, 8])
        cumtok = sb("cumtok", [P, TB, 8])
        biasb = sb("biasb", [P, 8, BIAS_W])
        stats = sb("stats", [P, TB, 6])
        var = sb("var", [P, 2, 8])
        std = sb("std", [P, 2, 8])
        eps = sb("eps", [P, 1])
        lam = sb("lam", [P, 4])
        posm = sb("posm", [P, TB, 17])
        gates = sb("gates", [P, TB, 17])
        flag = sb("flag", [1, 1], I32)
        lgt = biasb[0:8, 0, 0:TOK]

        extra = raw[:, DENSE_SLOTS * UNIT:]
        qa = extra[:, 0:1024].rearrange("p (b t) -> p b t", t=TOK)
        ka = extra[:, 1024:1536].rearrange("p (b t) -> p b t", t=TOK)
        qb = extra[:, 1536:2560].rearrange("p (b t) -> p b t", t=TOK)
        kb = extra[:, 2560:3584].rearrange("p (b t) -> p b t", t=TOK)
        ve = extra[:, 3584:4864].rearrange("p (t n) -> p t n", t=TB)
        fz = extra[:, 5376:5520].rearrange("p (i n) -> p i n", n=16)
        qo = extra[:, 0:2048].rearrange("p (b t) -> p b t", t=TOK)
        ko = extra[:, 2048:4096].rearrange("p (b t) -> p b t", t=TOK)
        vo = extra[:, 4096:6144].rearrange("p (t n) -> p t n", t=TB)
        S = [extra[:, 6144 + 2048 * i:8192 + 2048 * i].rearrange("p (h n) -> p h n", h=8) for i in range(2)]
        spare = biasb[:, :, :].rearrange("p h n -> p (h n)")
        PT2 = [extra[:, 10240 + 2048 * i:12288 + 2048 * i].rearrange("p (k n) -> p k n", k=2) for i in range(2)]
        PT = 2 * PT2 + [None, PT2[0], None, PT2[1]]

        def hidden(c):
            if c < FC - 1:
                return hth[:, :], htl[:, :]
            return (t[:, 0:2, :].rearrange("p k n -> p (k n)") for t in (xth, xtl))

        gb_extra = extra[:, 12288:14336].rearrange("p (i n) -> p i n", i=2)
        gb_last = raw[:, 0:2048].rearrange("p (i n) -> p i n", i=2)
        bias = work[:, 0:B_END]
        wr_raw = work[:, B_END:B_END + 64].rearrange("p (k n) -> p k n", n=8)
        sub_g = work[:, B_END + 64:B_END + 192]
        lam_in = work[:, B_END + 192:B_END + 384].rearrange("p (i n) -> p i n", n=DH)
        lam_in2 = biasb[:, 0, 0:DH]
        y = work[:, 0:1024]
        ohot = work[:, 1024:1280].rearrange("p (t s) -> p t s", t=TB)
        ohot_t = work[:, 1280:1536]
        rt = [htmp[:, 16 * i:16 * i + 16].rearrange("p (t n) -> p t n", t=TB) for i in range(16)]
        r1 = [htmp[:, 256 + 2 * i:258 + 2 * i] for i in range(8)]
        ident = con[:, C_ID:C_ID + 128]
        tri = con[:, C_TRI:C_TRI + 128]
        ones = con[:, C_TRI + 128:C_TRI + 256]
        iota = con[:, C_IOTA:C_IOTA + 128]
        revidx = con[:, C_REV:C_REV + 8]

        ps = [ctx.enter_context(nc.psum_tensor(f"ps{i}", [P, 512], F32)) for i in range(8)]

        loaded = [sem(f"loaded{i}") for i in range(SLOTS)]
        c_in = sem("consts_in")
        x_here = [sem(f"x_block{tb}_in") for tb in range(TB)]
        small_in = sem("small_rows_in")
        tables_in = sem("bias_and_router_in")
        gb_in = sem("gain_bias_in")
        hi_rdy = sem("hi_ready")
        lo_rdy = sem("lo_ready")
        w_used = sem("w_used")
        src_rdy = sem("src_ready")
        xt_ps = sem("xt_in_psum")
        xth_rdy = sem("xth_ready")
        xtl_rdy = sem("xtl_ready")
        in_ev = sem("proj_evacuated")
        s_ps = sem("scores_in_psum")
        s_max = sem("scores_biased")
        neg_rdy = sem("negmax_ready")
        e_rdy = sem("exp_ready")
        snk_exp = sem("sink_exp_ready")
        tr_ps = sem("probs_t_in_psum")
        pt_ev = sem("probs_t_ready")
        o_ps = sem("attn_out_in_psum")
        o_ev = sem("attn_out_ready")
        fg_v = sem("forget_vector")
        fg_s = sem("forget_scalar")
        cum_ps = sem("cum_in_psum")
        bb_rdy = sem("b_bias_ready")
        lam_v = sem("lambda_sums")
        lam_s = sem("lambda_exps")
        zeroed = sem("zeroed")
        combined = sem("maps_combined")
        added = sem("norm_input_ready")
        mean_rdy = sem("mean_ready")
        sq_rdy = sem("head_squares_ready")
        var_rdy = sem("head_variances_ready")
        std_rdy = sem("std_ready")
        sum_rdy = sem("branch_sum_ready")
        f_silu = sem("ffn_silu")
        f_h = sem("ffn_hidden")
        f_hi = sem("ffn_hidden_hi")
        f_lo = sem("ffn_hidden_lo")
        wr_h = sem("router_hi")
        wr_l = sem("router_lo")
        lg_ps = sem("logits_in_psum")
        lgt_rdy = sem("logits_t_ready")
        top_v = sem("top2_diff")
        top_s = sem("top2_exp")
        sel_rdy = sem("choice_ready")
        pos_ps = sem("positions_in_psum")
        flag_rdy = sem("flag_ready")
        m_silu = sem("expert_silu")
        m_h = sem("expert_hidden")
        m_tr = sem("expert_hidden_t_in_psum")
        m_hi = sem("expert_hidden_hi")
        m_lo = sem("expert_hidden_lo")
        ga_ps = sem("gathered_in_psum")
        ga_hi = sem("gathered_hi")
        ga_lo = sem("gathered_lo")
        oh_rdy = sem("onehot_ready")
        oht_ps = sem("onehot_t_in_psum")
        oht_rdy = sem("onehot_t_ready")
        ye_rdy = sem("expert_out_ready")
        sc_ps = sem("scattered_in_psum")
        sc_acc = sem("scattered_added")
        dve_self = sem("vector_chain")
        act_self = sem("scalar_chain")
        stored = sem("stored")


        OUT_BANKS = [(0,), (1,), (2,), (3,), None, (0, 1), None, (2, 3)]

        def prob_banks(g):
            return (0, 1) if g == 3 else (6, 7)

        def tile_of(t, i):
            if t == 1:
                return i % 2, i // 2, (2, 3, 0, 1)[i]
            return i // 2, i % 2, i

        BETWEEN = [{4: [("scores", 0, 4)], 5: [("turn", 0, 0), ("scores", 1, 0)],
                    6: [("values", 0, 0), ("turn", 1, 0)], 7: [("values", 1, 0)],
                    8: [("scores", 2, 8)], 9: [("turn", 2, 0)]},
                   {4: [("scores", 4, 4)], 8: [("scores", 5, 8)],
                    9: [("turn", 5, 0), ("scores", 6, 0)], 10: [("scores", 7, 0)],
                    11: [("values", 5, 12), ("turn", 7, 0)]}]

        def heads_in_psum(qblk):
            return [ps[OUT_BANKS[5 + 2 * qblk][h // 4]][:, (h % 4) * P:(h % 4) * P + P] for h in range(8)]

        VALUE_ORDER = (0, 1, 2, 3, 5, 7)

        SCORE_ORDER = (0, 2, 1, 3, 4, 6, 5, 7)

        def score_at(h):
            return ps[2 * (h % 2) + h // 4], (h // 2 % 2) * 256

        def unit(t, j):
            return t[:, j % SPLIT_AHEAD, :]

        def as_cols(t, j):
            return unit(t, j).rearrange("p (k n) -> p k n", k=KT)

        def as_rows(t, j):
            return unit(t, j).rearrange("p (k n) -> p k n", k=2)

        def as_half(t, j):
            return unit(t, j).rearrange("p (k n) -> p k n", k=4)

        def yb(tb, n):
            return ps[4 + 2 * tb + n]

        block = ctx.enter_context(nc.Block())

        @block.sync
        def _(sp):
            def load(src, s):
                sp.dma_start(raw[:, s * UNIT:(s + 1) * UNIT], src).then_inc(loaded[s], 16)

            for tb in range(TB):
                sp.dma_start(x[:, tb, :], x_in[0, tb * P:(tb + 1) * P, :]).then_inc(x_here[tb], 16)
            for k in range(N_DENSE):
                if k >= DENSE_SLOTS:
                    sp.wait_ge(lo_rdy, k - DENSE_SLOTS + 1)
                load(w_dense[k], dense_slot(k)[0])
            for m in range(SLOTS):
                if m < DENSE_SLOTS - 1:
                    sp.wait_ge(o_ps, 6)
                elif m == DENSE_SLOTS - 1:
                    sp.wait_ge(src_rdy, 8)
                else:
                    sp.wait_ge(lo_rdy, N_DENSE + m - 2 * DENSE_SLOTS + 1)
                load(w_moe[m], moe_slot(m)[0])
            with sp.Fori(0, N_EXP - 1) as e:
                for j in range(PER_EXP):
                    sp.wait_ge(lo_rdy, e * PER_EXP + (N_DENSE + j + 1))
                    load(w_moe[e * PER_EXP + (SLOTS + j)], moe_slot(SLOTS + j)[0])
            for m in range(SLOTS + (N_EXP - 1) * PER_EXP, N_PASS0):
                sp.wait_ge(lo_rdy, N_DENSE + m - SLOTS + 1)
                load(w_moe[m], moe_slot(m)[0])
            sp.wait_ge(flag_rdy, 1)
            more = sp.value_load(flag[0:1, 0:1], min_val=0, max_val=1)
            with sp.If(more > 0):
                with sp.Fori(N_EXP, 2 * N_EXP) as e:
                    for j in range(PER_EXP):
                        m0 = SPLIT_AHEAD + j
                        sp.wait_ge(lo_rdy, e * PER_EXP + (N_DENSE + m0 - SLOTS + 1))
                        load(w_moe[(e - N_EXP) * PER_EXP + m0], moe_slot(m0)[0])
            with sp.Else():
                sp.nop()
            for tb in range(TB):
                sp.wait_ge(src_rdy, 9 + tb)
                sp.dma_start(out[0, tb * P:(tb + 1) * P, :], x[:, tb, :]).then_inc(stored, 16)
            sp.wait_ge(stored, 32)

        @block.gpsimd
        def _(pool):
            pool.dma_start(snk[:, 0, :], sinks.partition_broadcast(P)).then_inc(small_in, 16)
            pool.dma_start(snk[:, 2, :], b_forget.partition_broadcast(P)).then_inc(small_in, 16)
            pool.dma_start(lam_in, lam_rows[0:3].partition_broadcast(P)).then_inc(small_in, 16)
            pool.dma_start(lam_in2, lam_rows[3].partition_broadcast(P)).then_inc(small_in, 16)
            pool.dma_start(sub_g, subln.partition_broadcast(P)).then_inc(small_in, 16)
            pool.wait_ge(loaded[1], 16)
            pool.dma_start(bias, bias_cst).then_inc(tables_in, 16)
            pool.dma_start(wr_raw, w_router).then_inc(tables_in, 16)
            for n, (s, v) in enumerate(((o_ev, 4), (src_rdy, 2), (o_ps, 6))):
                pool.wait_ge(s, v)
                pool.dma_start(gb_extra, vec_rows[n].partition_broadcast(P)).then_inc(gb_in, 16)
            pool.wait_ge(flag_rdy, 1)
            more = pool.value_load(flag[0:1, 0:1], min_val=0, max_val=1)
            with pool.If(more > 0):
                pool.wait_ge(lo_rdy, N_DENSE + N_MOE + N_PASS0)
            with pool.Else():
                pool.wait_ge(lo_rdy, N_DENSE + N_PASS0)
            pool.dma_start(gb_last, vec_rows[3].partition_broadcast(P)).then_inc(gb_in, 16)

        @block.tensor
        def _(pe):
            mm = pe.matmul

            def three(o, lh, ll, rh, rl, start, stop):
                mm(o, lh, rh, start=start, stop=False)
                mm(o, lh, rl, start=False, stop=False)
                return mm(o, ll, rh, start=False, stop=stop)

            def keep_warm(n, bank, tile=ident):
                for _ in range(n):
                    mm(ps[bank][:, 0:P], tile, tile, start=True, stop=True)

            def turn(t, tiles=range(4)):
                src = acc if t in (1, 4) else x
                for j in tiles:
                    if j == 2 and t in (2, 3, 5):
                        keep_warm(WARM_NORM, 3)
                    if j % 2 == 0 and t == 4:
                        keep_warm(WARM_HEADS, 4 - 2 * j)
                    tb, half, bank = tile_of(t, j)
                    if t == 0:
                        pe.wait_ge(x_here[tb], 16)
                        pe.wait_ge(c_in, 16)
                    elif t == 1:
                        pe.wait_ge(o_ev, 2 * half + tb + 1)
                    else:
                        pe.wait_ge(src_rdy, 2 * (t - 2) + tb + 1)
                    for i in range(4):
                        kt = 4 * half + i
                        r = pe.transpose(ps[bank][:, i * P:(i + 1) * P], src[:, tb, kt * P:(kt + 1) * P], ident)
                    r.then_inc(xt_ps, 1)
                pe.wait_ge(xth_rdy, 4 * t + tiles[-1] + 1)
                pe.wait_ge(xtl_rdy, 4 * t + tiles[-1] + 1)

            def to_rows(k, bank):
                h, l = as_cols(whi, k), as_cols(wlo, k)
                for b in range(2):
                    for kt in range(KT):
                        c = slice(b * P, b * P + P)
                        r = three(ps[bank][:, b * TOK:(b + 1) * TOK], h[:, kt, c], l[:, kt, c],
                                  xth[:, kt, :], xtl[:, kt, :], kt == 0, kt == KT - 1)
                return r

            def to_cols(k, bank, n, blocks=range(TB)):
                h, l = as_cols(whi, k), as_cols(wlo, k)
                for tb in blocks:
                    for kt in range(KT):
                        t = slice(tb * P, tb * P + P)
                        r = three(ps[bank][:, tb * 256:tb * 256 + n], xth[:, kt, t], xtl[:, kt, t],
                                  h[:, kt, 0:n], l[:, kt, 0:n], kt == 0, kt == KT - 1)
                return r

            def project(k0, kinds):
                g = 0 if k0 == 0 else 4
                seen = 0 if k0 == 0 else U_IN_E
                for i, width in enumerate(kinds):
                    k = k0 + i
                    if i >= 2:
                        pe.wait_ge(in_ev, seen + i - 1)
                    pe.wait_ge(lo_rdy, k + 1)
                    r = to_cols(k, 4 + i % 2, width) if width else to_rows(k, 4 + i % 2)
                    r.then_inc(w_used, 1)
                    if k == 3:
                        cumulate()
                    for what, j, n in BETWEEN[g // 4].get(i, ()):
                        if n:
                            pe.wait_ge(in_ev, seen + n)
                        if what == "scores":
                            scores(j)
                        if what == "turn":
                            turn_probs(j)
                        if what == "values":
                            values(j)

            def scores(g):
                kind, qblk, mp = GROUPS[g]
                nk = P * (qblk + 1)
                q_cols = slice(qblk * P, qblk * P + P)
                if g == 0:
                    pe.wait_ge(bb_rdy, 1)
                if g in (2, 4):
                    pe.wait_ge(o_ev, g)
                elif g:
                    pe.wait_ge(s_max, 8 * g)
                for h in SCORE_ORDER:
                    rows = slice(64 * (h % 2), 64 * (h % 2) + 64)
                    if kind == "A":
                        q, kk = qa[rows, h // 2, q_cols], ka[rows, int(h // 4 != h % 2), 0:nk]
                    elif kind == "B":
                        q, kk = qb[rows, h // 2, q_cols], kb[rows, h // 2, 0:nk]
                    else:
                        b = 4 * mp + h // 2
                        q, kk = qo[rows, b, q_cols], ko[rows, b, 0:nk]
                    bank, c0 = score_at(h)
                    r = mm(bank[:, c0:c0 + nk], q, kk, start=True, stop=True)
                    if h & 2:
                        r.then_inc(s_ps, 1)

            def cumulate():
                pe.wait_ge(fg_v, 4)
                mm(ps[6][:, 0:8], tri, logf[:, 0, :], start=True, stop=True)
                mm(ps[6][:, 8:16], ones, logf[:, 0, :], start=True, stop=False)
                mm(ps[6][:, 8:16], tri, logf[:, 1, :], start=False, stop=True).then_inc(cum_ps, 1)
                for h in range(8):
                    o = ps[h // 2][:, (h % 2) * 256:(h % 2) * 256 + 256]
                    f = [logf[:, b, h:h + 1].to_broadcast([P, P]) for b in range(TB)]
                    mm(o[:, 0:P], f[0], tri, start=True, stop=True)
                    mm(o[:, P:TOK], f[0], ones, start=True, stop=False)
                    r = mm(o[:, P:TOK], f[1], tri, start=False, stop=True)
                    if h % 2:
                        r.then_inc(cum_ps, 1)

            def turn_probs(g):
                n = TR_BEFORE[g]
                for kt in range(GROUPS[g][1] + 1):
                    for half in range(2):
                        if n >= 2:
                            pe.wait_ge(pt_ev, n - 1)
                        if g < 4:
                            pe.wait_ge(e_rdy, 8 * g + 4 * half + 4)
                        else:
                            pe.wait_ge(combined, 4 * (g - 5) + 4 * half + 4)
                        for i in range(4):
                            r = pe.transpose(ps[prob_banks(g)[half]][:, i * P:(i + 1) * P],
                                             S[0 if g >= 4 else g % 2][:, 4 * half + i, kt * P:(kt + 1) * P],
                                             ident)
                        r.then_inc(tr_ps, 1)
                        n += 1

            def values(g):
                kind, qblk, _ = GROUPS[g]
                pe.wait_ge(pt_ev, TR_BEFORE[g + 1])
                if g == 0:
                    pe.wait_ge(s_max, 8 * 2)
                if g == 5:
                    pe.wait_ge(s_max, 8 * len(GROUPS))
                for h in range(8):
                    if kind == "C":
                        o = ps[OUT_BANKS[g][h // 4]][:, (h % 4) * P:(h % 4) * P + P]
                    else:
                        o = ps[OUT_BANKS[g][0]][:, h * DH:(h + 1) * DH]
                    for kt in range(qblk + 1):
                        if kind == "A":
                            v = ve[:, kt, (h // 4) * DH:(h // 4) * DH + DH]
                        elif kind == "B":
                            v = ve[:, kt, A_KV + h * DH:A_KV + (h + 1) * DH]
                        else:
                            v = vo[:, kt, h * P:(h + 1) * P]
                        r = mm(o, PT[g][:, kt, h * P:(h + 1) * P], v, start=kt == 0, stop=kt == qblk)
                r.then_inc(o_ps, 1)

            def mix(k, tb, first, last, lh, ll):
                h, l = as_rows(whi, k), as_rows(wlo, k)
                for r2 in range(2):
                    for n in range(2):
                        c = slice(n * 512, n * 512 + 512)
                        r = three(yb(tb, n)[:, :], lh(r2, tb), ll(r2, tb), h[:, r2, c], l[:, r2, c],
                                  first and r2 == 0, last and r2 == 1)
                if tb == 1:
                    r.then_inc(w_used, 1)
                elif last:
                    r.then_inc(sum_rdy, 1)

            def out_rows(k0, u, tb):
                pe.wait_ge(lo_rdy, k0 + u + 1)
                mix(k0 + u, tb, u == 0, u == U_OUT - 1,
                    lambda r2, tb: xth[:, 2 * u + r2, tb * P:(tb + 1) * P],
                    lambda r2, tb: xtl[:, 2 * u + r2, tb * P:(tb + 1) * P])

            def even_end():
                k0 = K_OUT_E
                scores(3)
                pe.wait_ge(s_max, 8 * 4)
                turn(1, (0, 1))
                pe.wait_ge(in_ev, U_IN_E)
                pe.wait_ge(pt_ev, TR_BEFORE[3])
                out_rows(k0, 0, 0)
                out_rows(k0, 0, 1)
                turn_probs(3)
                values(2)
                values(3)
                out_rows(k0, 1, 0)
                out_rows(k0, 1, 1)
                turn(1, (2, 3))
                for tb in range(TB):
                    out_rows(k0, 2, tb)
                    out_rows(k0, 3, tb)

            def odd_end():
                k0 = K_OUT_O
                values(7)
                for tb in range(TB):
                    turn(4, (2 * tb, 2 * tb + 1))
                    for u in range(3):
                        out_rows(k0, u, tb)
                for tb in range(TB):
                    out_rows(k0, 3, tb)

            def down(c, tb, k):
                h, l = hidden(c)
                mix(k, tb, c == 0, c == FC - 1,
                    lambda r2, tb: h[:, r2 * TOK + tb * P:r2 * TOK + (tb + 1) * P],
                    lambda r2, tb: l[:, r2 * TOK + tb * P:r2 * TOK + (tb + 1) * P])

            pe.wait_ge(zeroed, 1)
            keep_warm(WARM_START, 5, htmp[:, 0:P])
            turn(0)
            keep_warm(WARM_FIRST, 5)
            project(0, [256] + 7 * [None] + [256, 256])
            even_end()
            turn(2)
            for i, (what, c) in enumerate(FFN_ORDER):
                k = K_FFN + i
                pe.wait_ge(lo_rdy, k + 1)
                if what == "down":
                    if c < FC - 2:
                        pe.wait_ge(f_lo, c + 1)
                        down(c, 0, k)
                        down(c, 1, k)
                    elif c == FC - 1:
                        pe.wait_ge(f_lo, c)
                        down(c - 1, 0, k - 1)
                        pe.wait_ge(f_lo, c + 1)
                        down(c, 0, k)
                        down(c - 1, 1, k - 1)
                        down(c, 1, k)
                else:
                    if what == "gate" and c >= 2:
                        pe.wait_ge(f_h, c - 1)
                    r = to_rows(k, (0 if what == "gate" else 2) + c % 2)
                    r.then_inc(w_used, 1)
            turn(3)
            project(K_IN_O, 8 * [None] + 4 * [256])
            odd_end()
            turn(5)

            pe.wait_ge(wr_l, 1)
            for kt in range(KT):
                for i, (a, b) in enumerate(((wrh, xth), (wrh, xtl), (wrl, xth), (wrl, xtl))):
                    r = mm(ps[0][0:8, 0:TOK], a[:, kt, :], b[:, kt, :],
                           start=kt == 0 and i == 0, stop=kt == KT - 1 and i == 3)
            r.then_inc(lg_ps, 1)
            pe.wait_ge(lgt_rdy, 1)
            for tb in range(TB):
                r = pe.transpose(ps[2][:, tb * 8:tb * 8 + 8], lgt[:, tb * P:(tb + 1) * P], ident[0:8, 0:8])
            r.then_inc(lg_ps, 1)
            keep_warm(WARM_ROUTE[0], 5)
            pe.wait_ge(sel_rdy, 1)
            chosen = rt[10]
            mm(ps[1][:, 0:8], tri, chosen[:, 0, :], start=True, stop=True)
            mm(ps[1][:, 8:16], ones, chosen[:, 0, :], start=True, stop=False)
            mm(ps[1][:, 8:16], tri, chosen[:, 1, :], start=False, stop=True)
            mm(ps[1][0:1, 16:24], ones[:, 0:1], chosen[:, 0, :], start=True, stop=False)
            mm(ps[1][0:1, 16:24], ones[:, 0:1], chosen[:, 1, :], start=False, stop=True).then_inc(pos_ps, 1)
            keep_warm(WARM_ROUTE[1], 5)

            def gather(n):
                pe.wait_ge(oh_rdy, n + 1)
                for kt in range(KT):
                    bank = ps[1 if kt < 4 else 3]
                    for tb in range(TB):
                        r = mm(bank[:, (kt % 4) * P:(kt % 4) * P + P], x[:, tb, kt * P:(kt + 1) * P],
                               ohot[:, tb, :], start=tb == 0, stop=tb == TB - 1)
                r.then_inc(ga_ps, 1)

            def scatter(n, tb):
                if tb == 0:
                    pe.wait_ge(ye_rdy, n + 1)
                    pe.wait_ge(oht_rdy, n + 1)
                for nn in range(2):
                    i = 2 * tb + nn
                    if tb == 1:
                        pe.wait_ge(sc_acc, n * 4 + (i - 1))
                    mm(ps[7 if i % 2 == 0 else 4][:, :], ohot_t[:, tb * P:(tb + 1) * P],
                       y[:, nn * 512:(nn + 1) * 512], start=True, stop=True).then_inc(sc_ps, 1)

            def expert(e):
                def hidden_t(c):
                    pe.wait_ge(m_h, e * EC + (c + 1))
                    if c == 0:
                        pe.wait_ge(sc_acc, e * 4 + 4)
                    for i in range(4):
                        r = pe.transpose(ps[4][:, i * P:(i + 1) * P], htmp[:, i * P:(i + 1) * P], ident)
                    r.then_inc(m_tr, 1)

                for j, (what, c, half) in enumerate(EXP_ORDER):
                    if j == 0:
                        pe.wait_ge(ga_lo, e + 1)
                    pe.wait_ge(lo_rdy, e * PER_EXP + (N_DENSE + j + 1))
                    if what == "down":
                        if half == 0:
                            pe.wait_ge(m_lo, e * EC + (c + 1))
                        h, l = as_rows(whi, j), as_rows(wlo, j)
                        for r2 in range(2):
                            f = slice((2 * half + r2) * P, (2 * half + r2 + 1) * P)
                            for n in range(2):
                                cc = slice(n * 512, n * 512 + 512)
                                r = three(ps[5 + n][:, :], hth[:, f], htl[:, f], h[:, r2, cc], l[:, r2, cc],
                                          c == 0 and half == 0 and r2 == 0,
                                          c == EC - 1 and half == 1 and r2 == 1)
                    else:
                        bank = ps[(0 if what == "gate" else 2) + c % 2]
                        h, l = as_half(whi, j), as_half(wlo, j)
                        for i in range(4):
                            kt = 4 * half + i
                            r = three(bank[:, :], xth[:, kt, 0:P], xtl[:, kt, 0:P], h[:, i, :], l[:, i, :],
                                      kt == 0, kt == KT - 1)
                    r.then_inc(w_used, 1)
                    if j == 1:
                        scatter(e, 0)
                    if j == 3:
                        scatter(e, 1)
                    if j == 5:
                        pe.wait_ge(sc_acc, e * 4 + 3)
                        for tb in range(TB):
                            r = pe.transpose(ps[7][:, tb * P:(tb + 1) * P], ohot[:, tb, :], ident)
                        r.then_inc(oht_ps, 1)
                    if (what, half) == ("gate", 1) and c:
                        hidden_t(c - 1)
                    if j == PER_EXP - 3:
                        hidden_t(EC - 1)
                        gather(e + 1)

            gather(0)
            keep_warm(WARM_ROUTE[2], 5)
            with pe.Fori(0, N_EXP) as e:
                expert(e)
            keep_warm(WARM_TAIL, 0)
            pe.wait_ge(flag_rdy, 1)
            more = pe.value_load(flag[0:1, 0:1], min_val=0, max_val=1)
            with pe.If(more > 0):
                with pe.Fori(N_EXP, 2 * N_EXP) as e:
                    expert(e)
                scatter(2 * N_EXP, 0)
                scatter(2 * N_EXP, 1)
            with pe.Else():
                scatter(N_EXP, 0)
                scatter(N_EXP, 1)

        @block.scalar
        def _(act):
            A = act.activation

            def hi(wait, used, j, slot):
                act.wait_ge(loaded[slot], wait)
                if used is not None:
                    act.wait_ge(w_used, used)
                A(unit(whi, j), raw[:, slot * UNIT:(slot + 1) * UNIT], ACT.Copy).then_inc(hi_rdy, 1)

            def split(k):
                s, n = dense_slot(k)
                hi(16 * n, k - SPLIT_AHEAD + 1 if k >= SPLIT_AHEAD else None, k, s)

            def splits(k):
                if k + 2 not in (K_FFN, K_IN_O, N_DENSE):
                    split(k + SPLIT_AHEAD)

            def turned(t, tiles=range(4)):
                for i in tiles:
                    tb, half, bank = tile_of(t, i)
                    act.wait_ge(xt_ps, 4 * t + i + 1)
                    A(xth[:, 4 * half:4 * half + 4, tb * P:(tb + 1) * P],
                      ps[bank][:, :].rearrange("p (k n) -> p k n", k=4), ACT.Copy).then_inc(xth_rdy, 1)

            chained = [0]

            def link(r):
                chained[0] += 1
                r.then_inc(act_self, 1)
                act.wait_ge(act_self, chained[0])

            def root(i, v, n):
                A(std[:, i, 0:v.shape[1]], v, ACT.Sqrt, bias=eps[:, 0:1], scale=1.0 / n).then_inc(std_rdy, 1)

            def norm_mean(n, tb):
                st = stats[:, tb, :]
                for h in range(2):
                    act.wait_ge(added, 4 * n + 2 * tb + h + 1)
                    r = A(spare[:, h * 512:(h + 1) * 512], acc[:, tb, h * 512:(h + 1) * 512], ACT.Copy,
                          accum_out=st[:, h:h + 1])
                link(r)
                link(A(st[:, 2:3], st[:, 1:2], ACT.Copy, scale=-1.0 / D))
                A(st[:, 3:4], st[:, 0:1], ACT.Identity, bias=st[:, 2:3], scale=-1.0 / D).then_inc(mean_rdy, 1)

            def norm_root(n, tb):
                st = stats[:, tb, :]
                act.wait_ge(mean_rdy, 2 * n + tb + 1)
                link(A(spare[:, 1024:2048], acc[:, tb, :], ACT.Square, bias=st[:, 3:4], accum_out=st[:, 4:5]))
                root(tb, st[:, 4:5], D)

            def norm(k, n, t):
                A(stats[:, 0, 5:6], eps[:, 0:1], ACT.Sqrt)
                norm_mean(n, 0)
                norm_root(n, 0)
                norm_mean(n, 1)
                norm_root(n, 1)
                turned(t)
                split(k - 1 + SPLIT_AHEAD)

            def exps(g):
                act.wait_ge(neg_rdy, g + 1)
                nk = P * (GROUPS[g][1] + 1)
                for h in range(8):
                    A(S[g % 2][:, h, 0:nk], S[g % 2][:, h, 0:nk], ACT.Exp, bias=negm[:, g % 2, h:h + 1],
                      accum_out=sm[:, g % 4, h:h + 1]).then_inc(e_rdy, 1)
                if GROUPS[g][0] == "A":
                    A(den[:, g % 2, :], den[:, g % 2, :], ACT.Exp).then_inc(snk_exp, 1)

            def probs_out(g):
                n = TR_BEFORE[g]
                if g >= 2:
                    act.wait_ge(o_ps, min(g - 1, 4))
                for kt in range(GROUPS[g][1] + 1):
                    for half in range(2):
                        act.wait_ge(tr_ps, n + 1)
                        A(PT[g][:, kt, half * 512:(half + 1) * 512], ps[prob_banks(g)[half]][:, :],
                          ACT.Copy).then_inc(pt_ev, 1)
                        n += 1

            def between(layer, i):
                for what, g, _ in BETWEEN[layer].get(i, ()):
                    if what == "scores":
                        exps(g)
                    if what == "turn":
                        probs_out(g)

            def even_end():
                turned(1, (0, 1))
                exps(3)
                split(U_IN_E - 1 + SPLIT_AHEAD)
                probs_out(3)
                turned(1, (2, 3))

            def evac_even(i):
                b = ps[4 + i % 2][:, :].rearrange("p (b t) -> p b t", b=2)
                act.wait_ge(w_used, i + 1)
                if i == 0:
                    A(ve[:, :, 0:A_KV], b[:, :, 0:A_KV], ACT.Copy)
                    r = A(fz[:, 0, :].rearrange("p (t n) -> p t n", t=TB), b[:, :, A_KV:A_KV + 8], ACT.Copy)
                elif i < 3:
                    for s in range(2):
                        blk = 2 * (i - 1) + s
                        r = A(qa[:, blk, :], b[:, s, :], ACT.Copy, scale=con[:, C_QS + blk:C_QS + blk + 1])
                elif i == 3:
                    r = A(ka[:, :, :], b, ACT.Copy)
                elif i < 6:
                    r = A(qb[:, 2 * (i - 4):2 * (i - 4) + 2, :], b, ACT.Copy, scale=DH ** -0.5)
                elif i < 8:
                    r = A(kb[:, 2 * (i - 6):2 * (i - 6) + 2, :], b, ACT.Copy)
                else:
                    r = A(ve[:, :, A_KV + (i - 8) * 256:A_KV + (i - 7) * 256], b, ACT.Copy)
                r.then_inc(in_ev, 1)

            def evac_odd(i):
                b = ps[4 + i % 2][:, :].rearrange("p (b t) -> p b t", b=2)
                act.wait_ge(w_used, K_IN_O + i + 1)
                if i >= 8:
                    r = A(vo[:, :, (i - 8) * 256:(i - 7) * 256], b, ACT.Copy)
                else:
                    blk = 4 * (i // 4) + 2 * (i % 2)
                    if i % 4 < 2:
                        for s in range(2):
                            r = A(qo[:, blk + s, :], b[:, s, :], ACT.Copy,
                                  scale=con[:, C_QS + (blk + s) % 4:C_QS + (blk + s) % 4 + 1])
                    else:
                        r = A(ko[:, blk:blk + 2, :], b, ACT.Copy)
                r.then_inc(in_ev, 1)

            act.dma_start(con[:, :], cst).then_inc(c_in, 16)
            act.wait_ge(c_in, 16)
            A(lam[:, 0:1], con[:, 0:1], ACT.Copy)
            turned(0)
            split(0)
            split(1)
            split(2)
            for k in range(N_DENSE):
                if k < U_IN_E:
                    evac_even(k)
                if K_IN_O <= k < K_OUT_O:
                    evac_odd(k - K_IN_O)
                if k == K_FFN - 1:
                    norm(k, 0, 2)
                if K_FFN <= k < K_IN_O:
                    what, c = FFN_ORDER[k - K_FFN]
                    if what == "up":
                        act.wait_ge(w_used, k + 1)
                        if c:
                            act.wait_ge(f_lo, c)
                        A(htmp[:, :], ps[c % 2][:, :], ACT.Silu).then_inc(f_silu, 1)
                    n = hidden_after(what, c)
                    if n is not None:
                        act.wait_ge(w_used, k + 1)
                        act.wait_ge(f_h, n + 1)
                        A(list(hidden(n))[0], htmp[:, :], ACT.Copy).then_inc(f_hi, 1)
                if k == K_IN_O - 1:
                    norm(k, 1, 3)
                if k == N_DENSE - 1:
                    norm(k, 2, 5)
                if k != U_IN_E - 1:
                    splits(k)
                if k < U_IN_E:
                    between(0, k)
                if K_IN_O <= k < K_OUT_O:
                    between(1, k - K_IN_O)
                if k == 1:
                    act.wait_ge(lam_v, 1)
                    A(lam[:, 0:2], lam[:, 0:2], ACT.Exp).then_inc(lam_s, 1)
                    act.wait_ge(fg_v, 1)
                    A(fz[:, 2, :], fz[:, 2, :], ACT.Exp, scale=-1.0).then_inc(fg_s, 1)
                    act.wait_ge(fg_v, 2)
                    A(fz[:, 4, :], fz[:, 3, :], ACT.Ln).then_inc(fg_s, 1)
                if k == 3:
                    act.wait_ge(tables_in, 2 * 16)
                    A(wrh[:, :, :], wr_raw, ACT.Copy).then_inc(wr_h, 1)
                if k == U_IN_E - 1:
                    even_end()
                if k == K_OUT_O - 1:
                    A(stats[:, 0, 5:6], eps[:, 0:1], ACT.Sqrt)
                    for tb in range(TB):
                        act.wait_ge(o_ps, VALUE_ORDER.index(5 + 2 * tb) + 1)
                        for h, o in enumerate(heads_in_psum(tb)):
                            r = A(spare[:, (8 * tb + h) * P:(8 * tb + h + 1) * P], o, ACT.Square,
                                  accum_out=var[:, tb, h:h + 1])
                        r.then_inc(sq_rdy, 1)
                        act.wait_ge(var_rdy, tb + 1)
                        root(tb, var[:, tb, :], P)
                        turned(4, (2 * tb, 2 * tb + 1))
            act.wait_ge(top_v, 1)
            A(r1[3], r1[2], ACT.Exp).then_inc(top_s, 1)
            act.wait_ge(flag_rdy, 1)
            A(y, iota.unsqueeze(1).to_broadcast([P, 8, P]), ACT.Copy, scale=0.0).then_inc(ye_rdy, 1)
            A(ohot_t, con[:, 0:256], ACT.Copy, scale=0.0).then_inc(oht_rdy, 1)

            def gathered(n):
                for q in range(2):
                    act.wait_ge(ga_ps, n + 1)
                    r = A(xth[:, 4 * q:4 * q + 4, 0:P], ps[1 + 2 * q][:, :].rearrange("p (k n) -> p k n", k=4), ACT.Copy)
                r.then_inc(ga_hi, 1)

            def expert(e):
                for j, (what, c, half) in enumerate(EXP_ORDER):
                    s, n = moe_slot(j + SPLIT_AHEAD)
                    if j != PER_EXP - 3:
                        hi(e * (16 * (PER_EXP // SLOTS)) + 16 * n, e * PER_EXP + (N_DENSE + j + 1), j, s)
                    if j == 6:
                        act.wait_ge(oht_ps, e + 1)
                        A(ohot_t, ps[7][:, 0:256], ACT.Copy).then_inc(oht_rdy, 1)
                    if (what, half) == ("up", 1):
                        act.wait_ge(w_used, e * PER_EXP + (N_DENSE + j + 1))
                        A(htmp[:, :], ps[c % 2][:, :], ACT.Silu).then_inc(m_silu, 1)
                    if ((what, half) == ("gate", 1) and c) or j == PER_EXP - 3:
                        act.wait_ge(m_tr, e * EC + (c if j != PER_EXP - 3 else EC))
                        A(hth[:, :], ps[4][:, :], ACT.Copy).then_inc(m_hi, 1)
                    if j == PER_EXP - 3:
                        hi(e * (16 * (PER_EXP // SLOTS)) + 16 * n, e * PER_EXP + (N_DENSE + j + 1), j, s)
                        gathered(e + 1)
                    if j == PER_EXP - 1:
                        act.wait_ge(w_used, e * PER_EXP + (N_DENSE + j + 1))
                        for nn in range(2):
                            r = A(y[:, nn * 512:(nn + 1) * 512], ps[5 + nn][:, :], ACT.Copy)
                        r.then_inc(ye_rdy, 1)

            gathered(0)
            A(r1[3], r1[3], ACT.Silu)
            with act.Fori(0, N_EXP) as e:
                expert(e)
            more = act.value_load(flag[0:1, 0:1], min_val=0, max_val=1)
            with act.If(more > 0):
                with act.Fori(N_EXP, 2 * N_EXP) as e:
                    expert(e)
            with act.Else():
                act.nop()
            A(stats[:, 1, 5:6], eps[:, 0:1], ACT.Sqrt)
            for tb in range(TB):
                norm_mean(3, tb)
                norm_root(3, tb)

        @block.vector
        def _(dve):
            chained = [0]

            def link(r):
                chained[0] += 1
                r.then_inc(dve_self, 1)
                dve.wait_ge(dve_self, chained[0])

            def lo(count, j, slot):
                dve.wait_ge(hi_rdy, count)
                dve.tensor_tensor(unit(wlo, j), raw[:, slot * UNIT:(slot + 1) * UNIT],
                                  unit(whi, j).bitcast(F32), ALU.subtract).then_inc(lo_rdy, 1)

            def split(k):
                lo(k + 1, k, dense_slot(k)[0])

            def splits(k):
                if k + 2 not in (K_FFN, K_IN_O, N_DENSE):
                    split(k + SPLIT_AHEAD)

            def turned(t, tiles=range(4)):
                for i in tiles:
                    tb, half, bank = tile_of(t, i)
                    part = (slice(None), slice(4 * half, 4 * half + 4), slice(tb * P, (tb + 1) * P))
                    dve.wait_ge(xth_rdy, 4 * t + i + 1)
                    dve.tensor_tensor(xtl[part], ps[bank][:, :].rearrange("p (k n) -> p k n", k=4),
                                      xth[part].bitcast(F32), ALU.subtract).then_inc(xtl_rdy, 1)

            def score_max(g):
                kind, qblk, _ = GROUPS[g]
                nk = P * (qblk + 1)
                b0 = P * qblk
                if g in (2, 3, 6):
                    dve.wait_ge(tr_ps, TR_BEFORE[6 if g == 6 else g - 1])
                for i, h in enumerate(SCORE_ORDER):
                    dve.wait_ge(s_ps, 4 * g + i // 2 + 1)
                    bank, c0 = score_at(h)
                    dve.tensor_tensor_reduce(
                        out=S[g % 2][:, h, 0:nk], in0=bank[:, c0:c0 + nk],
                        in1=biasb[:, h, b0:b0 + nk] if kind == "B" else
                        bias[:, (B_A if kind == "A" else B_C) + b0:(B_A if kind == "A" else B_C) + b0 + nk],
                        scale=1.0 if kind == "B" else slope(h), scalar=-BIG,
                        op0=ALU.subtract if kind == "B" else ALU.add, op1=ALU.max,
                        accum_out=mx[:, g % 2, h:h + 1]).then_inc(s_max, 1)
                dve.wait_ge(s_max, 8 * g + 8)
                if kind == "A":
                    link(dve.scalar_tensor_tensor(out=negm[:, g % 2, :], in0=mx[:, g % 2, :], scalar=-1.0,
                                                  in1=snk[:, 1, :], op0=ALU.mult, op1=ALU.min))
                    dve.tensor_tensor(den[:, g % 2, :], snk[:, 0, :], negm[:, g % 2, :], ALU.add).then_inc(neg_rdy, 1)
                else:
                    dve.tensor_scalar(negm[:, g % 2, :], mx[:, g % 2, :], -1.0, None, ALU.mult).then_inc(neg_rdy, 1)

            def head_out(g):
                kind, qblk, _ = GROUPS[g]
                r8 = rec[:, g % 2, :]
                dve.wait_ge(e_rdy, 8 * g + 8)
                if kind == "A":
                    dve.wait_ge(snk_exp, g + 1)
                    link(dve.tensor_tensor(sm[:, g % 4, :], sm[:, g % 4, :], den[:, g % 2, :], ALU.add))
                link(dve.reciprocal(r8, sm[:, g % 4, :]))
                dve.wait_ge(o_ps, g + 1)
                o = acc[:, qblk, (0 if kind == "A" else 512):(512 if kind == "A" else 1024)]
                dve.tensor_tensor(o.rearrange("p (h n) -> p h n", h=8),
                                  ps[OUT_BANKS[g][0]][:, :].rearrange("p (h n) -> p h n", h=8),
                                  r8.unsqueeze(2).to_broadcast([P, 8, DH]), ALU.mult).then_inc(o_ev, 1)

            def combine(g):
                _, qblk, _ = GROUPS[g]
                nk = P * (qblk + 1)
                ratio = cumtok[:, qblk, :]
                dve.wait_ge(e_rdy, 8 * g + 8)
                link(dve.reciprocal(ratio, sm[:, g % 4, :]))
                link(dve.tensor_tensor(ratio, ratio, sm[:, g % 4 - 1, :], ALU.mult))
                link(dve.tensor_scalar(ratio, ratio, lam[:, 3:4], None, ALU.mult))
                for h in range(8):
                    dve.scalar_tensor_tensor(out=S[0][:, h, 0:nk], in0=S[1][:, h, 0:nk], scalar=ratio[:, h:h + 1],
                                             in1=S[0][:, h, 0:nk], op0=ALU.mult, op1=ALU.add).then_inc(combined, 1)
                link(dve.reciprocal(rec[:, qblk, :], sm[:, g % 4 - 1, :]))
                dve.tensor_tensor(den[:, qblk, :], rec[:, qblk, :], rec[:, qblk, :], ALU.mult)

            def head_norm(qblk):
                dve.wait_ge(sq_rdy, qblk + 1)
                dve.tensor_tensor(var[:, qblk, :], var[:, qblk, :], den[:, qblk, :], ALU.mult).then_inc(var_rdy, 1)

            def head_norm_end(qblk):
                dve.wait_ge(std_rdy, 5 + qblk)
                link(dve.reciprocal(std[:, qblk, :], std[:, qblk, :]))
                link(dve.tensor_tensor(std[:, qblk, :], std[:, qblk, :], rec[:, qblk, :], ALU.mult))
                for h, o in enumerate(heads_in_psum(qblk)):
                    r = dve.scalar_tensor_tensor(out=acc[:, qblk, h * P:(h + 1) * P], in0=o,
                                                 scalar=std[:, qblk, h:h + 1], in1=sub_g,
                                                 op0=ALU.mult, op1=ALU.mult)
                r.then_inc(src_rdy, 1)

            def between(layer, i):
                for what, g, _ in BETWEEN[layer].get(i, ()):
                    if what == "scores":
                        score_max(g)
                    if what == "values" and layer == 0:
                        head_out(g)

            def even_end():
                score_max(3)
                turned(1, (0, 1))
                head_out(2)
                split(U_IN_E - 1 + SPLIT_AHEAD)
                head_out(3)
                turned(1, (2, 3))

            def odd_end():
                head_norm(0)
                head_norm_end(0)
                turned(4, (0, 1))
                split(K_OUT_O - 1 + SPLIT_AHEAD)
                head_norm(1)
                head_norm_end(1)
                turned(4, (2, 3))

            def norm_sum(k, n, tb):
                if tb == 0:
                    dve.wait_ge(sum_rdy, n + 1)
                else:
                    dve.wait_ge(w_used, k + 1)
                for h in range(2):
                    c = slice(h * 512, h * 512 + 512)
                    dve.scalar_tensor_tensor(out=acc[:, tb, c], in0=x[:, tb, c], scalar=ALPHA,
                                             in1=yb(tb, h)[:, :], op0=ALU.mult, op1=ALU.add).then_inc(added, 1)

            def norm_end(n, tb, roots, gb):
                if tb == 0:
                    dve.wait_ge(gb_in, 16 * (n + 1))
                dve.wait_ge(mean_rdy, 2 * n + tb + 1)
                link(dve.scalar_tensor_tensor(out=x[:, tb, :], in0=acc[:, tb, :], scalar=stats[:, tb, 3:4],
                                              in1=gb[:, 0, :], op0=ALU.add, op1=ALU.mult))
                dve.wait_ge(std_rdy, roots + tb + 1)
                link(dve.reciprocal(std[:, tb, 0:1], std[:, tb, 0:1]))
                dve.scalar_tensor_tensor(out=x[:, tb, :], in0=x[:, tb, :], scalar=std[:, tb, 0:1],
                                         in1=gb[:, 1, :], op0=ALU.mult, op1=ALU.add).then_inc(src_rdy, 1)

            def norm(k, n, roots, t):
                norm_sum(k, n, 0)
                norm_end(n, 0, roots, gb_extra)
                norm_sum(k, n, 1)
                norm_end(n, 1, roots, gb_extra)
                turned(t)
                split(k - 1 + SPLIT_AHEAD)

            dve.memset(htmp[:, 0:P], 0.0).then_inc(zeroed, 1)
            link(dve.memset(eps[:, :], EPS))
            dve.wait_ge(c_in, 16)
            turned(0)
            split(0)
            split(1)
            split(2)
            for k in range(N_DENSE):
                if k < U_IN_E:
                    between(0, k)
                if K_IN_O <= k < K_OUT_O:
                    between(1, k - K_IN_O)
                if k == K_FFN - 1:
                    norm(k, 0, 0, 2)
                if K_FFN <= k < K_IN_O:
                    what, c = FFN_ORDER[k - K_FFN]
                    if what == "up":
                        dve.wait_ge(f_silu, c + 1)
                        dve.tensor_tensor(htmp[:, :], htmp[:, :], ps[2 + c % 2][:, :], ALU.mult).then_inc(f_h, 1)
                    n = hidden_after(what, c)
                    if n is not None:
                        h, l = hidden(n)
                        dve.wait_ge(f_hi, n + 1)
                        dve.tensor_tensor(l, htmp[:, :], h.bitcast(F32), ALU.subtract).then_inc(f_lo, 1)
                if k == K_IN_O - 1:
                    norm(k, 1, 2, 3)
                if k == N_DENSE - 1:
                    norm(k, 2, 6, 5)
                if k not in (U_IN_E - 1, K_OUT_O - 1):
                    splits(k)
                if k == 1:
                    dve.wait_ge(small_in, 5 * 16)
                    link(dve.tensor_scalar(snk[:, 1, :], snk[:, 0, :], -1.0, None, ALU.mult))
                    link(dve.tensor_tensor_reduce(out=htmp[:, 0:DH], in0=lam_in[:, 0, :], in1=lam_in[:, 1, :], scale=1.0,
                                                  scalar=0.0, op0=ALU.mult, op1=ALU.add, accum_out=lam[:, 0:1]))
                    dve.tensor_tensor_reduce(out=htmp[:, DH:2 * DH], in0=lam_in[:, 2, :], in1=lam_in2, scale=1.0,
                                             scalar=0.0, op0=ALU.mult, op1=ALU.add, accum_out=lam[:, 1:2]).then_inc(lam_v, 1)
                    dve.wait_ge(lam_s, 1)
                    link(dve.tensor_tensor(lam[:, 2:3], lam[:, 1:2], lam[:, 0:1], ALU.subtract))
                    link(dve.tensor_scalar(lam[:, 3:4], lam[:, 2:3], -LAMBDA_INIT, None, ALU.add))
                    link(dve.tensor_scalar(sub_g, sub_g, 1.0 - LAMBDA_INIT, None, ALU.mult))
                    dve.wait_ge(in_ev, 1)
                    for tb in range(TB):
                        link(dve.tensor_tensor(fz[:, 1, 8 * tb:8 * tb + 8], fz[:, 0, 8 * tb:8 * tb + 8],
                                               snk[:, 2, :], ALU.add))
                    dve.scalar_tensor_tensor(out=fz[:, 2, :], in0=fz[:, 1, :], scalar=-1.0, in1=fz[:, 1, :],
                                             op0=ALU.mult, op1=ALU.max).then_inc(fg_v, 1)
                    dve.wait_ge(fg_s, 1)
                    dve.tensor_scalar(fz[:, 3, :], fz[:, 2, :], 1.0, None, ALU.add).then_inc(fg_v, 1)
                    dve.wait_ge(fg_v, 2)
                    link(dve.tensor_scalar(fz[:, 5, :], fz[:, 3, :], -1.0, None, ALU.add))
                    link(dve.tensor_tensor(fz[:, 5, :], fz[:, 2, :], fz[:, 5, :], ALU.subtract))
                    link(dve.reciprocal(fz[:, 6, :], fz[:, 3, :]))
                    link(dve.tensor_tensor(fz[:, 5, :], fz[:, 5, :], fz[:, 6, :], ALU.mult))
                    dve.wait_ge(fg_s, 2)
                    link(dve.tensor_tensor(fz[:, 7, :], fz[:, 4, :], fz[:, 5, :], ALU.add))
                    dve.tensor_scalar(fz[:, 8, :], fz[:, 1, :], 0.0, None, ALU.min).then_inc(fg_v, 1)
                    dve.wait_ge(fg_v, 3)
                    dve.tensor_tensor(logf[:, :, :], fz[:, 8, :].rearrange("p (t n) -> p t n", t=TB),
                                      fz[:, 7, :].rearrange("p (t n) -> p t n", t=TB), ALU.subtract).then_inc(fg_v, 1)
                if k == 3:
                    dve.wait_ge(tables_in, 2 * 16)
                    dve.wait_ge(cum_ps, 1)
                    link(dve.tensor_copy(cumtok[:, :, :], ps[6][:, 0:16].rearrange("p (t n) -> p t n", t=TB)))
                    for h in range(8):
                        dve.wait_ge(cum_ps, 2 + h // 2)
                        for b in range(TB):
                            c = slice(P * b, P * b + P * (b + 1))
                            r = dve.scalar_tensor_tensor(
                                out=biasb[:, h, c], in0=ps[h // 2][:, (h % 2) * 256:(h % 2) * 256 + P * (b + 1)],
                                scalar=cumtok[:, b, h:h + 1], in1=bias[:, B_B + P * b:B_B + P * b + P * (b + 1)],
                                op0=ALU.subtract, op1=ALU.subtract)
                    r.then_inc(bb_rdy, 1)
                    dve.wait_ge(bb_rdy, 1)
                    dve.wait_ge(wr_h, 1)
                    dve.tensor_tensor(wrl[:, :, :], wr_raw, wrh[:, :, :].bitcast(F32), ALU.subtract).then_inc(wr_l, 1)
                if k == U_IN_E - 1:
                    even_end()
                if k == K_IN_O + 8:
                    combine(5)
                if k == K_IN_O + 10:
                    combine(7)
                if k == K_OUT_O - 1:
                    odd_end()

            lg, eq, cand, oh1, lg2, oh2, g1o, g2o, chosen, pos = (rt[i] for i in (0, 1, 2, 3, 4, 5, 6, 7, 10, 11))
            rev_b = revidx.unsqueeze(1).to_broadcast([P, TB, 8])

            def over(a):
                return a.unsqueeze(2).to_broadcast([P, TB, 8])

            def pick_top(src, m, k1, oh):
                link(dve.tensor_reduce(m, src, AX_X, ALU.max))
                link(dve.tensor_tensor(eq, src, over(m), ALU.is_equal))
                link(dve.tensor_tensor(cand, eq, rev_b, ALU.mult))
                link(dve.tensor_reduce(k1, cand, AX_X, ALU.max))
                link(dve.tensor_tensor(oh, cand, over(k1), ALU.is_equal))

            dve.wait_ge(lg_ps, 1)
            dve.tensor_copy(lgt[:, :], ps[0][0:8, 0:TOK]).then_inc(lgt_rdy, 1)
            dve.wait_ge(lg_ps, 2)
            link(dve.tensor_copy(lg, ps[2][:, 0:16].rearrange("p (t n) -> p t n", t=TB)))
            pick_top(lg, r1[0], r1[4], oh1)
            link(dve.scalar_tensor_tensor(out=lg2, in0=oh1, scalar=-BIG, in1=lg, op0=ALU.mult, op1=ALU.add))
            pick_top(lg2, r1[1], r1[5], oh2)
            link(dve.tensor_tensor(r1[2], r1[1], r1[0], ALU.subtract))
            dve.tensor_tensor(chosen, oh1, oh2, ALU.add).then_inc(sel_rdy, 1)
            link(dve.memset(gates[:, :, 0:1], 0.0))
            dve.memset(posm[:, :, 16:17], -1.0).then_inc(top_v, 1)
            dve.wait_ge(top_s, 1)
            link(dve.tensor_scalar(r1[6], r1[3], 1.0, None, ALU.add))
            link(dve.reciprocal(r1[6], r1[6]))
            link(dve.tensor_tensor(r1[7], r1[3], r1[6], ALU.mult))
            link(dve.tensor_tensor(g1o, oh1, over(r1[6]), ALU.mult))
            link(dve.tensor_tensor(g2o, oh2, over(r1[7]), ALU.mult))
            link(dve.tensor_tensor(gates[:, :, 1:9], g1o, g2o, ALU.add))
            link(dve.tensor_copy(gates[:, :, 9:17], gates[:, :, 1:9]))
            dve.wait_ge(pos_ps, 1)
            link(dve.tensor_tensor(pos, ps[1][:, 0:16].rearrange("p (t n) -> p t n", t=TB), chosen, ALU.mult))
            link(dve.tensor_scalar(posm[:, :, 0:8], pos, -1.0, None, ALU.add))
            link(dve.tensor_scalar(posm[:, :, 8:16], pos, -1.0 - P, None, ALU.add))
            link(dve.tensor_reduce(r1[4][0:1, 0:1], ps[1][0:1, 16:24], AX_X, ALU.max))
            link(dve.tensor_scalar(r1[4][0:1, 0:1], r1[4][0:1, 0:1], float(P), None, ALU.is_gt))
            dve.tensor_copy(flag[:, :], r1[4][0:1, 0:1]).then_inc(flag_rdy, 1)
            link(dve.tensor_scalar(acc[:, :, :], x[:, :, :], ALPHA, None, ALU.mult))

            def one_hot(n, e):
                for tb in range(TB):
                    r = dve.tensor_scalar(ohot[:, tb, :], iota, posm[:, tb, bass.ds(e, 1)], None, ALU.is_equal)
                r.then_inc(oh_rdy, 1)

            def gathered(n):
                dve.wait_ge(ga_hi, n + 1)
                for q in range(2):
                    part = (slice(None), slice(4 * q, 4 * q + 4), slice(0, P))
                    r = dve.tensor_tensor(xtl[part], ps[1 + 2 * q][:, :].rearrange("p (k n) -> p k n", k=4),
                                          xth[part].bitcast(F32), ALU.subtract)
                r.then_inc(ga_lo, 1)

            def scattered(n, tb):
                for nn in range(2):
                    i = 2 * tb + nn
                    o = acc[:, tb, nn * 512:(nn + 1) * 512]
                    dve.wait_ge(sc_ps, n * 4 + (i + 1))
                    dve.scalar_tensor_tensor(out=o, in0=ps[7 if i % 2 == 0 else 4][:, :],
                                             scalar=gates[:, tb, bass.ds(n, 1)], in1=o,
                                             op0=ALU.mult, op1=ALU.add).then_inc(sc_acc, 1)

            def expert(e):
                for j, (what, c, half) in enumerate(EXP_ORDER):
                    if j != PER_EXP - 3:
                        lo(e * PER_EXP + (N_DENSE + j + SPLIT_AHEAD + 1), j, moe_slot(j + SPLIT_AHEAD)[0])
                    if (what, half) == ("up", 1):
                        dve.wait_ge(m_silu, e * EC + (c + 1))
                        dve.tensor_tensor(htmp[:, :], htmp[:, :], ps[2 + c % 2][:, :], ALU.mult).then_inc(m_h, 1)
                    if j == 1:
                        scattered(e, 0)
                    if j == 3:
                        scattered(e, 1)
                    if j == 6:
                        dve.wait_ge(oht_ps, e + 1)
                        one_hot(e + 1, e + 1)
                    if ((what, half) == ("gate", 1) and c) or j == PER_EXP - 3:
                        dve.wait_ge(m_hi, e * EC + (c if j != PER_EXP - 3 else EC))
                        dve.tensor_tensor(htl[:, :], ps[4][:, :], hth[:, :].bitcast(F32), ALU.subtract).then_inc(m_lo, 1)
                    if j == PER_EXP - 3:
                        lo(e * PER_EXP + (N_DENSE + j + SPLIT_AHEAD + 1), j, moe_slot(j + SPLIT_AHEAD)[0])
                        gathered(e + 1)

            one_hot(0, 0)
            gathered(0)
            with dve.Fori(0, N_EXP) as e:
                expert(e)
            dve.wait_ge(flag_rdy, 1)
            more = dve.value_load(flag[0:1, 0:1], min_val=0, max_val=1)
            with dve.If(more > 0):
                with dve.Fori(N_EXP, 2 * N_EXP) as e:
                    expert(e)
                scattered(2 * N_EXP, 0)
                scattered(2 * N_EXP, 1)
                dve.wait_ge(sc_acc, 4 * (2 * N_EXP + 1))
            with dve.Else():
                scattered(N_EXP, 0)
                scattered(N_EXP, 1)
                dve.wait_ge(sc_acc, 4 * (N_EXP + 1))
            dve.memset(stats[:, 0, 5:6], 0.0).then_inc(added, 4)
            for tb in range(TB):
                norm_end(3, tb, 8, gb_last)


def constants():
    c = np.zeros((P, C_END), np.float32)
    c[:, C_ID:C_ID + P] = np.eye(P)
    c[:, C_TRI:C_TRI + P] = np.triu(np.ones((P, P)))
    c[:, C_TRI + P:C_TRI + 2 * P] = 1.0
    for b in range(4):
        for r in range(2):
            c[64 * r:64 * r + 64, C_QS + b] = DH ** -0.5 / slope(2 * b + r)
    c[:, C_IOTA:C_IOTA + P] = np.arange(P)
    c[:, C_REV:C_REV + 8] = np.arange(8, 0, -1)
    t, s = np.arange(TOK)[:, None], np.arange(TOK)[None, :]
    near = -np.abs(t - s).astype(np.float32)
    ok = {B_A: (s // CHUNK <= t // CHUNK) & (s // CHUNK >= t // CHUNK - 1), B_B: s <= t, B_C: s // CHUNK <= t // CHUNK}
    b = np.zeros((P, B_END), np.float32)
    for at, valid in ok.items():
        full = np.where(valid, 0.0 if at == B_B else near, -1e30 if at == B_B else -1e34)
        b[:, at:at + P] = full[0:P, 0:P]
        b[:, at + P:at + BIAS_W] = full[P:TOK, :]
    return c, b


def col_units(w):
    n = w.shape[1] // 256
    return w.reshape(KT, P, n, 256).transpose(2, 1, 0, 3).reshape(n, P, UNIT)


def row_units(w):
    n = w.shape[0] // 256
    return w.reshape(n, 2, P, D).transpose(0, 2, 1, 3).reshape(n, P, UNIT)


def dense_stream(e_w_in, e_w_out, e_w_gate, e_w_up, e_w_down, o_w_in, o_w_out):
    w = e_w_in
    k0 = A_Q
    b0 = A_Q + 2 * A_KV
    ka = w[:, k0:k0 + A_KV]
    cols = [w[:, k0 + A_KV:b0], w[:, b0 + 3 * B_W:], np.zeros((D, 120), w.dtype),
            w[:, 0:A_Q], ka, ka[:, DH:], ka[:, :DH],
            w[:, b0:b0 + 3 * B_W]]
    gate, up, down = col_units(e_w_gate), col_units(e_w_up), row_units(e_w_down)
    part = {"gate": gate, "up": up, "down": down}
    ffn = np.stack([part[what][c] for what, c in FFN_ORDER])
    return np.concatenate([col_units(np.concatenate(cols, axis=1)), row_units(e_w_out), ffn,
                           col_units(o_w_in)[[0, 1, 4, 5, 2, 3, 6, 7, 8, 9, 10, 11]], row_units(o_w_out)])


def expert_stream(w_gate, w_up, w_down):
    out = np.empty((N_MOE + SPLIT_AHEAD, P, UNIT), w_gate.dtype)
    for e in range(N_EXP):
        for j, (what, c, half) in enumerate(EXP_ORDER):
            if what == "down":
                r = c * 512 + half * 256
                u = w_down[e, r:r + 256].reshape(2, P, D)
            else:
                w = w_gate if what == "gate" else w_up
                u = w[e, half * 512:half * 512 + 512, c * 512:(c + 1) * 512].reshape(4, P, 512)
            out[e * PER_EXP + j] = u.transpose(1, 0, 2).reshape(P, UNIT)
    out[N_MOE:] = out[:SPLIT_AHEAD]
    return out


def kernel(**inputs):
    import concourse.bacc as bacc
    from concourse.bass_utils import run_bass_kernel_spmd

    a = {k: np.asarray(v) for k, v in inputs.items()}
    cst, bias_cst = constants()
    arrays = {
        "x_in": a["x"],
        "w_dense": dense_stream(a["e_w_in"][0], a["e_w_out"][0], a["e_w_gate"][0], a["e_w_up"][0],
                                a["e_w_down"][0], a["o_w_in"][0], a["o_w_out"][0]),
        "w_moe": expert_stream(a["o_w_gate"][0], a["o_w_up"][0], a["o_w_down"][0]),
        "cst": cst,
        "bias_cst": bias_cst,
        "vec_rows": np.stack([np.stack([a[f"{l}_ln{n}_g"][0], a[f"{l}_ln{n}_b"][0]])
                              for l in "eo" for n in (1, 2)]),
        "sinks": a["e_sinks"][0],
        "b_forget": a["e_b_forget"][0],
        "lam_rows": np.stack([a["o_lambda_q1"][0], a["o_lambda_k1"][0], a["o_lambda_q2"][0], a["o_lambda_k2"][0]]),
        "subln": a["o_subln_g"][0],
        "w_router": a["o_w_router"][0].reshape(KT, P, N_EXP).transpose(1, 0, 2),
    }
    nc = bacc.Bacc("TRN2", target_bir_lowering=False, num_devices=1, dynamic_dma_scratch_size=4096)
    arrays = {k: np.ascontiguousarray(v) for k, v in arrays.items()}
    args = [nc.dram_tensor(k, v.shape, mybir.dt.from_np(v.dtype), kind="ExternalInput").ap()
            for k, v in arrays.items()]
    out = nc.dram_tensor("out", (1, TOK, D), F32, kind="ExternalOutput").ap()
    trunk(nc, *args, out)
    r = run_bass_kernel_spmd(nc, [arrays], core_ids=[0])
    return r.results[0]["out"]
```
